# Optimizing a Trainium2 kernel written in Bass

```python
import math
import jax
import jax.numpy as jnp
from jax import lax
import numpy as np

D_MODEL = 1024
BATCH = 1
SEQ = 256
DEPTH = 2

CTX_LEN = 256
GRID_W = 64
EPS = 1e-6
N_DIR = 2
N_BRANCH = 3

GLA_HEADS = 4
GLA_DK = 128
GLA_DV = 256
GLA_GATE_RANK = 16
GLA_GATE_NORMALIZER = 16.0
GLA_CHUNK = 64

GDN_HEADS = 8
GDN_DK = 128
GDN_DV = 128
GDN_CONV = 5
GDN_CHUNK = 64
GDN_QKV = 2 * GDN_HEADS * GDN_DK + GDN_HEADS * GDN_DV

MLA_HEADS = 8
MLA_Q_LORA = 384
MLA_KV_LORA = 256
MLA_NOPE = 128
MLA_ROPE = 64
MLA_DV = 128
MLA_SCALE = (MLA_NOPE + MLA_ROPE) ** -0.5
MLA_Q_BLOCK = 128
ROPE_FREQ = MLA_ROPE // 4
ROPE_BASE = 10000.0

BRANCH_W = GLA_HEADS * GLA_DV

IN_NAMES = ('gla_q', 'gla_k', 'gla_v', 'gla_gate_lr', 'gla_z',
            'gdn_qkv', 'gdn_a', 'gdn_b', 'gdn_z',
            'mla_q_down', 'mla_kv_down', 'mla_k_rope', 'mla_z',
            'merge_gate')
IN_SIZES = (GLA_HEADS * GLA_DK, GLA_HEADS * GLA_DK, GLA_HEADS * GLA_DV, N_DIR * GLA_GATE_RANK, BRANCH_W,
            GDN_QKV, N_DIR * GDN_HEADS, N_DIR * GDN_HEADS, BRANCH_W,
            MLA_Q_LORA, MLA_KV_LORA, MLA_ROPE, BRANCH_W,
            N_BRANCH * D_MODEL)
N_IN = sum(IN_SIZES)

kernel_name = 'hybrid_gla_gdn_mla_flow_block'

def rmsnorm(x, w):
    xf = x.astype(jnp.float32)
    y = xf * lax.rsqrt(jnp.mean(xf * xf, axis=-1, keepdims=True) + EPS)
    return (y * w.astype(jnp.float32)).astype(x.dtype)

def l2norm(x):
    xf = x.astype(jnp.float32)
    return (xf * lax.rsqrt(jnp.sum(xf * xf, axis=-1, keepdims=True) + EPS)).astype(x.dtype)

def in_projection(h, w_in):
    parts = jnp.split(h @ w_in, np.cumsum(IN_SIZES)[:-1].tolist(), axis=-1)
    return dict(zip(IN_NAMES, parts))

def axial_rope_tables(rows):
    row = jnp.repeat(jnp.arange(rows, dtype=jnp.float32), GRID_W)
    col = jnp.tile(jnp.arange(GRID_W, dtype=jnp.float32), rows)
    inv_freq = jnp.power(ROPE_BASE, -jnp.arange(ROPE_FREQ, dtype=jnp.float32) / ROPE_FREQ)
    ang = jnp.stack([row[:, None] * inv_freq, col[:, None] * inv_freq], axis=1)
    return jnp.cos(ang), jnp.sin(ang)

def apply_axial_rope(x, cos, sin):
    shp = x.shape
    xr = x.reshape(shp[:-1] + (2, 2, ROPE_FREQ))
    x1, x2 = xr[..., 0, :], xr[..., 1, :]
    cos = cos.astype(x.dtype)
    sin = sin.astype(x.dtype)
    out = jnp.stack([x1 * cos - x2 * sin, x2 * cos + x1 * sin], axis=-2)
    return out.reshape(shp)

def centred_depthwise_conv(x, w):
    half = w.shape[0] // 2
    return lax.conv_general_dilated(x, w[:, None, :].astype(x.dtype), window_strides=(1,),
                                    padding=[(half, half)], dimension_numbers=('NWC', 'WIO', 'NWC'),
                                    feature_group_count=x.shape[-1])

def gla_chunk_scan(q, k, v, log_a, s0):
    B, T, H, _ = q.shape
    DV = v.shape[-1]
    N = T // GLA_CHUNK

    def blocks(a):
        return a.astype(jnp.float32).reshape((B, N, GLA_CHUNK) + a.shape[2:])

    q, k, v, log_a = blocks(q), blocks(k), blocks(v), blocks(log_a)
    b = jnp.cumsum(log_a, axis=2)
    b_last = b[:, :, -1]
    q_dec = q * jnp.exp(b)
    k_inv = k * jnp.exp(-b)
    k_end = k * jnp.exp(b_last[:, :, None] - b)
    incl = jnp.tril(jnp.ones((GLA_CHUNK, GLA_CHUNK), dtype=bool))
    att = jnp.where(incl, jnp.einsum('bnthd,bnshd->bnhts', q_dec, k_inv), 0.0)
    o_intra = jnp.einsum('bnhts,bnshv->bnthv', att, v)
    writes = jnp.einsum('bnshd,bnshv->bnhdv', k_end, v)

    def step(s, inp):
        decay, write = inp
        return s * decay[..., None] + write, s

    s_fin, s_prev = lax.scan(step, s0, (jnp.moveaxis(jnp.exp(b_last), 1, 0), jnp.moveaxis(writes, 1, 0)))
    o_inter = jnp.einsum('bnthd,nbhdv->bnthv', q_dec, s_prev)
    return (o_intra + o_inter).reshape(B, T, H, DV), s_fin

def gdn_chunk_scan(q, k, v, g, beta, s0):
    B, T, H, _ = q.shape
    DV = v.shape[-1]
    C = GDN_CHUNK
    N = T // C

    def blocks(a):
        return a.astype(jnp.float32).reshape((B, N, C) + a.shape[2:])

    q, k, v, g, beta = map(blocks, (q, k, v, g, beta))
    g_cum = jnp.cumsum(g, axis=2)
    g_h = jnp.swapaxes(g_cum, 2, 3)
    incl = jnp.tril(jnp.ones((C, C), dtype=bool))
    strict = jnp.tril(jnp.ones((C, C), dtype=bool), k=-1)
    diff = g_h[..., :, None] - g_h[..., None, :]
    decay = jnp.where(incl, jnp.exp(jnp.where(incl, diff, 0.0)), 0.0)
    k_beta = k * beta[..., None]
    v_beta = v * beta[..., None]
    l_strict = jnp.where(strict, jnp.einsum('bnthd,bnshd->bnhts', k_beta, k) * decay, 0.0)
    eye = jnp.eye(C, dtype=jnp.float32)
    t_inv = lax.linalg.triangular_solve(eye + l_strict, jnp.broadcast_to(eye, l_strict.shape),
                                        left_side=True, lower=True, unit_diagonal=True)
    u = jnp.einsum('bnhts,bnshv->bnthv', t_inv, v_beta)
    w = jnp.einsum('bnhts,bnshd->bnthd', t_inv, k_beta * jnp.exp(g_cum)[..., None])
    att = jnp.where(incl, jnp.einsum('bnthd,bnshd->bnhts', q, k) * decay, 0.0)
    q_dec = q * jnp.exp(g_cum)[..., None]
    k_end = k * jnp.exp(g_cum[:, :, -1:] - g_cum)[..., None]
    chunk_decay = jnp.exp(g_cum[:, :, -1])

    def step(s, inp):
        w_n, u_n, qd_n, att_n, ke_n, d_n = inp
        v_new = u_n - jnp.einsum('bthd,bhdv->bthv', w_n, s)
        o_n = jnp.einsum('bthd,bhdv->bthv', qd_n, s) + jnp.einsum('bhts,bshv->bthv', att_n, v_new)
        s = s * d_n[..., None, None] + jnp.einsum('bshd,bshv->bhdv', ke_n, v_new)
        return s, o_n

    xs = tuple(jnp.moveaxis(a, 1, 0) for a in (w, u, q_dec, att, k_end, chunk_decay))
    s_fin, o = lax.scan(step, s0, xs)
    return jnp.moveaxis(o, 0, 1).reshape(B, T, H, DV), s_fin

def bidirectional(scan_fn, ctx_fwd, ctx_bwd, lat_fwd, lat_bwd, s0):
    flip = lambda a: jnp.flip(a, axis=1)
    o_cf, s_cf = scan_fn(*ctx_fwd, s0)
    o_cb, s_cb = scan_fn(*map(flip, ctx_bwd), s0)
    o_xf, _ = scan_fn(*lat_fwd, s_cf)
    o_xb, _ = scan_fn(*map(flip, lat_bwd), s_cb)
    return o_cf + flip(o_cb), o_xf + flip(o_xb)

def gla_prepare(pt, gate_w2, gate_b):
    B, T, _ = pt['gla_q'].shape
    q = pt['gla_q'].reshape(B, T, GLA_HEADS, GLA_DK) * GLA_DK ** -0.5
    k = pt['gla_k'].reshape(B, T, GLA_HEADS, GLA_DK)
    v = pt['gla_v'].reshape(B, T, GLA_HEADS, GLA_DV)
    lr = pt['gla_gate_lr'].reshape(B, T, N_DIR, GLA_GATE_RANK)
    logit = jnp.einsum('btir,irk->btik', lr, gate_w2) + gate_b
    log_a = (jax.nn.log_sigmoid(logit.astype(jnp.float32)) / GLA_GATE_NORMALIZER).reshape(
        B, T, N_DIR, GLA_HEADS, GLA_DK)
    return (q, k, v, log_a[:, :, 0]), (q, k, v, log_a[:, :, 1])

def gdn_prepare(pt, conv_w, a_log, dt_bias):
    qkv = jax.nn.silu(centred_depthwise_conv(pt['gdn_qkv'], conv_w))
    B, T, _ = qkv.shape
    hk = GDN_HEADS * GDN_DK
    q, k, v = jnp.split(qkv, [hk, 2 * hk], axis=-1)
    q = l2norm(q.reshape(B, T, GDN_HEADS, GDN_DK)) * GDN_DK ** -0.5
    k = l2norm(k.reshape(B, T, GDN_HEADS, GDN_DK))
    v = v.reshape(B, T, GDN_HEADS, GDN_DV)
    a = pt['gdn_a'].reshape(B, T, N_DIR, GDN_HEADS).astype(jnp.float32)
    g = -jnp.exp(a_log.astype(jnp.float32)) * jax.nn.softplus(a + dt_bias.astype(jnp.float32))
    beta = jax.nn.sigmoid(pt['gdn_b'].reshape(B, T, N_DIR, GDN_HEADS).astype(jnp.float32))
    return (q, k, v, g[:, :, 0], beta[:, :, 0]), (q, k, v, g[:, :, 1], beta[:, :, 1])

def mla_prepare(pt, p, cos, sin):
    B, T, _ = pt['mla_q_down'].shape
    q = (rmsnorm(pt['mla_q_down'], p['mla_q_norm_w']) @ p['mla_q_up']).reshape(
        B, T, MLA_HEADS, MLA_NOPE + MLA_ROPE)
    kv = (rmsnorm(pt['mla_kv_down'], p['mla_kv_norm_w']) @ p['mla_kv_up']).reshape(
        B, T, MLA_HEADS, MLA_NOPE + MLA_DV)
    q_nope = rmsnorm(q[..., :MLA_NOPE], p['mla_qn_nope'])
    q_rope = rmsnorm(q[..., MLA_NOPE:], p['mla_qn_rope'])
    k_nope = rmsnorm(kv[..., :MLA_NOPE], p['mla_kn_nope'])
    k_rope = rmsnorm(pt['mla_k_rope'], p['mla_kn_rope'])
    v = kv[..., MLA_NOPE:]
    if cos is not None:
        q_rope = apply_axial_rope(q_rope, cos[:, None], sin[:, None])
        k_rope = apply_axial_rope(k_rope, cos, sin)
    return q_nope, q_rope, k_nope, k_rope, v

def mla_attend(qn, qr, kn, kr, v):
    s = jnp.einsum('bqhd,bkhd->bhqk', qn, kn) + jnp.einsum('bqhr,bkr->bhqk', qr, kr)
    prob = jax.nn.softmax(s.astype(jnp.float32) * MLA_SCALE, axis=-1)
    return jnp.einsum('bhqk,bkhd->bqhd', prob.astype(v.dtype), v)

def mla_attend_blocked(qn, qr, kn, kr, v):
    B, T = qn.shape[:2]
    nb = T // MLA_Q_BLOCK

    def to_blocks(a):
        return jnp.moveaxis(a.reshape((B, nb, MLA_Q_BLOCK) + a.shape[2:]), 1, 0)

    o = lax.map(lambda qs: mla_attend(qs[0], qs[1], kn, kr, v), (to_blocks(qn), to_blocks(qr)))
    return jnp.moveaxis(o, 0, 1).reshape(B, T, MLA_HEADS * MLA_DV)

def gated_head_norm(o, w, z):
    B, T, H, Dh = o.shape
    return rmsnorm(o.astype(z.dtype), w).reshape(B, T, H * Dh) * jax.nn.silu(z)

def merge_branches(ya, yb, yc, gate_logits, w_branch, w_out):
    B, T, _ = ya.shape
    ys = jnp.einsum('btiw,iwd->btid', jnp.stack([ya, yb, yc], axis=2), w_branch)
    gates = jax.nn.sigmoid(gate_logits.reshape(B, T, N_BRANCH, D_MODEL))
    return jnp.einsum('btd,de->bte', jnp.sum(gates * ys, axis=2), w_out)

def hybrid_layer(x, ctx, c, c_ctx, p, cos, sin, update_ctx):
    B, T, _ = x.shape
    Lc = ctx.shape[1]
    mod_x = jax.nn.silu(c) @ p['ada_w'] + p['ada_b']
    mod_c = jax.nn.silu(c_ctx) @ p['ada_w'] + p['ada_b']
    shift_x, scale_x, gate_x = jnp.split(mod_x[:, None, :], 3, axis=-1)
    shift_c, scale_c, gate_c = jnp.split(mod_c, 3)
    px = in_projection(rmsnorm(x, p['norm_w']) * (1 + scale_x) + shift_x, p['w_in'])
    pc = in_projection(rmsnorm(ctx, p['norm_w']) * (1 + scale_c) + shift_c, p['w_in'])

    a_cf, a_cb = gla_prepare(pc, p['gla_gate_w2'], p['gla_gate_b'])
    a_xf, a_xb = gla_prepare(px, p['gla_gate_w2'], p['gla_gate_b'])
    s0_a = jnp.zeros((B, GLA_HEADS, GLA_DK, GLA_DV), jnp.float32)
    oa_c, oa_x = bidirectional(gla_chunk_scan, a_cf, a_cb, a_xf, a_xb, s0_a)

    b_cf, b_cb = gdn_prepare(pc, p['gdn_conv_w'], p['gdn_a_log'], p['gdn_dt_bias'])
    b_xf, b_xb = gdn_prepare(px, p['gdn_conv_w'], p['gdn_a_log'], p['gdn_dt_bias'])
    s0_b = jnp.zeros((B, GDN_HEADS, GDN_DK, GDN_DV), jnp.float32)
    ob_c, ob_x = bidirectional(gdn_chunk_scan, b_cf, b_cb, b_xf, b_xb, s0_b)

    qn_c, qr_c, kn_c, kr_c, v_c = mla_prepare(pc, p, None, None)
    qn_x, qr_x, kn_x, kr_x, v_x = mla_prepare(px, p, cos, sin)
    oc_x = mla_attend_blocked(qn_x, qr_x,
                              jnp.concatenate([kn_c, kn_x], axis=1),
                              jnp.concatenate([kr_c, kr_x], axis=1),
                              jnp.concatenate([v_c, v_x], axis=1))

    x = x + gate_x * merge_branches(
        gated_head_norm(oa_x, p['gla_norm_w'], px['gla_z']),
        gated_head_norm(ob_x, p['gdn_norm_w'], px['gdn_z']),
        oc_x * jax.nn.silu(px['mla_z']),
        px['merge_gate'], p['w_branch'], p['w_out'])

    if update_ctx:
        oc_c = mla_attend(qn_c, qr_c, kn_c, kr_c, v_c).reshape(B, Lc, BRANCH_W)
        ctx = ctx + gate_c * merge_branches(
            gated_head_norm(oa_c, p['gla_norm_w'], pc['gla_z']),
            gated_head_norm(ob_c, p['gdn_norm_w'], pc['gdn_z']),
            oc_c * jax.nn.silu(pc['mla_z']),
            pc['merge_gate'], p['w_branch'], p['w_out'])
    return x, ctx

def setup_inputs(seed: int = 0) -> dict:
    key = jax.random.key(seed)
    ks = jax.random.split(key, 25)
    L, D = DEPTH, D_MODEL

    def normal(k, shape, scale):
        return jax.random.normal(k, shape, jnp.float32) * scale

    def gain(k, shape):
        return 1.0 + 0.02 * jax.random.normal(k, shape, jnp.float32)

    dt = jnp.exp(jax.random.uniform(ks[13], (L, N_DIR, GDN_HEADS), jnp.float32,
                                    math.log(1e-3), math.log(1e-1)))
    return {
        'x': normal(ks[0], (BATCH, SEQ, D), 1.0),
        'c': normal(ks[1], (BATCH, D), 1.0),
        'ctx': normal(ks[2], (BATCH, CTX_LEN, D), 1.0),
        'c_ctx': normal(ks[3], (D,), 1.0),
        'norm_w': gain(ks[4], (L, D)),
        'ada_w': normal(ks[5], (L, D, 3 * D), 0.5 * D ** -0.5),
        'ada_b': normal(ks[6], (L, 3 * D), 0.02),
        'w_in': normal(ks[7], (L, D, N_IN), D ** -0.5),
        'gla_gate_w2': normal(ks[8], (L, N_DIR, GLA_GATE_RANK, GLA_HEADS * GLA_DK), GLA_GATE_RANK ** -0.5),
        'gla_gate_b': normal(ks[9], (L, N_DIR, GLA_HEADS * GLA_DK), 0.1),
        'gla_norm_w': gain(ks[10], (L, GLA_DV)),
        'gdn_conv_w': normal(ks[11], (L, GDN_CONV, GDN_QKV), GDN_CONV ** -0.5),
        'gdn_a_log': jnp.log(jax.random.uniform(ks[12], (L, N_DIR, GDN_HEADS), jnp.float32, 1.0, 16.0)),
        'gdn_dt_bias': dt + jnp.log(-jnp.expm1(-dt)),
        'gdn_norm_w': gain(ks[14], (L, GDN_DV)),
        'mla_q_norm_w': gain(ks[15], (L, MLA_Q_LORA)),
        'mla_q_up': normal(ks[16], (L, MLA_Q_LORA, MLA_HEADS * (MLA_NOPE + MLA_ROPE)), MLA_Q_LORA ** -0.5),
        'mla_kv_norm_w': gain(ks[17], (L, MLA_KV_LORA)),
        'mla_kv_up': normal(ks[18], (L, MLA_KV_LORA, MLA_HEADS * (MLA_NOPE + MLA_DV)), MLA_KV_LORA ** -0.5),
        'mla_qn_nope': gain(ks[19], (L, MLA_NOPE)),
        'mla_qn_rope': gain(ks[20], (L, MLA_ROPE)),
        'mla_kn_nope': gain(ks[21], (L, MLA_NOPE)),
        'mla_kn_rope': gain(ks[22], (L, MLA_ROPE)),
        'w_branch': normal(ks[23], (L, N_BRANCH, BRANCH_W, D), BRANCH_W ** -0.5),
        'w_out': normal(ks[24], (L, D, D), D ** -0.5),
    }

def reference(x, c, ctx, c_ctx, norm_w, ada_w, ada_b, w_in, gla_gate_w2, gla_gate_b, gla_norm_w,
              gdn_conv_w, gdn_a_log, gdn_dt_bias, gdn_norm_w, mla_q_norm_w, mla_q_up, mla_kv_norm_w,
              mla_kv_up, mla_qn_nope, mla_qn_rope, mla_kn_nope, mla_kn_rope, w_branch, w_out):
    ROWS = x.shape[1] // GRID_W
    cos, sin = axial_rope_tables(ROWS)
    for l in range(DEPTH):
        p = dict(norm_w=norm_w[l], ada_w=ada_w[l], ada_b=ada_b[l], w_in=w_in[l],
                 gla_gate_w2=gla_gate_w2[l], gla_gate_b=gla_gate_b[l], gla_norm_w=gla_norm_w[l],
                 gdn_conv_w=gdn_conv_w[l], gdn_a_log=gdn_a_log[l], gdn_dt_bias=gdn_dt_bias[l],
                 gdn_norm_w=gdn_norm_w[l], mla_q_norm_w=mla_q_norm_w[l], mla_q_up=mla_q_up[l],
                 mla_kv_norm_w=mla_kv_norm_w[l], mla_kv_up=mla_kv_up[l], mla_qn_nope=mla_qn_nope[l],
                 mla_qn_rope=mla_qn_rope[l], mla_kn_nope=mla_kn_nope[l], mla_kn_rope=mla_kn_rope[l],
                 w_branch=w_branch[l], w_out=w_out[l])
        x, ctx = hybrid_layer(x, ctx, c, c_ctx, p, cos, sin, update_ctx=(l < DEPTH - 1))
    return x


_drawn_inputs = setup_inputs


def setup_inputs(seed=0):
    import zlib

    import numpy as np

    out = dict(_drawn_inputs(seed))
    spreads = {}
    factors = {'norm_w': 7.495,
     'ada_b': 2.879,
     'gla_gate_b': 8.0,
     'gla_norm_w': 8.0,
     'gdn_norm_w': 8.0,
     'mla_q_norm_w': 8.0,
     'mla_q_up': 4.261,
     'mla_kv_norm_w': 8.0,
     'mla_qn_nope': 8.0,
     'mla_qn_rope': 8.0,
     'mla_kn_nope': 8.0,
     'mla_kn_rope': 8.0}
    for name, (base, spread) in spreads.items():
        noise = np.random.default_rng([zlib.crc32(name.encode()), seed]).standard_normal(out[name].shape)
        drawn = base * np.exp(spread * noise) if base else spread * noise
        out[name] = jnp.asarray(drawn.astype(out[name].dtype))
    for name, factor in factors.items():
        out[name] = (out[name] * factor).astype(out[name].dtype)
    return out
```

```python
import math
from contextlib import ExitStack

import numpy as np

import concourse.bass as bass
from concourse import mybir

ALU = mybir.AluOpType
ACT = mybir.ActivationFunctionType
F32 = mybir.dt.float32
U32 = mybir.dt.uint32
AX_X = mybir.AxisListType.X

P = 128
D = 1024
KT = D // P
DEPTH = 2
LC = LX = 256
T = LC + LX
TT = T // P
CH = 64
NCH = T // CH
EPS = 1e-6
GRID_W = 64

AH, ADK, ADV = 4, 128, 256
RANK = 16
BH, BDK = 8, 128
CONV = 5
MH, NOPE, ROPE, MDV = 8, 128, 64, 128
QL, KVL = 384, 256
MSCALE = (NOPE + ROPE) ** -0.5

SIZES = (("aq", 512), ("ak", 512), ("av", 1024), ("alr", 32), ("az", 1024),
         ("bq", 1024), ("bk", 1024), ("bv", 1024), ("bab", 32), ("bz", 1024),
         ("cq", QL), ("ckv", KVL), ("ckr", ROPE), ("cz", 1024), ("mg", 3 * D))
COL = {}
_at = 0
for _n, _s in SIZES:
    COL[_n] = _at
    _at += _s
N_IN = _at

NLEV = 6
C_ID, C_CUM, C_REV, C_LEV, C_COS, C_SIN = 0, 128, 384, 640, 640 + 2 * NLEV * 128, 640 + 2 * NLEV * 128 + 256
NCONST = C_SIN + 256


def constants():
    c = np.zeros((P, NCONST), np.float32)
    i, j = np.meshgrid(np.arange(P), np.arange(P), indexing="ij")
    same = (i // CH) == (j // CH)
    c[:, C_ID:C_ID + P] = i == j
    c[:, C_CUM:C_CUM + P] = same & (i <= j)
    c[:, C_CUM + P:C_CUM + 2 * P] = same & (i >= j)
    c[:, C_REV:C_REV + P] = same & (i > j)
    c[:, C_REV + P:C_REV + 2 * P] = same & (i < j)
    for lev in range(NLEV):
        b = 2 ** lev
        bi, bj = i // b, j // b
        c[:, C_LEV + (2 * lev) * P:C_LEV + (2 * lev + 1) * P] = (bi % 2 == 1) & (bj == bi - 1)
        c[:, C_LEV + (2 * lev + 1) * P:C_LEV + (2 * lev + 2) * P] = (bi % 2 == 0) & (bj == bi + 1)
    f = ROPE // 4
    inv = np.power(np.float32(10000.0), -np.arange(f, dtype=np.float32) / np.float32(f)).astype(np.float32)
    t = np.arange(LX)
    ang = np.stack([(t // GRID_W).astype(np.float32)[:, None] * inv,
                    (t % GRID_W).astype(np.float32)[:, None] * inv], axis=1)
    cos = np.ones((TT, P, 2, 2, f), np.float32)
    sin = np.zeros((TT, P, 2, 2, f), np.float32)
    q0 = LC // P
    cos[q0:] = np.cos(ang).reshape(TT - q0, P, 2, 1, f)
    sin[q0:, :, :, 0] = -np.sin(ang).reshape(TT - q0, P, 2, f)
    sin[q0:, :, :, 1] = np.sin(ang).reshape(TT - q0, P, 2, f)
    c[:, C_COS:C_COS + 256] = cos.transpose(1, 0, 2, 3, 4).reshape(P, 256)
    c[:, C_SIN:C_SIN + 256] = sin.transpose(1, 0, 2, 3, 4).reshape(P, 256)
    return c


PR_NORM, PR_ADAB, PR_GLA, PR_GDN, PR_QN, PR_KVN, PR_QNN, PR_KNN, PR_C, PR_CC = 0, 8, 32, 34, 35, 38, 40, 41, 42, 50
PR_N = 58


def weave(*seqs):
    seqs = [list(s) for s in seqs if len(s)]
    tagged = [((i + 0.5) / len(s), n, i, it) for n, s in enumerate(seqs) for i, it in enumerate(s)]
    return [t[3] for t in sorted(tagged, key=lambda t: t[:3])]


def chunk_of(r, n):
    if r == 0:
        return n
    return NCH // 2 - 1 - n if n < NCH // 2 else 3 * NCH // 2 - 1 - n


def step_of(r, c):
    return [chunk_of(r, n) for n in range(NCH)].index(c)


def tiles(l):
    return list(range(TT)) if l < DEPTH - 1 else list(range(LC // P, TT))


def schedule():
    s = [("xin", tt, h) for tt in range(TT) for h in range(2)]
    s += [("par", l) for l in range(DEPTH)]
    s += [("mod", 0, j) for j in range(6)]

    def zs(l, br):
        return [("z", l, br, tt, h) for h in range(2) for tt in tiles(l)]

    def yts(l, br):
        return [("yT", l, br, tt, h) for tt in tiles(l) for h in range(2)]

    def merge(l, br):
        out = []
        for e in range(8):
            out += [("gate", l, br, e), ("ys", l, br, e)]
        return out

    def gla(l):
        out = [("lr", l, 0), ("lr", l, 1)]
        for g in range(2):
            out += weave([("gqk", l, g, j) for j in range(4)] + [("gv", l, g, tt) for tt in range(TT)],
                         [("ga", l, g, tt) for tt in range(TT)])
            out += [("ge", l, g, tt) for tt in range(TT)]
            for h in (2 * g, 2 * g + 1):
                out += [("gb", l, h, r) for r in range(2)]
                out += [("gatt", l, h, r) for r in range(2)]
                out += [("gw", l, h, 0, 0), ("gw", l, h, 1, 0), ("gw", l, h, 0, 1), ("gw", l, h, 1, 1)]
                out += [("go", l, h, tt) for tt in tiles(l) if tt < 2]
                out += [("gw", l, h, 0, 2), ("gw", l, h, 1, 2), ("gw", l, h, 0, 3), ("gw", l, h, 1, 3)]
                out += [("go", l, h, tt) for tt in tiles(l) if tt >= 2]
        return out

    def dproj(l, g):
        out = []
        for j in range(6):
            out += [("dqkv", l, g, j), ("dsilu", l, g, j)]
            if 1 <= j < 5:
                out.append(("dn", l, g, j - 1))
        return out

    def prep(l, g, tt):
        out = [("d1", l, g, tt), ("d2", l, g, tt), ("d3", l, g, tt)]
        for lev in range(NLEV):
            out += [("dx", l, g, tt, lev), ("dy", l, g, tt, lev)]
        return out + [("du", l, g, tt)]

    def scan(l, g, a, b):
        out = []
        for n in range(a, b):
            out += [("sv", l, g, n), ("so", l, g, n)]
        return out

    def gdn(l):
        first = [("ab", l), ("dg", l)] + dproj(l, 0) + weave(prep(l, 0, 0), prep(l, 0, 1))
        rest = []
        for g in range(4):
            if g:
                rest += weave(prep(l, g, 0), prep(l, g, 1))
            rest += weave(scan(l, g, 0, 4), prep(l, g, 2))
            rest += prep(l, g, 3)
            rest += weave(scan(l, g, 4, 8), dproj(l, g + 1) if g < 3 else [])
        return first, rest

    def up(l, g):
        out = []
        for tt in range(TT):
            out.append(("muk", l, g, tt))
            if tt in tiles(l):
                out.append(("muq", l, g, tt))
        for tt in range(TT):
            out.append(("mkT", l, g, tt))
            if tt in tiles(l):
                out.append(("mqT", l, g, tt))
        return out

    def att(l, g):
        u = [(l, h, tt) for h in (2 * g, 2 * g + 1) for tt in tiles(l)]
        out = []
        for i in range(len(u) + 2):
            if i < len(u):
                out.append(("ms",) + u[i])
            if 1 <= i <= len(u):
                out.append(("mp",) + u[i - 1])
            if i >= 2:
                out.append(("mo",) + u[i - 2])
        return out

    def mla(l):
        first = []
        for tt in range(TT):
            first.append(("mkv", l, tt))
            if tt in tiles(l):
                first.append(("mq", l, tt))
        first += up(l, 0)
        rest = att(l, 0)
        for g in range(1, 4):
            rest += up(l, g) + att(l, g)
        return first, rest

    for l in range(DEPTH):
        s += [("norm", l)]
        s += gla(l)
        s += [("rstd", l, 0)]
        first, rest = gdn(l)
        s += weave(first, zs(l, 0) + yts(l, 0))
        s += weave(rest, merge(l, 0) + ([("mod", l + 1, j) for j in range(6)] if l + 1 < DEPTH else []))
        s += [("rstd", l, 1)]
        first, rest = mla(l)
        s += weave(first, zs(l, 1) + yts(l, 1))
        s += weave(rest, merge(l, 1))
        s += zs(l, 2) + yts(l, 2) + merge(l, 2)
        s += [("out", l, e) for e in range(8)]
    s += [("xout", tt, h) for tt in tiles(DEPTH - 1) for h in range(2)]
    return s


PHASE = {"lr": 0, "gqk": 0, "gv": 0, "ga": 0, "ge": 0, "gb": 0, "gatt": 0, "gw": 0, "go": 0,
         "ab": 1, "dg": 1, "dqkv": 1, "dsilu": 1, "dn": 1, "d1": 1, "d2": 1, "d3": 1, "dx": 1, "dy": 1,
         "du": 1, "sv": 1, "so": 1,
         "mkv": 2, "mq": 2, "muk": 2, "muq": 2, "mkT": 2, "mqT": 2, "ms": 2, "mp": 2, "mo": 2}

PROJ = {"xin", "par", "mod", "norm", "z", "yT", "gate", "ys", "out", "xout", "lr", "gqk", "gv", "dqkv",
        "ab", "mkv", "mq"}
NBANK = {"dsilu": 0, "rstd": 0, "dy": 2, "du": 2, "so": 3, "gw": 2, "ge": 2, "mkv": 1, "d3": 1}
READERS = {"xin": ("act",), "par": ("act",), "mod": ("dve",), "norm": ("act",), "z": ("act", "dve"),
           "yT": ("dve",), "gate": ("act",), "ys": ("dve",), "out": ("dve",), "xout": ("act",),
           "lr": ("act",), "gqk": ("act",), "gv": ("act",), "ga": ("act", "dve"), "ge": ("act", "dve"),
           "gb": ("act",), "gatt": ("dve",), "gw": ("dve",), "go": ("act", "dve"),
           "ab": ("dve",), "dg": ("act", "dve"), "dqkv": ("act",), "dn": ("act",), "d1": ("act", "dve"),
           "d2": ("dve",), "d3": ("act",), "dx": ("dve",), "dy": ("dve",), "du": ("act",),
           "sv": ("dve",), "so": ("dve",), "mkv": ("act", "dve"), "mq": ("act", "dve"),
           "muk": ("act", "dve"), "muq": ("act", "dve"), "mkT": ("act",), "mqT": ("act", "dve"),
           "ms": ("act", "dve"), "mp": ("act",), "mo": ("dve",)}


NWORK = 17000
UNIT = 256
NSLOT_W = 6


def units_of(it):
    k, l = it[0], it[1]

    def two(name, *key):
        return [((name, l) + key + (i,), i * UNIT, UNIT) for i in range(2)]

    if k == "mod":
        return two("ada", it[2])
    if k == "lr":
        return [(("alr", l), 0, 32)]
    if k == "gqk":
        return [(("aq" if it[3] < 2 else "ak", l, it[2]), 0, UNIT)]
    if k == "gv":
        return two("av", it[2])
    if k == "z":
        return two("z", it[2], it[4])
    if k in ("gate", "ys"):
        return [((k, l, it[2], it[3] // 2), 0, UNIT)]
    if k == "out":
        return [(("wo", l, it[2] // 2), 0, UNIT)]
    if k == "ab":
        return [(("bab", l), 0, 32)]
    if k == "dqkv":
        return [((("bq", "bk", "bv")[it[3] // 2], l, it[2]), 0, UNIT)]
    if k == "mkv":
        return [(("ckv", l), 0, KVL), (("ckr", l), KVL, ROPE)]
    if k == "mq":
        return [(("cq", l, 0), 0, UNIT), (("cq", l, 1), UNIT, QL - UNIT)]
    if k == "muk":
        return [(("kup", l, it[2]), 0, 512)]
    if k == "muq":
        return [(("qup", l, it[2]), 0, 384)]
    return []


def hybrid_block(nc, x, c, ctx_in, c_ctx, norm_w, ada_w, ada_b, w_in, gla_gate_w2, gla_gate_b, gla_norm_w,
                 gdn_conv_w, gdn_a_log, gdn_dt_bias, gdn_norm_w, mla_q_norm_w, mla_q_up, mla_kv_norm_w,
                 mla_kv_up, mla_qn_nope, mla_qn_rope, mla_kn_nope, mla_kn_rope, w_branch, w_out,
                 consts, out):
    plan = schedule()
    assert len(set(plan)) == len(plan)
    where = {it: i for i, it in enumerate(plan)}
    kinds = {}
    for it in plan:
        kinds.setdefault(it[0], []).append(it)

    banks, before, holder, turn = {}, {}, {}, [0, 0]
    NPROJ = 3
    for it in plan:
        k = it[0]
        ring = 0 if k in PROJ else 1
        size, base = (NPROJ, 0) if ring == 0 else (8 - NPROJ, NPROJ)
        banks[it], before[it] = [], []
        for _ in range(NBANK.get(k, 1)):
            b = base + turn[ring] % size
            turn[ring] += 1
            banks[it].append(b)
            if b in holder:
                before[it].append(holder[b])
            holder[b] = it

    units, width, last_use = [], {}, {}
    for it in plan:
        for u, _, w in units_of(it):
            if u not in last_use:
                units.append(u)
                width[u] = w
            last_use[u] = it
    slot, occupant, replaced, nload, load_of = {}, [None] * NSLOT_W, {}, [0] * NSLOT_W, {}
    first_use = {}
    for it in plan:
        for u, _, _ in units_of(it):
            first_use.setdefault(u, it)
    for u in units:
        i = min(range(NSLOT_W), key=lambda i: -1 if occupant[i] is None else where[last_use[occupant[i]]])
        if occupant[i] is not None:
            assert where[last_use[occupant[i]]] < where[first_use[u]], (u, occupant)
            replaced[u] = occupant[i]
        occupant[i], slot[u] = u, i
        nload[i] += 1
        load_of[u] = nload[i]

    with ExitStack() as stack:
        def sb(name, shape):
            return stack.enter_context(nc.sbuf_tensor(name, shape, F32))

        hT = sb("hT", [P, KT, T])
        ring = sb("ring", [P, NSLOT_W, KT * UNIT])
        MT = sb("MT", [P, KT, T])
        yT = sb("yT", [P, KT, T])
        O = sb("O", [P, TT, D])
        K = sb("K", [P, NCONST])
        PAR = sb("PAR", [P, DEPTH, P])
        CW = sb("CW", [P, DEPTH, CONV * 24])
        MOD = sb("MOD", [P, DEPTH, 24, 2])
        SC = sb("SC", [P, 16])
        SCt = sb("SCt", [P, 2, 16])
        SCW = sb("SCW", [P, 8, 2])
        NW4 = sb("NW4", [P, DEPTH, 2, 4])
        QKW = sb("QKW", [P, DEPTH])
        ONES = sb("ONES", [P, P])
        ALB = sb("ALB", [P, DEPTH, 32])
        RW = sb("RW", [P, DEPTH, 2, ROPE])
        SSQ = sb("SSQ", [P, 2, TT, 8])
        EPSC = sb("EPSC", [P, 1])
        E1 = sb("E1", [P, 2, 512])
        GT = sb("GT", [P, 512])
        SQ = sb("SQ", [P, 2, 512])
        RS = sb("RS", [P, 512])
        WORK = sb("WORK", [P, NWORK])
        xs = nc.dram_tensor("xs", (DEPTH, P, KT, T), F32, kind="Internal").ap()

        top = {}

        def area(phase, n):
            at = top.get(phase, 0)
            top[phase] = at + n
            assert top[phase] <= NWORK, (phase, top[phase])
            return WORK[:, at:at + n]

        W2A = area(0, 1024).rearrange("p (r n) -> p r n", r=2)
        LRT = area(0, 1024).rearrange("p (r n) -> p r n", r=2)
        QK = area(0, 2048).rearrange("p (j n) -> p j n", j=4)
        V = area(0, 2048).rearrange("p (t n) -> p t n", t=4)
        LA = area(0, 2048).rearrange("p (t n) -> p t n", t=4)
        LT1 = area(0, 512)
        EB = area(0, 512)
        EI = area(0, 512)
        AQ = area(0, 1024).rearrange("p (r n) -> p r n", r=2)
        AKI = area(0, 1024).rearrange("p (r n) -> p r n", r=2)
        AKE = area(0, 2048).rearrange("p (t n) -> p t n", t=4)
        AER = EB
        HS = area(0, 2048).rearrange("p (r s n) -> p r s n", r=2, s=4)
        ATT = area(0, 1024).rearrange("p (r n) -> p r n", r=2)
        ADEC = area(0, 16).rearrange("p (r n) -> p r n", r=2)
        NSLOT = 3
        bATT = area(1, NSLOT * 512).rearrange("p (s n) -> p s n", s=NSLOT)
        bQD = area(1, NSLOT * 512).rearrange("p (s n) -> p s n", s=NSLOT)
        bKT = area(1, NSLOT * 256).rearrange("p (s n) -> p s n", s=NSLOT)
        bWT = area(1, NSLOT * 512).rearrange("p (s n) -> p s n", s=NSLOT)
        bU = area(1, NSLOT * 512).rearrange("p (s n) -> p s n", s=NSLOT)
        bD = area(1, NSLOT * 8).rearrange("p (s n) -> p s n", s=NSLOT)
        bLT = area(1, 1024).rearrange("p (s n) -> p s n", s=2)
        bX = area(1, 1024).rearrange("p (s n) -> p s n", s=2)
        bXT = area(1, 1024).rearrange("p (s n) -> p s n", s=2)
        bP = area(1, 1024).rearrange("p (s n) -> p s n", s=2)
        bV2 = area(1, 512).rearrange("p (s n) -> p s n", s=2)
        bDEC = bX
        KQV = area(1, 3072).rearrange("p (j n) -> p j n", j=6)
        PAD = area(1, 520).rearrange("p (s n) -> p s n", s=2)
        bS = area(1, 512)
        bVN = area(1, 256)
        bVE = area(1, 256)
        GG = area(1, 64).rearrange("p (t n) -> p t n", t=4)
        BETA = area(1, 64).rearrange("p (t n) -> p t n", t=4)
        GTMP = area(1, 64).rearrange("p (t n) -> p t n", t=4)
        GTM2 = area(1, 64).rearrange("p (t n) -> p t n", t=4)
        GC = area(1, 64).rearrange("p (t n) -> p t n", t=4)
        EGC = area(1, 64).rearrange("p (t n) -> p t n", t=4)
        ERV = area(1, 64).rearrange("p (t n) -> p t n", t=4)
        EAL = area(1, 16)
        RT = area(2, 4 * TT * ROPE).rearrange("p (q n) -> p q n", q=4)
        MQL = area(2, 3 * 512).rearrange("p (k n) -> p k n", k=3)
        MKL = area(2, 2 * 512).rearrange("p (k n) -> p k n", k=2)
        KRT = area(2, 512)
        MT1 = area(2, 512)
        MT2 = area(2, 512)
        MT3 = area(2, 512)
        ROT = area(2, 256)
        mS = area(2, 16)
        QN = area(2, 512 * 4).rearrange("p (t n) -> p t n", t=4)
        KN = area(2, 256 * 4).rearrange("p (t n) -> p t n", t=4)
        MV = area(2, 2048).rearrange("p (g t n) -> p g t n", g=2, t=4)
        QNT = area(2, 1024).rearrange("p (h n) -> p h n", h=2)
        QRT = area(2, 512)
        KNT = area(2, 1024).rearrange("p (h n) -> p h n", h=2)
        PM = area(2, 1024).rearrange("p (s n) -> p s n", s=2)
        PT = area(2, 1024).rearrange("p (s n) -> p s n", s=2)
        MST = area(2, 24).rearrange("p (s n) -> p s n", s=4)

        bank = [stack.enter_context(nc.psum_tensor(f"bank{i}", [P, 512], F32)) for i in range(8)]

        sems, order = {}, {}

        def signal(it, who, mark=""):
            key = (it[0], who, mark)
            if key not in sems:
                sems[key] = stack.enter_context(nc.semaphore("_".join(x for x in key if x)))
            return sems[key]

        def nth(it, who):
            k = it[0]
            if (k, who) not in order:
                mine = [i for i in kinds[k] if takes_part(i, who)]
                order[k, who] = {i: n + 1 for n, i in enumerate(mine)}
            return order[k, who][it]

        def takes_part(it, who):
            if it[0] == "sv" and who == "pe":
                return it[3] > 0
            if who == "pool":
                return it[3] in tiles(it[1])
            return True

        def done(it, who, mark=""):
            assert takes_part(it, who), (it, who)
            return signal(it, who, mark), nth(it, who)

        chain_sem = {w: stack.enter_context(nc.semaphore(f"{w}_chain")) for w in ("dve", "act", "pool")}
        chain_n = {w: 0 for w in chain_sem}

        def link(eng, me, ins):
            chain_n[me] += 1
            ins.then_inc(chain_sem[me], 1)
            eng.wait_ge(chain_sem[me], chain_n[me])

        s_unit = [stack.enter_context(nc.semaphore(f"unit_in{i}")) for i in range(NSLOT_W)]
        s_const = stack.enter_context(nc.semaphore("const_in"))
        s_tok = stack.enter_context(nc.semaphore("tokens_in"))
        s_par = stack.enter_context(nc.semaphore("par_in"))
        s_row = stack.enter_context(nc.semaphore("rows_in"))
        s_w2 = stack.enter_context(nc.semaphore("w2_in"))
        s_one = stack.enter_context(nc.semaphore("ones_set"))
        s_spill = stack.enter_context(nc.semaphore("spilled"))
        s_back = stack.enter_context(nc.semaphore("reloaded"))
        s_out = stack.enter_context(nc.semaphore("out_written"))
        s_sq = stack.enter_context(nc.semaphore("norm_squares"))
        s_squ = stack.enter_context(nc.semaphore("norm_summed"))
        s_rt = stack.enter_context(nc.semaphore("rotary_tables"))
        s_zero = stack.enter_context(nc.semaphore("zeros_set"))

        def kc(at, n=P):
            return K[:, at:at + n]

        ident = kc(C_ID)

        def cum(r):
            return kc(C_CUM + r * P)

        def rev(r):
            return kc(C_REV + r * P)

        def bc(ap, axis, shape):
            return ap.unsqueeze(axis).broadcast_to(shape)

        def rh(ap, r=2):
            return ap.rearrange("p (r h n) -> p r h n", r=r, h=2)

        def prev_kind(it, back=1):
            i = nth(it, "order") - 1 - back
            return kinds[it[0]][i] if i >= 0 else None

        phase_items = {}
        for it in plan:
            if it[0] in PHASE:
                phase_items.setdefault((it[1], PHASE[it[0]]), []).append(it)
        phase_last = {}
        for key, its in phase_items.items():
            d = {}
            for it in its:
                d[it[0]] = it
            phase_last[key] = list(d.values())

        parts = {"pe": set(), "act": set(), "dve": set(), "pool": set()}
        NOACT = {"mod", "ys", "out", "yT", "dx", "dy", "gatt", "gw", "sv", "so", "mo", "d2", "ab"}
        NODVE = {"xin", "gqk", "gv", "lr", "du", "mp", "xout", "mkT"}
        POOLK = {"d1"}
        for k in kinds:
            if k not in ("dsilu", "rstd"):
                parts["pe"].add(k)
            if k not in NOACT:
                parts["act"].add(k)
            if k not in NODVE:
                parts["dve"].add(k)
            if k in POOLK:
                parts["pool"].add(k)

        def fence(eng, me, it, entered):
            key = (it[1], PHASE[it[0]])
            if key in entered:
                return
            entered.add(key)
            n = key[0] * 3 + key[1]
            if n == 0:
                return
            for lit in phase_last[(n - 1) // 3, (n - 1) % 3]:
                for who in ("pe", "act", "dve", "pool"):
                    if who != me and lit[0] in parts[who]:
                        eng.wait_ge(*done(lit, who))
                if me in ("act", "dve", "pool") and lit[0] in parts[me]:
                    eng.wait_ge(*done(lit, me))

        def psum(it, i=0):
            return bank[banks[it][i]]

        def claim(pe, it):
            for b in before[it]:
                for who in READERS[b[0]]:
                    pe.wait_ge(*done(b, who))
                if b[0] in ("mq", "mkv"):
                    pe.wait_ge(*done(b, "dve", "turned"))

        def rows_of(u):
            return {"kup": KVL // P, "qup": QL // P}.get(u[0], KT)

        def weights(it, i=0):
            u = units_of(it)[i][0]
            n = rows_of(u)
            return ring[:, slot[u], 0:n * width[u]].rearrange("p (k n) -> p k n", k=n)

        def units_here(pe, it):
            for u, _, _ in units_of(it):
                pe.wait_ge(s_unit[slot[u]], 16 * load_of[u])

        def unit_source(u):
            kind, l = u[0], u[1]
            w = w_in[l]
            at = {"ada": lambda: (ada_w[l], u[2] * 512 + u[3] * UNIT),
                  "alr": lambda: (w, COL["alr"]),
                  "aq": lambda: (w, COL["aq"] + u[2] * UNIT),
                  "ak": lambda: (w, COL["ak"] + u[2] * UNIT),
                  "av": lambda: (w, COL["av"] + u[2] * 512 + u[3] * UNIT),
                  "z": lambda: (w, COL["abc"[u[2]] + "z"] + u[3] * 512 + u[4] * UNIT),
                  "gate": lambda: (w, COL["mg"] + u[2] * D + u[3] * UNIT),
                  "ys": lambda: (w_branch[l, u[2]], u[3] * UNIT),
                  "wo": lambda: (w_out[l], u[2] * UNIT),
                  "bab": lambda: (w, COL["bab"]),
                  "bq": lambda: (w, COL["bq"] + u[2] * UNIT),
                  "bk": lambda: (w, COL["bk"] + u[2] * UNIT),
                  "bv": lambda: (w, COL["bv"] + u[2] * UNIT),
                  "ckv": lambda: (w, COL["ckv"]),
                  "ckr": lambda: (w, COL["ckr"]),
                  "cq": lambda: (w, COL["cq"] + u[2] * UNIT),
                  "qup": lambda: (mla_q_up[l], u[2] * 384),
                  "kup": lambda: (mla_kv_up[l], u[2] * 512)}[kind]
            src, c0 = at()
            return src[:, c0:c0 + width[u]].rearrange("(k p) n -> p k n", p=P)

        E1T = SQ

        def dpar(it):
            return it[3] % 2

        def slot_of(it):
            return (it[2] * TT + it[3]) % NSLOT

        def slot_free(eng, me, it):
            l, g, tt = it[1], it[2], it[3]
            n = g * TT + tt - NSLOT
            if n >= 0:
                pg, pt = n // TT, n % TT
                eng.wait_ge(*done(("so", l, pg, 3 if pt < 2 else 7), "pe"))
                eng.wait_ge(*done(("so", l, pg, 3 if pt < 2 else 7), "dve"))

        def seg(ap2d, s):
            return ap2d[:, s * LC:(s + 1) * LC]

        bSQ = RS

        def ms_par(it):
            return nth(it, "act") % 2

        def exp_sig(act, out_ap, in_ap):
            return nc.scalar.activation(out_ap, in_ap, ACT.Exp, scale=-1.0)

        CA = GT
        CE = sb("CE", [P, T])

        zg = [i for i in plan if i[0] in ("z", "gate")]
        zg_index = {i: n for n, i in enumerate(zg)}

        def plan_prev(it, ks):
            i = where[it] - 1
            while i >= 0:
                if plan[i][0] in ks:
                    return plan[i]
                i -= 1
            return None

        def tile_before(it, n):
            d1s = kinds["d1"]
            i = d1s.index(("d1", it[1], it[2], it[3])) - n
            return d1s[i] if i >= 0 else None

        def rope(dve, dst, src, q, tt, nh):
            cwt = RT[:, 2 * q, tt * ROPE:(tt + 1) * ROPE]
            swt = RT[:, 2 * q + 1, tt * ROPE:(tt + 1) * ROPE]
            for i in range(nh):
                sv = src[:, i * ROPE:(i + 1) * ROPE]
                link(dve, "dve", nc.vector.tensor_tensor(dst[:, i * ROPE:(i + 1) * ROPE], sv, cwt, ALU.mult))
                for hf in range(2):
                    s4 = sv.rearrange("p (a h f) -> p a h f", a=2, h=2)[:, :, 1 - hf, :]
                    w4 = swt.rearrange("p (a h f) -> p a h f", a=2, h=2)[:, :, hf, :]
                    d4 = ROT[:, i * ROPE:(i + 1) * ROPE].rearrange("p (a h f) -> p a h f", a=2, h=2)[:, :, hf, :]
                    ins = nc.vector.tensor_tensor(d4, s4, w4, ALU.mult)
                link(dve, "dve", ins)
                ins = nc.vector.tensor_tensor(dst[:, i * ROPE:(i + 1) * ROPE], dst[:, i * ROPE:(i + 1) * ROPE],
                                              ROT[:, i * ROPE:(i + 1) * ROPE], ALU.add)
            return ins
        block = stack.enter_context(nc.Block())

        @block.sync
        def _(sp):
            sp.dma_start(K[:, :], consts).then_inc(s_const, 16)
            sp.dma_start(O[:, 0:2, :], ctx_in[0].rearrange("(t p) d -> p t d", p=P)).then_inc(s_tok, 16)
            sp.dma_start(O[:, 2:4, :], x[0].rearrange("(t p) d -> p t d", p=P)).then_inc(s_tok, 16)
            for l in range(DEPTH):
                st = MT[:, l, 0:P]
                for row, src in ((PR_NORM, norm_w[l]), (PR_ADAB, ada_b[l]), (PR_GLA, gla_norm_w[l]),
                                 (PR_GDN, gdn_norm_w[l]), (PR_QN, mla_q_norm_w[l]), (PR_KVN, mla_kv_norm_w[l]),
                                 (PR_QNN, mla_qn_nope[l]), (PR_KNN, mla_kn_nope[l]), (PR_C, c[0]), (PR_CC, c_ctx)):
                    n = src.shape[0] // P
                    sp.dma_start(MT[row:row + n, l, 0:P], src.rearrange("(r c) -> r c", c=P)).then_inc(s_par, 16)
                sp.dma_start(MT[0:CONV * 24, 2 + l, 0:P], gdn_conv_w[l].rearrange("j (r c) -> (j r) c", c=P)).then_inc(s_par, 16)
                sp.dma_start(ALB[:, l, 0:16], gdn_a_log[l].rearrange("r h -> (r h)").partition_broadcast(P)).then_inc(s_row, 16)
                sp.dma_start(ALB[:, l, 16:32], gdn_dt_bias[l].rearrange("r h -> (r h)").partition_broadcast(P)).then_inc(s_row, 16)
                sp.dma_start(RW[:, l, 0, :], mla_qn_rope[l].partition_broadcast(P)).then_inc(s_row, 16)
                sp.dma_start(RW[:, l, 1, :], mla_kn_rope[l].partition_broadcast(P)).then_inc(s_row, 16)
            for u in units:
                if u in replaced:
                    sp.wait_ge(*done(last_use[replaced[u]], "pe"))
                n = rows_of(u)
                sp.dma_start(ring[:, slot[u], 0:n * width[u]].rearrange("p (k n) -> p k n", k=n),
                             unit_source(u)).then_inc(s_unit[slot[u]], 16)

        @block.gpsimd
        def _(pool):
            entered = set()
            pool.memset(ONES[:, :], 1.0).then_inc(s_one, 1)
            pool.memset(EPSC[:, :], EPS).then_inc(s_one, 1)
            for it in plan:
                k = it[0]
                if k in PHASE and (k in POOLK or k in ("lr", "dqkv")):
                    fence(pool, "pool", it, entered)
                if k == "lr" and it[2] == 0:
                    l = it[1]
                    pool.dma_start(W2A[0:RANK, :, :], gla_gate_w2[l].rearrange("r i k -> i r k")).then_inc(s_w2, 16)
                    pool.dma_start(W2A[RANK:RANK + 1, :, :], gla_gate_b[l:l + 1]).then_inc(s_w2, 16)
                    pool.memset(LRT[0:RANK + 1, :, :], 1.0).then_inc(s_zero, 1)
                    pool.memset(ATT[:, :, :], 0.0).then_inc(s_zero, 1)
                elif k == "dqkv" and it[2] == 0 and it[3] == 0:
                    pool.memset(PAD[:, :, :], 0.0).then_inc(s_zero, 1)
                elif k == "d1":
                    _, l, g, tt = it
                    sl = slot_of(it)
                    if tt in tiles(l):
                        pool.wait_ge(*done(it, "act", "egr"))
                        pool.wait_ge(*done(("dn", l, g, 1), "dve"))
                        slot_free(pool, "pool", it)
                        for r in range(2):
                            ins = pool.tensor_tensor(
                                bQD[:, sl, r * 256:r * 256 + 256].rearrange("p (h n) -> p h n", h=2),
                                KQV[:, 0:2, tt * P:tt * P + P],
                                E1T[:, dpar(it), r * 256:r * 256 + 256].rearrange("p (h n) -> p h n", h=2),
                                ALU.mult)
                        ins.then_inc(signal(it, "pool"), 1)
                elif k == "norm":
                    l = it[1]
                    last = ("xin", TT - 1, 1) if l == 0 else ("out", l - 1, 7)
                    pool.wait_ge(*done(last, "act" if l == 0 else "dve"))
                    pool.dma_start(xs[l], yT[:, :, :]).then_inc(s_spill, 16)
                elif k == "out" and it[2] == 0:
                    l = it[1]
                    pool.wait_ge(s_spill, 16 * (l + 1))
                    pool.wait_ge(*done(("ys", l, 2, 7), "pe"))
                    pool.dma_start(yT[:, :, :], xs[l]).then_inc(s_back, 16)
            for tt in tiles(DEPTH - 1):
                pool.wait_ge(*done(("xout", tt, 1), "act"))
                r0 = tt * P - LC
                pool.dma_start(out[0, r0:r0 + P, :], O[:, tt, :]).then_inc(s_out, 16)
            pool.wait_ge(s_out, 16 * len(tiles(DEPTH - 1)))

        @block.tensor
        def _(pe):
            entered = set()

            def mm(o, a, b, start=True, stop=True):
                return nc.tensor.matmul(o, a, b, start=start, stop=stop, skip_group_check=True)

            def tr(o, a):
                return nc.tensor.transpose(o, a, ident)

            pe.wait_ge(s_const, 16)
            pe.wait_ge(s_one, 2)
            for it in plan:
                k, l = it[0], it[1]
                if k not in parts["pe"] or not takes_part(it, "pe"):
                    continue
                if k in PHASE:
                    fence(pe, "pe", it, entered)
                claim(pe, it)
                ps = psum(it)
                q0 = 0 if (len(it) and k not in ("xin", "xout", "par") and l < DEPTH - 1) else LC
                if k == "xin":
                    _, tt, h = it
                    pe.wait_ge(s_tok, 32)
                    for j in range(4):
                        ins = tr(ps[:, j * P:(j + 1) * P], O[:, tt, (4 * h + j) * P:(4 * h + j + 1) * P])
                elif k == "xout":
                    _, tt, h = it
                    pe.wait_ge(*done(("out", DEPTH - 1, 7), "dve"))
                    for j in range(4):
                        ins = tr(ps[:, j * P:(j + 1) * P], yT[:, 4 * h + j, tt * P:(tt + 1) * P])
                elif k == "par":
                    pe.wait_ge(s_par, 16 * 22)
                    tr_in = MT[0:PR_N, l, 0:P]
                    nc.tensor.transpose(ps[:, 0:PR_N], tr_in, K[0:PR_N, C_ID:C_ID + PR_N])
                    n = CONV * 24
                    ins = nc.tensor.transpose(ps[:, P:P + n], MT[0:n, 2 + l, 0:P], K[0:n, C_ID:C_ID + n])
                elif k == "mod":
                    units_here(pe, it)
                    pe.wait_ge(*done(("par", 0), "dve"))
                    for t in range(4):
                        w = weights(it, t // 2)
                        for kk in range(KT):
                            ins = mm(ps[:, 2 * t:2 * t + 2], w[:, kk, (t % 2) * P:(t % 2 + 1) * P], SC[:, kk:kk + 9:8],
                                     kk == 0, kk == KT - 1)
                elif k == "norm":
                    for kk in range(KT):
                        pe.wait_ge(s_sq, l * KT + kk + 1)
                        ins = mm(ps[:, :], ONES[:, :], SQ[:, kk % 2, :], kk == 0, kk == KT - 1)
                        if kk < KT - 1:
                            ins.then_inc(s_squ, 1)
                elif k == "lr":
                    units_here(pe, it)
                    pe.wait_ge(*done(("norm", l), "dve"))
                    w = weights(it)
                    for kk in range(KT):
                        ins = mm(ps[0:RANK, :], w[:, kk, it[2] * RANK:(it[2] + 1) * RANK], hT[:, kk, :],
                                 kk == 0, kk == KT - 1)
                elif k in ("gqk", "dqkv", "gate", "ys", "out"):
                    units_here(pe, it)
                    src, j = hT, it[-1]
                    if k == "ys":
                        src = yT
                        for tt in tiles(l):
                            pe.wait_ge(*done(("yT", l, it[2], tt, 1), "dve"))
                    elif k == "out":
                        src = MT
                        pe.wait_ge(*done(("ys", l, 2, 7), "dve"))
                    a0 = 0 if (k in ("gqk", "dqkv") and j >= 2) else q0
                    w = weights(it)[:, :, (j % 2) * P:(j % 2 + 1) * P]
                    for kk in range(KT):
                        ins = mm(ps[:, a0:T], w[:, kk, :], src[:, kk, a0:T], kk == 0, kk == KT - 1)
                elif k in ("gv", "z", "mkv", "mq"):
                    units_here(pe, it)
                    tt = it[3] if k in ("gv", "z") else it[2]
                    for i, (_, c0, wd) in enumerate(units_of(it)):
                        for kk in range(KT):
                            ins = mm(ps[:, c0:c0 + wd], hT[:, kk, tt * P:(tt + 1) * P], weights(it, i)[:, kk, :],
                                     kk == 0, kk == KT - 1)
                elif k == "ab":
                    units_here(pe, it)
                    for tt in range(TT):
                        for kk in range(KT):
                            ins = mm(ps[:, tt * 32:tt * 32 + 32], hT[:, kk, tt * P:(tt + 1) * P], weights(it)[:, kk, :],
                                     kk == 0, kk == KT - 1)
                elif k == "yT":
                    _, l, br, tt, h = it
                    pe.wait_ge(*done(("z", l, br, tt, h), "dve"))
                    for j in range(4):
                        ins = tr(ps[:, j * P:(j + 1) * P], O[:, tt, (4 * h + j) * P:(4 * h + j + 1) * P])
                elif k == "ga":
                    _, l, g, tt = it
                    pe.wait_ge(*done(("lr", l, 0), "act"))
                    pe.wait_ge(*done(("lr", l, 1), "act"))
                    pe.wait_ge(s_w2, 32 * (l + 1))
                    for r in range(2):
                        ins = mm(ps[:, r * 256:r * 256 + 256], LRT[0:RANK + 1, r, tt * P:(tt + 1) * P],
                                 W2A[0:RANK + 1, r, g * 256:g * 256 + 256])
                elif k == "gb":
                    _, l, h, r = it
                    g, hh = h // 2, h % 2
                    for tt in range(TT):
                        pe.wait_ge(*done(("ga", l, g, tt), "dve"))
                        ins = mm(ps[:, tt * P:(tt + 1) * P], LA[:, tt, (2 * r + hh) * P:(2 * r + hh + 1) * P], cum(r))
                elif k == "ge":
                    _, l, g, tt = it
                    pe.wait_ge(*done(("ga", l, g, tt), "dve"))
                    for r in range(2):
                        mm(ps[:, r * 256:r * 256 + 256], rev(r), LA[:, tt, r * 256:r * 256 + 256])
                    for hh in range(2):
                        pe.wait_ge(*done(("gqk", l, g, 2 + hh), "act"))
                        ins = tr(psum(it, 1)[:, hh * P:(hh + 1) * P], QK[:, 2 + hh, tt * P:(tt + 1) * P])
                elif k == "gatt":
                    _, l, h, r = it
                    pe.wait_ge(*done(("gb", l, h, r), "dve"))
                    for tt in tiles(l):
                        ins = mm(ps[:, tt * P:(tt + 1) * P], AKI[:, r, tt * P:(tt + 1) * P],
                                 AQ[:, r, tt * P:(tt + 1) * P])
                elif k == "gw":
                    _, l, h, r, m = it
                    hh = h % 2
                    for i in range(2):
                        n = 2 * m + i
                        if n == NCH - 1:
                            continue
                        cc = chunk_of(r, n)
                        tt, p0 = cc // 2, (cc % 2) * CH
                        pe.wait_ge(*done(("ge", l, h // 2, tt), "dve"))
                        pe.wait_ge(*done(("gv", l, h // 2, tt), "act"))
                        ins = mm(psum(it, i)[:, 0:256], AKE[p0:p0 + CH, tt, (2 * r + hh) * P:(2 * r + hh + 1) * P],
                                 V[p0:p0 + CH, tt, hh * ADV:(hh + 1) * ADV])
                elif k == "go":
                    _, l, h, tt = it
                    hh = h % 2
                    for r in range(2):
                        pe.wait_ge(*done(("gatt", l, h, r), "dve"))
                        pe.wait_ge(*done(("gw", l, h, r, 1 if tt < 2 else 3), "dve"))
                        mm(ps[:, 0:ADV], ATT[:, r, tt * P:(tt + 1) * P], V[:, tt, hh * ADV:(hh + 1) * ADV],
                           r == 0, False)
                    todo = [(r, cc) for r in range(2) for cc in (2 * tt, 2 * tt + 1) if step_of(r, cc) > 0]
                    for i, (r, cc) in enumerate(todo):
                        p0 = (cc % 2) * CH
                        ins = mm(ps[p0:p0 + CH, 0:ADV], AQ[:, r, cc * CH:(cc + 1) * CH],
                                 HS[:, r, step_of(r, cc) % 4, :], False, i >= len(todo) - 2)
                elif k == "dg":
                    pe.wait_ge(*done(it, "dve", "gg"))
                    for tt in range(TT):
                        for r in range(2):
                            a = GG[:, tt, r * BH:(r + 1) * BH]
                            mm(ps[:, tt * 16 + r * BH:tt * 16 + (r + 1) * BH], cum(r), a)
                            ins = mm(ps[:, 64 + tt * 16 + r * BH:64 + tt * 16 + (r + 1) * BH], rev(r), a)
                elif k == "dn":
                    pe.wait_ge(*done(it, "act", "sq"))
                    a0 = q0 if it[3] < 2 else 0
                    ins = mm(ps[:, a0:T], ONES[:, :], bSQ[:, a0:T])
                elif k == "d1":
                    _, l, g, tt = it
                    pe.wait_ge(*done(("dg", l), "dve"))
                    for r in range(2):
                        for hh in range(2):
                            u = 2 * r + hh
                            ins = mm(ps[:, u * P:(u + 1) * P],
                                     GG[:, tt, r * BH + 2 * g + hh:r * BH + 2 * g + hh + 1].broadcast_to([P, P]), cum(r))
                elif k == "d2":
                    _, l, g, tt = it
                    for j in range(4):
                        if j >= 2 or l < DEPTH - 1 or tt >= 2:
                            pe.wait_ge(*done(("dn", l, g, j), "dve"))
                    for hh in range(2):
                        kk = KQV[:, 2 + hh, tt * P:(tt + 1) * P]
                        ins = mm(ps[:, hh * P:(hh + 1) * P], kk, kk)
                    if tt in tiles(l):
                        for hh in range(2):
                            ins = mm(ps[:, (2 + hh) * P:(3 + hh) * P], KQV[:, 2 + hh, tt * P:(tt + 1) * P],
                                     KQV[:, hh, tt * P:(tt + 1) * P])
                elif k == "d3":
                    _, l, g, tt = it
                    pe.wait_ge(*done(("dsilu", l, g, 5), "dve"))
                    for j in range(4):
                        ins = tr(ps[:, j * P:(j + 1) * P], KQV[:, 2 + j, tt * P:(tt + 1) * P])
                elif k == "dx":
                    _, l, g, tt, lev = it
                    s = dpar(it)
                    pe.wait_ge(*done(("dy", l, g, tt, lev - 1) if lev else ("d3", l, g, tt), "dve"))
                    for u in range(4):
                        ins = mm(ps[:, u * P:(u + 1) * P], bLT[:, s, u * P:(u + 1) * P], bX[:, s, u * P:(u + 1) * P])
                elif k == "dy":
                    _, l, g, tt, lev = it
                    s = dpar(it)
                    pe.wait_ge(*done(("dx", l, g, tt, lev), "dve"))
                    for u in range(4):
                        c4 = slice(u * P, (u + 1) * P)
                        if lev < NLEV - 1:
                            mm(ps[:, c4], bXT[:, s, c4], bP[:, s, c4])
                        ins = mm(psum(it, 1)[:, c4], bP[:, s, c4], bXT[:, s, c4])
                elif k == "du":
                    _, l, g, tt = it
                    s = dpar(it)
                    pe.wait_ge(*done(("dy", l, g, tt, NLEV - 1), "dve"))
                    pe.wait_ge(*done(("d3", l, g, tt), "act"))
                    for u in range(4):
                        c4 = slice(u * P, (u + 1) * P)
                        mm(ps[:, c4], bXT[:, s, c4], bV2[:, s, (u % 2) * P:(u % 2 + 1) * P])
                        ins = mm(psum(it, 1)[:, c4], bKT[:, slot_of(it), (u % 2) * P:(u % 2 + 1) * P], bP[:, s, c4])
                elif k == "sv":
                    _, l, g, n = it
                    pe.wait_ge(*done(("so", l, g, n - 1), "dve"))
                    for r in range(2):
                        cc = chunk_of(r, n)
                        tt, p0 = cc // 2, (cc % 2) * CH
                        pe.wait_ge(*done(("du", l, g, tt), "act"))
                        sl = slot_of(("d1", l, g, tt))
                        for hh in range(2):
                            u = 2 * r + hh
                            ins = mm(ps[p0:p0 + CH, hh * P:(hh + 1) * P],
                                     bWT[:, sl, u * P + p0:u * P + p0 + CH], bS[:, u * P:(u + 1) * P])
                elif k == "so":
                    _, l, g, n = it
                    pe.wait_ge(*done(("sv", l, g, n), "dve"))
                    for r in range(2):
                        cc = chunk_of(r, n)
                        tt, p0 = cc // 2, (cc % 2) * CH
                        sl = slot_of(("d1", l, g, tt))
                        if tt in tiles(l):
                            pe.wait_ge(*done(("d1", l, g, tt), "pool"))
                        for hh in range(2):
                            u = 2 * r + hh
                            vn = bVN[p0:p0 + CH, hh * P:(hh + 1) * P]
                            if tt in tiles(l):
                                o = ps[p0:p0 + CH, hh * P:(hh + 1) * P]
                                if n:
                                    mm(o, bQD[:, sl, u * P + p0:u * P + p0 + CH], bS[:, u * P:(u + 1) * P], True, False)
                                ins = mm(o, bATT[p0:p0 + CH, sl, u * P + p0:u * P + p0 + CH], vn, n == 0, True)
                            if n < NCH - 1:
                                ins = mm(psum(it, 1 + r)[:, hh * P:(hh + 1) * P], bKT[p0:p0 + CH, sl, hh * P:(hh + 1) * P],
                                         bVE[p0:p0 + CH, hh * P:(hh + 1) * P])
                elif k == "muk":
                    _, l, g, tt = it
                    units_here(pe, it)
                    pe.wait_ge(*done(("mkv", l, tt), "dve", "turned"))
                    w = weights(it)
                    for kk in range(2):
                        ins = mm(ps[:, :], MKL[:, kk, tt * P:(tt + 1) * P], w[:, kk, :], kk == 0, kk == 1)
                elif k == "muq":
                    _, l, g, tt = it
                    units_here(pe, it)
                    pe.wait_ge(*done(("mq", l, tt), "dve", "turned"))
                    w = weights(it)
                    for kk in range(3):
                        ins = mm(ps[:, 0:384], MQL[:, kk, tt * P:(tt + 1) * P], w[:, kk, :], kk == 0, kk == 2)
                elif k == "mkT":
                    _, l, g, tt = it
                    pe.wait_ge(*done(("muk", l, g, tt), "dve"))
                    for hh in range(2):
                        ins = tr(ps[:, hh * P:(hh + 1) * P], KN[:, tt, hh * P:(hh + 1) * P])
                elif k == "mqT":
                    _, l, g, tt = it
                    pe.wait_ge(*done(("muq", l, g, tt), "dve"))
                    for j in range(3):
                        ins = tr(ps[:, j * P:(j + 1) * P], QN[:, tt, j * P:(j + 1) * P])
                elif k == "ms":
                    _, l, h, tt = it
                    g, hh = h // 2, h % 2
                    nk = LC if tt < 2 else T
                    pe.wait_ge(*done(("mqT", l, g, tt), "act"))
                    pe.wait_ge(*done(("mqT", l, g, tt), "dve"))
                    pe.wait_ge(*done(("mkT", l, g, nk // P - 1), "act"))
                    mm(ps[:, 0:nk], QNT[:, hh, tt * P:(tt + 1) * P], KNT[:, hh, 0:nk], True, False)
                    ins = mm(ps[:, 0:nk], QRT[hh * 64:hh * 64 + 64, tt * P:(tt + 1) * P],
                             KRT[hh * 64:hh * 64 + 64, 0:nk], False, True)
                elif k == "mp":
                    _, l, h, tt = it
                    nk = LC if tt < 2 else T
                    pe.wait_ge(*done(("ms", l, h, tt), "act"))
                    s = ms_par(it)
                    for j in range(nk // P):
                        ins = tr(ps[:, j * P:(j + 1) * P], PM[:, s, j * P:(j + 1) * P])
                elif k == "mo":
                    _, l, h, tt = it
                    nk = LC if tt < 2 else T
                    pe.wait_ge(*done(("mp", l, h, tt), "act"))
                    s = ms_par(it)
                    n = nk // P
                    for j in range(n):
                        ins = mm(ps[:, 0:P], PT[:, s, j * P:(j + 1) * P],
                                 MV[:, (h // 2) % 2, j, (h % 2) * P:(h % 2 + 1) * P], j == 0, j == n - 1)
                else:
                    raise AssertionError(k)
                ins.then_inc(signal(it, "pe"), 1)
                if k in ("mq", "mkv"):
                    pe.wait_ge(*done(it, "dve"))
                    nt = 3
                    for j in range(nt):
                        ins = tr(ps[:, j * P:(j + 1) * P], MT1[:, j * P:(j + 1) * P])
                    ins.then_inc(signal(it, "pe", "turned"), 1)

        @block.scalar
        def _(act):
            entered = set()

            def rsqrt(dst, src, n, final=None):
                link(act, "act", nc.scalar.activation(dst, src, ACT.Ln, bias=EPSC[0:dst.shape[0], :], scale=1.0 / n))
                return nc.scalar.activation(dst, dst, ACT.Exp, scale=-0.5)

            act.wait_ge(s_one, 2)
            for it in plan:
                k, l = it[0], it[1]
                if k not in parts["act"]:
                    continue
                if k in PHASE:
                    fence(act, "act", it, entered)
                ps = psum(it) if banks[it] else None
                if k in parts["pe"] and k not in ("norm", "dg", "dn"):
                    act.wait_ge(*done(it, "pe"))
                mine = signal(it, "act")
                q0 = 0 if (k not in ("xin", "xout", "par") and l < DEPTH - 1) else LC
                if k == "xin":
                    _, tt, h = it
                    ins = nc.scalar.activation(yT[:, 4 * h:4 * h + 4, tt * P:(tt + 1) * P],
                                               ps[:, :].rearrange("p (j n) -> p j n", j=4), ACT.Copy)
                elif k == "xout":
                    _, tt, h = it
                    ins = nc.scalar.activation(O[:, tt, h * 512:(h + 1) * 512], ps[:, :], ACT.Copy)
                elif k == "par":
                    nc.scalar.activation(CW[:, l, :], ps[:, P:P + CONV * 24], ACT.Copy)
                    link(act, "act", nc.scalar.activation(PAR[:, l, 0:PR_N], ps[:, 0:PR_N], ACT.Copy))
                    ins = nc.scalar.activation(SCt[:, 0, :], PAR[:, l, PR_C:PR_C + 16], ACT.Exp, scale=-1.0) if l == 0 else \
                        nc.scalar.activation(SCt[:, 1, 0:1], EPSC[:, :], ACT.Copy)
                elif k == "norm":
                    if l:
                        act.wait_ge(*done(("out", l - 1, 7), "dve"))
                    else:
                        act.wait_ge(*done(("xin", TT - 1, 1), "act"))
                    for kk in range(KT):
                        n = l * (KT - 1) + kk
                        if kk >= 2:
                            act.wait_ge(s_squ, l * (KT - 1) + kk - 1)
                        elif l:
                            act.wait_ge(*done(("norm", l - 1), "pe"))
                        nc.scalar.activation(SQ[:, kk % 2, :], yT[:, kk, :], ACT.Square).then_inc(s_sq, 1)
                    act.wait_ge(*done(it, "pe"))
                    if l:
                        act.wait_ge(*done(("norm", l - 1), "dve"))
                    ins = rsqrt(RS[:, :], ps[:, :], D)
                elif k == "lr":
                    act.wait_ge(s_zero, 3 * l + 1)
                    ins = nc.scalar.activation(LRT[0:RANK, it[2], :], ps[0:RANK, :], ACT.Copy)
                elif k == "gqk":
                    _, l, g, j = it
                    if g:
                        act.wait_ge(*done(("gb", l, 2 * g - 1, 1), "dve"))
                        act.wait_ge(*done(("ge", l, g - 1, TT - 1), "pe"))
                    a0 = q0 if j < 2 else 0
                    ins = nc.scalar.activation(QK[:, j, a0:T], ps[:, a0:T], ACT.Copy)
                elif k == "gv":
                    _, l, g, tt = it
                    if g:
                        act.wait_ge(*done(("go", l, 2 * g - 1, TT - 1), "pe"))
                    ins = nc.scalar.activation(V[:, tt, :], ps[:, :], ACT.Copy)
                elif k == "ga":
                    p = prev_kind(it)
                    if p:
                        act.wait_ge(*done(p, "dve"))
                    p = plan_prev(it, ("go",))
                    if p:
                        act.wait_ge(*done(p, "act"))
                    link(act, "act", nc.scalar.activation(LT1, ps[:, :], ACT.Abs))
                    link(act, "act", nc.scalar.activation(LT1, LT1, ACT.Exp, scale=-1.0))
                    ins = nc.scalar.activation(LT1, LT1, ACT.Ln, bias=1.0)
                elif k == "gb":
                    p = prev_kind(it)
                    if p:
                        act.wait_ge(*done(p, "dve"))
                    act.wait_ge(*done(("ge", l, it[2] // 2, TT - 1), "dve"))
                    nc.scalar.activation(EB, ps[:, :], ACT.Exp, scale=1.0 / 16)
                    ins = nc.scalar.activation(EI, ps[:, :], ACT.Exp, scale=-1.0 / 16)
                elif k == "ge":
                    p = prev_kind(it)
                    if p:
                        act.wait_ge(*done(p, "dve"))
                    if it[2] and it[3] == 0:
                        act.wait_ge(*done(("gb", l, 2 * it[2] - 1, 1), "dve"))
                    ins = nc.scalar.activation(AER, ps[:, :], ACT.Exp, scale=1.0 / 16)
                elif k == "go":
                    _, l, h, tt = it
                    act.wait_ge(*done(plan_prev(it, ("go", "ga")), "act"))
                    if plan_prev(it, ("go", "ga"))[0] == "ga":
                        act.wait_ge(*done(plan_prev(it, ("ga",)), "dve"))
                    ins = nc.scalar.activation(LT1[:, 0:ADV], ps[:, 0:ADV], ACT.Square,
                                               accum_out=SSQ[:, 0, tt, h:h + 1])
                elif k == "rstd":
                    _, l, br = it
                    t0 = tiles(l)[0]
                    nh = AH if br == 0 else BH
                    hd = D // nh
                    if br == 0:
                        act.wait_ge(*done(("go", l, AH - 1, TT - 1), "act"))
                    else:
                        act.wait_ge(*done(("so", l, 3, NCH - 1), "dve"))
                        for tt in tiles(l):
                            for h in range(BH):
                                if h == 0 and tt == t0:
                                    pass
                                link(act, "act", nc.scalar.activation(RS[:, 0:P], O[:, tt, h * P:(h + 1) * P], ACT.Square,
                                                       accum_out=SSQ[:, 1, tt, h:h + 1]))
                    ins = rsqrt(SSQ[:, br, t0:TT, 0:nh], SSQ[:, br, t0:TT, 0:nh], hd)
                elif k in ("z", "gate"):
                    n = zg_index[it]
                    if n >= 2:
                        act.wait_ge(*done(zg[n - 2], "dve"))
                        if zg[n - 2][0] == "gate":
                            act.wait_ge(*done(("ys",) + zg[n - 2][1:], "dve"))
                    a0 = q0 if k == "gate" else 0
                    ins = exp_sig(act, E1[:, n % 2, a0:512], ps[:, a0:512])
                elif k == "dg":
                    act.wait_ge(s_row, 16 * 8)
                    nc.scalar.activation(EAL, ALB[:, l, 0:16], ACT.Exp)
                    act.wait_ge(*done(it, "dve", "adt"))
                    link(act, "act", nc.scalar.activation(GTM2[:, :, :], GTMP[:, :, :], ACT.Abs))
                    nc.scalar.activation(BETA[:, :, :], BETA[:, :, :], ACT.Exp, scale=-1.0)
                    link(act, "act", nc.scalar.activation(GTM2[:, :, :], GTM2[:, :, :], ACT.Exp, scale=-1.0))
                    nc.scalar.activation(GTM2[:, :, :], GTM2[:, :, :], ACT.Ln, bias=1.0).then_inc(signal(it, "act", "sp"), 1)
                    act.wait_ge(*done(it, "pe"))
                    nc.scalar.activation(EGC[:, :, :], ps[:, 0:64].rearrange("p (t n) -> p t n", t=4), ACT.Exp)
                    ins = nc.scalar.activation(ERV[:, :, :], ps[:, 64:128].rearrange("p (t n) -> p t n", t=4), ACT.Exp)
                elif k == "dqkv":
                    act.wait_ge(s_zero, 3 * l + 3)
                    p = prev_kind(it)
                    if p:
                        act.wait_ge(*done(p, "dve"))
                    a0 = 1 if (it[3] < 2 and l == DEPTH - 1) else 0
                    ins = nc.scalar.activation(PAD[:, a0:2, 2:258],
                                               ps[:, a0 * LC:T].rearrange("p (s n) -> p s n", n=LC), ACT.Copy)
                elif k == "dsilu":
                    act.wait_ge(*done(("dqkv",) + it[1:], "dve"))
                    p = prev_kind(it)
                    if p:
                        act.wait_ge(*done(p, "dve"))
                    a0 = q0 if it[3] < 2 else 0
                    ins = exp_sig(act, CE[:, a0:T], CA[:, a0:T])
                elif k == "dn":
                    _, l, g, j = it
                    a0 = q0 if j < 2 else 0
                    act.wait_ge(*done(("dsilu", l, g, j), "dve"))
                    p = prev_kind(it)
                    if p:
                        act.wait_ge(*done(p, "dve"))
                    nc.scalar.activation(bSQ[:, a0:T], KQV[:, j, a0:T], ACT.Square).then_inc(signal(it, "act", "sq"), 1)
                    act.wait_ge(*done(it, "pe"))
                    ins = rsqrt(bSQ[:, a0:T], ps[:, a0:T], 1.0)
                elif k == "d1":
                    _, l, g, tt = it
                    s = dpar(it)
                    pit = tile_before(it, 2)
                    if pit:
                        if pit[3] in tiles(pit[1]):
                            act.wait_ge(*done(pit, "pool"))
                        act.wait_ge(*done(pit, "dve"))
                    nc.scalar.activation(E1T[:, s, :], ps[:, :], ACT.Exp).then_inc(signal(it, "act", "egr"), 1)
                    act.wait_ge(*done(it, "dve", "dif"))
                    ins = nc.scalar.activation(bDEC[:, s, :], bDEC[:, s, :], ACT.Exp)
                elif k == "d3":
                    _, l, g, tt = it
                    s = dpar(it)
                    pit = tile_before(it, 2)
                    if pit:
                        act.wait_ge(*done(("du",) + pit[1:], "pe"))
                    slot_free(act, "act", it)
                    nc.scalar.activation(bKT[:, slot_of(it), :], ps[:, 0:256], ACT.Copy)
                    ins = nc.scalar.activation(bV2[:, s, :], ps[:, 256:512], ACT.Copy)
                elif k == "du":
                    sl = slot_of(it)
                    slot_free(act, "act", it)
                    nc.scalar.activation(bU[:, sl, :], ps[:, :], ACT.Copy)
                    ins = nc.scalar.activation(bWT[:, sl, :], psum(it, 1)[:, :], ACT.Copy)
                elif k in ("mq", "mkv"):
                    p = plan_prev(it, ("mq", "mkv"))
                    if p:
                        act.wait_ge(*done(p, "dve"))
                    w = QL if k == "mq" else KVL
                    nc.scalar.activation(MT2[:, 0:w], ps[:, 0:w], ACT.Square, accum_out=mS[:, 0:1])
                    if k == "mkv":
                        nc.scalar.activation(MT2[:, w:w + 64], ps[:, w:w + 64], ACT.Square, accum_out=mS[:, 1:2])
                        link(act, "act", nc.scalar.activation(mS[:, 3:4], EPSC[:, :], ACT.Copy))
                        rsq = nc.scalar.activation(mS[:, 1:2], mS[:, 1:2], ACT.Ln, bias=EPSC[:, :], scale=1.0 / ROPE)
                        link(act, "act", rsq)
                    else:
                        link(act, "act", nc.scalar.activation(mS[:, 3:4], EPSC[:, :], ACT.Copy))
                    link(act, "act", nc.scalar.activation(mS[:, 0:1], mS[:, 0:1], ACT.Ln, bias=EPSC[:, :], scale=1.0 / w))
                    n = 2 if k == "mkv" else 1
                    ins = nc.scalar.activation(mS[:, 0:n], mS[:, 0:n], ACT.Exp, scale=-0.5)
                elif k == "muk":
                    _, l, g, tt = it
                    p = plan_prev(it, ("muk", "muq", "mq", "mkv"))
                    if p:
                        act.wait_ge(*done(p, "dve"))
                    v4 = ps[:, :].rearrange("p (h w n) -> p h w n", h=2, w=2)
                    if g >= 2:
                        act.wait_ge(*done(("mo", l, 2 * (g - 2) + 1, TT - 1), "pe"))
                    nc.scalar.activation(MV[:, g % 2, tt, :].rearrange("p (h n) -> p h n", h=2), v4[:, :, 1, :], ACT.Copy)
                    nc.scalar.activation(MT2[:, 0:256].rearrange("p (h n) -> p h n", h=2), v4[:, :, 0, :],
                                         ACT.Square).then_inc(signal(it, "act", "sq"), 1)
                    act.wait_ge(*done(it, "dve", "ssq"))
                    ins = rsqrt(mS[:, 4:6], mS[:, 4:6], NOPE)
                elif k == "muq":
                    p = plan_prev(it, ("muk", "muq", "mq", "mkv"))
                    act.wait_ge(*done(p, "dve"))
                    nc.scalar.activation(MT2[:, 0:384], ps[:, 0:384], ACT.Square).then_inc(signal(it, "act", "sq"), 1)
                    act.wait_ge(*done(it, "dve", "ssq"))
                    nc.scalar.activation(mS[:, 4:6], mS[:, 4:6], ACT.Ln, bias=EPSC[:, :], scale=1.0 / NOPE)
                    link(act, "act", nc.scalar.activation(mS[:, 6:8], mS[:, 6:8], ACT.Ln, bias=EPSC[:, :], scale=1.0 / ROPE))
                    ins = nc.scalar.activation(mS[:, 4:8], mS[:, 4:8], ACT.Exp, scale=-0.5)
                elif k == "mkT":
                    _, l, g, tt = it
                    if g:
                        act.wait_ge(*done(("ms", l, 2 * g - 1, TT - 1), "pe"))
                    ins = nc.scalar.activation(KNT[:, :, tt * P:(tt + 1) * P],
                                               ps[:, 0:256].rearrange("p (h n) -> p h n", h=2), ACT.Copy)
                elif k == "mqT":
                    _, l, g, tt = it
                    if g:
                        act.wait_ge(*done(("ms", l, 2 * g - 1, TT - 1), "pe"))
                    ins = nc.scalar.activation(QRT[:, tt * P:(tt + 1) * P], ps[:, 256:384], ACT.Copy)
                elif k == "ms":
                    _, l, h, tt = it
                    nk = LC if tt < 2 else T
                    s = ms_par(it)
                    act.wait_ge(*done(it, "dve", "max"))
                    p = prev_kind(it, 2)
                    if p:
                        act.wait_ge(*done(("mp",) + p[1:], "pe"))
                    ins = nc.scalar.activation(PM[:, s, 0:nk], ps[:, 0:nk], ACT.Exp, bias=MST[:, nth(it, "act") % 4, 0:1],
                                               scale=MSCALE, accum_out=MST[:, nth(it, "act") % 4, 1:2])
                elif k == "mp":
                    _, l, h, tt = it
                    nk = LC if tt < 2 else T
                    s = ms_par(it)
                    p = prev_kind(it, 2)
                    if p:
                        act.wait_ge(*done(("mo",) + p[1:], "pe"))
                    ins = nc.scalar.activation(PT[:, s, 0:nk], ps[:, 0:nk], ACT.Copy)
                else:
                    raise AssertionError(k)
                ins.then_inc(mine, 1)

        @block.vector
        def _(dve):
            entered = set()
            V_ = nc.vector
            for it in plan:
                k, l = it[0], it[1]
                if k not in parts["dve"]:
                    continue
                if k in PHASE:
                    fence(dve, "dve", it, entered)
                ps = psum(it) if banks[it] else None
                if k in parts["pe"] and takes_part(it, "pe") and k not in ("dg",):
                    dve.wait_ge(*done(it, "pe"))
                mine = signal(it, "dve")
                q0 = 0 if (k not in ("par",) and l < DEPTH - 1) else LC

                def ln(ins):
                    link(dve, "dve", ins)

                if k == "par":
                    dve.wait_ge(*done(it, "act"))
                    if l == 0:
                        ln(V_.tensor_scalar(SCt[:, 0, :], SCt[:, 0, :], 1.0, None, ALU.add))
                        ln(V_.reciprocal(SCt[:, 0, :], SCt[:, 0, :]))
                        ln(V_.tensor_tensor(SC[:, :], SCt[:, 0, :], PAR[:, l, PR_C:PR_C + 16], ALU.mult))
                    V_.tensor_tensor(QKW[:, l:l + 1], PAR[:, l, PR_QNN:PR_QNN + 1], PAR[:, l, PR_KNN:PR_KNN + 1], ALU.mult)
                    V_.tensor_copy(NW4[:, l, 0, :].rearrange("p (a b) -> p a b", a=2),
                                   bc(PAR[:, l, PR_GLA:PR_GLA + 2], 1, [P, 2, 2]))
                    ins = V_.tensor_copy(NW4[:, l, 1, :], PAR[:, l, PR_GDN:PR_GDN + 1].broadcast_to([P, 4]))
                elif k == "mod":
                    _, l, j = it
                    o = V_.tensor_tensor(MOD[:, l, 4 * j:4 * j + 4, :], ps[:, 0:8].rearrange("p (t s) -> p t s", s=2),
                                         bc(PAR[:, l, PR_ADAB + 4 * j:PR_ADAB + 4 * j + 4], 2, [P, 4, 2]), ALU.add)
                    ins = o
                elif k == "norm":
                    dve.wait_ge(*done(it, "act"))
                    dve.wait_ge(*done(("mod", l, 5), "dve"))
                    ln(V_.tensor_scalar(SCW[:, :, :], MOD[:, l, 8:16, :], 1.0, None, ALU.add))
                    ln(V_.tensor_tensor(SCW[:, :, :], SCW[:, :, :], bc(PAR[:, l, PR_NORM:PR_NORM + 8], 2, [P, 8, 2]), ALU.mult))
                    if l:
                        for br in range(3):
                            dve.wait_ge(*done(("gate", l - 1, br, 7), "pe"))
                    for kk in range(KT):
                        ins = V_.tensor_tensor(hT[:, kk, :], yT[:, kk, :], RS[:, :], ALU.mult)
                    ln(ins)
                    for kk in range(KT):
                        for s in range(2):
                            sel = 1 - s
                            ins = V_.tensor_scalar(seg(hT[:, kk, :], s), seg(hT[:, kk, :], s), SCW[:, kk, sel:sel + 1],
                                                   MOD[:, l, kk, sel:sel + 1], ALU.mult, ALU.add)
                elif k == "z":
                    _, l, br, tt, h = it
                    n = zg_index[it]
                    e = E1[:, n % 2, :]
                    dve.wait_ge(*done(it, "act"))
                    ln(V_.tensor_scalar(e, e, 1.0, None, ALU.add))
                    ln(V_.reciprocal(e, e))
                    o = O[:, tt, h * 512:(h + 1) * 512]
                    if br < 2:
                        nh = (AH if br == 0 else BH) // 2
                        dve.wait_ge(*done(("rstd", l, br), "act"))
                        V_.tensor_tensor(e, e, ps[:, :], ALU.mult)
                        if br == 0:
                            dve.wait_ge(*done(("go", l, AH - 1, TT - 1), "dve"))
                        else:
                            dve.wait_ge(*done(("so", l, 3, NCH - 1), "dve"))
                        ln(V_.tensor_tensor(o.rearrange("p (h n) -> p h n", h=nh), o.rearrange("p (h n) -> p h n", h=nh),
                                            bc(SSQ[:, br, tt, h * nh:(h + 1) * nh], 2, [P, nh, 512 // nh]), ALU.mult))
                    else:
                        dve.wait_ge(*done(("mo", l, MH - 1, TT - 1), "dve"))
                        ln(V_.tensor_tensor(e, e, ps[:, :], ALU.mult))
                    ins = V_.tensor_tensor(o, o, e, ALU.mult)
                elif k == "yT":
                    _, l, br, tt, h = it
                    if br:
                        dve.wait_ge(*done(("ys", l, br - 1, 7), "pe"))
                    else:
                        dve.wait_ge(s_spill, 16 * (l + 1))
                    dst = yT[:, 4 * h:4 * h + 4, tt * P:(tt + 1) * P]
                    src = ps[:, :].rearrange("p (j n) -> p j n", j=4)
                    if br < 2:
                        ins = V_.tensor_tensor(dst, src, bc(NW4[:, l, br, :], 2, [P, 4, P]), ALU.mult)
                    else:
                        ins = V_.tensor_copy(dst, src)
                elif k == "gate":
                    n = zg_index[it]
                    e = E1[:, n % 2, q0:512]
                    dve.wait_ge(*done(it, "act"))
                    ln(V_.tensor_scalar(e, e, 1.0, None, ALU.add))
                    ins = V_.reciprocal(e, e)
                elif k == "ys":
                    _, l, br, e8 = it
                    gi = ("gate",) + it[1:]
                    e = E1[:, zg_index[gi] % 2, q0:512]
                    dve.wait_ge(*done(gi, "dve"))
                    m = MT[:, e8, q0:T]
                    if br == 0:
                        if l:
                            dve.wait_ge(*done(("out", l - 1, 7), "pe"))
                        ins = V_.tensor_tensor(m, ps[:, q0:T], e, ALU.mult)
                    else:
                        dve.wait_ge(*done(("ys", l, br - 1, e8), "dve"))
                        ln(V_.tensor_tensor(e, ps[:, q0:T], e, ALU.mult))
                        ins = V_.tensor_tensor(m, m, e, ALU.add)
                elif k == "out":
                    _, l, e8 = it
                    dve.wait_ge(s_back, 16 * (l + 1))
                    for s in range(q0 // LC, 2):
                        sel = 1 - s
                        ins = V_.scalar_tensor_tensor(seg(yT[:, e8, :], s), ps[:, s * LC:(s + 1) * LC],
                                                      MOD[:, l, 16 + e8, sel:sel + 1], seg(yT[:, e8, :], s),
                                                      ALU.mult, ALU.add)
                elif k == "ga":
                    _, l, g, tt = it
                    dve.wait_ge(*done(it, "act"))
                    if g:
                        dve.wait_ge(*done(("gb", l, 2 * g - 1, 1), "pe"))
                        dve.wait_ge(*done(("ge", l, g - 1, TT - 1), "pe"))
                    ins = V_.scalar_tensor_tensor(LA[:, tt, :], ps[:, :], 0.0, LT1, ALU.min, ALU.subtract)
                elif k == "gb":
                    _, l, h, r = it
                    g, hh = h // 2, h % 2
                    dve.wait_ge(*done(it, "act"))
                    if h:
                        dve.wait_ge(*done(("go", l, h - 1, TT - 1), "pe"))
                        dve.wait_ge(*done(("gatt", l, h - 1, 1), "pe"))
                        dve.wait_ge(*done(("gw", l, h - 1, r, 3), "dve"))
                    e0 = CH - 1 if r == 0 else 0
                    V_.tensor_copy(ADEC[:, r, :], EB[:, e0:e0 + T - CH + 1:CH])
                    dve.wait_ge(*done(("gqk", l, g, hh), "act"))
                    V_.scalar_tensor_tensor(AQ[:, r, q0:T], QK[:, hh, q0:T], ADK ** -0.5, EB[:, q0:T], ALU.mult, ALU.mult)
                    dve.wait_ge(*done(("gqk", l, g, 2 + hh), "act"))
                    ins = V_.tensor_tensor(AKI[:, r, :], QK[:, 2 + hh, :], EI, ALU.mult)
                elif k == "ge":
                    _, l, g, tt = it
                    dve.wait_ge(*done(it, "act"))
                    if g:
                        dve.wait_ge(*done(("gw", l, 2 * g - 1, 1, 3), "pe"))
                        dve.wait_ge(*done(("gw", l, 2 * g - 1, 0, 3), "pe"))
                    kt = psum(it, 1)[:, 0:256].rearrange("p (h n) -> p h n", h=2)
                    for r in range(2):
                        ins = V_.tensor_tensor(AKE[:, tt, r * 256:(r + 1) * 256].rearrange("p (h n) -> p h n", h=2),
                                               AER[:, r * 256:(r + 1) * 256].rearrange("p (h n) -> p h n", h=2), kt, ALU.mult)
                elif k == "gatt":
                    _, l, h, r = it
                    if h:
                        dve.wait_ge(*done(("go", l, h - 1, TT - 1), "pe"))
                    dve.wait_ge(s_zero, 3 * l + 2)
                    nt = len(tiles(l))
                    ins = V_.copy_predicated(ATT[:, r, q0:T].rearrange("p (t n) -> p t n", t=nt),
                                             bc(cum(r).bitcast(U32), 1, [P, nt, P]),
                                             ps[:, q0:T].rearrange("p (t n) -> p t n", t=nt))
                elif k == "gw":
                    _, l, h, r, m = it
                    if m >= 2 and l < DEPTH - 1:
                        dve.wait_ge(*done(("go", l, h, 1), "pe"))
                    elif h:
                        dve.wait_ge(*done(("go", l, h - 1, TT - 1), "pe"))
                    dve.wait_ge(*done(("gb", l, h, r), "dve"))
                    for i in range(2):
                        n = 2 * m + i
                        if n == NCH - 1:
                            continue
                        cc = chunk_of(r, n)
                        w = psum(it, i)[:, 0:256]
                        if n == 0:
                            ln(V_.tensor_copy(HS[:, r, 1, :], w))
                        else:
                            if i == 0:
                                dve.wait_ge(*done(("gw", l, h, r, m - 1), "dve"))
                            ins = V_.scalar_tensor_tensor(HS[:, r, (n + 1) % 4, :], HS[:, r, n % 4, :], ADEC[:, r, cc:cc + 1],
                                                          w, ALU.mult, ALU.add)
                            if i == 0 and n + 1 < NCH - 1:
                                ln(ins)
                elif k == "go":
                    _, l, h, tt = it
                    dve.wait_ge(*done(it, "act"))
                    ins = V_.tensor_copy(O[:, tt, h * ADV:(h + 1) * ADV], ps[:, 0:ADV])
                elif k == "rstd":
                    ins = V_.tensor_copy(SCt[:, 1, 1:2], EPSC[:, :])
                elif k == "ab":
                    dve.wait_ge(s_row, 16 * 8)
                    v = ps[:, 0:128].rearrange("p (t n) -> p t n", t=4)
                    V_.tensor_tensor(GTMP[:, :, :], v[:, :, 0:16], bc(ALB[:, l, 16:32], 1, [P, 4, 16]), ALU.add)
                    ins = V_.tensor_copy(BETA[:, :, :], v[:, :, 16:32])
                elif k == "dg":
                    dve.wait_ge(*done(("ab", l), "dve"))
                    ln(V_.tensor_copy(GC[:, :, :], GTMP[:, :, :]))
                    V_.tensor_scalar(GC[:, :, :], GC[:, :, :], 0.0, None, ALU.max).then_inc(signal(it, "dve", "adt"), 1)
                    dve.wait_ge(*done(it, "act", "sp"))
                    ln(V_.tensor_scalar(BETA[:, :, :], BETA[:, :, :], 1.0, None, ALU.add))
                    ln(V_.reciprocal(BETA[:, :, :], BETA[:, :, :]))
                    ln(V_.tensor_tensor(GG[:, :, :], GC[:, :, :], GTM2[:, :, :], ALU.add))
                    V_.scalar_tensor_tensor(GG[:, :, :], GG[:, :, :], -1.0, bc(EAL, 1, [P, 4, 16]), ALU.mult,
                                            ALU.mult).then_inc(signal(it, "dve", "gg"), 1)
                    dve.wait_ge(*done(it, "pe"))
                    dve.wait_ge(*done(it, "act"))
                    ln(V_.tensor_copy(GC[:, :, :], ps[:, 0:64].rearrange("p (t n) -> p t n", t=4)))
                    ins = V_.memset(bS, 0.0)
                elif k == "dqkv":
                    _, l, g, j = it
                    dve.wait_ge(*done(it, "act"))
                    p = prev_kind(it)
                    if p:
                        dve.wait_ge(*done(("dsilu",) + p[1:], "act"))
                        dve.wait_ge(*done(("dsilu",) + p[1:], "dve"))
                    a0 = 1 if (j < 2 and l == DEPTH - 1) else 0
                    tile = (j // 2) * 8 + 2 * g + j % 2
                    acc = CA[:, a0 * LC:T].rearrange("p (s n) -> p s n", n=LC)
                    for tap in range(CONV):
                        wv = CW[:, l, tap * 24 + tile:tap * 24 + tile + 1]
                        src = PAD[:, a0:2, tap:tap + LC]
                        if tap == 0:
                            ln(V_.tensor_scalar(acc, src, wv, None, ALU.mult))
                        else:
                            ins = V_.scalar_tensor_tensor(acc, src, wv, acc, ALU.mult, ALU.add)
                            if tap < CONV - 1:
                                ln(ins)
                elif k == "dsilu":
                    _, l, g, j = it
                    dve.wait_ge(*done(it, "act"))
                    a0 = q0 if j < 2 else 0
                    ln(V_.tensor_scalar(CE[:, a0:T], CE[:, a0:T], 1.0, None, ALU.add))
                    ln(V_.reciprocal(CE[:, a0:T], CE[:, a0:T]))
                    if g:
                        dve.wait_ge(*done(("d3", l, g - 1, TT - 1), "pe"))
                        dve.wait_ge(*done(("d1", l, g - 1, TT - 1), "pool"))
                    ins = V_.tensor_tensor(KQV[:, j, a0:T], CA[:, a0:T], CE[:, a0:T], ALU.mult)
                elif k == "dn":
                    _, l, g, j = it
                    dve.wait_ge(*done(it, "act"))
                    a0 = q0 if j < 2 else 0
                    sc = BDK ** -0.5 if j < 2 else 1.0
                    ins = V_.scalar_tensor_tensor(KQV[:, j, a0:T], KQV[:, j, a0:T], sc, bSQ[:, a0:T], ALU.mult, ALU.mult)
                elif k == "d1":
                    _, l, g, tt = it
                    s, sl = dpar(it), slot_of(it)
                    pit = tile_before(it, 2)
                    if pit:
                        dve.wait_ge(*done(("dx",) + pit[1:] + (NLEV - 1,), "pe"))
                    slot_free(dve, "dve", it)
                    dve.wait_ge(*done(it, "act", "egr"))
                    dif = bDEC[:, s, :].rearrange("p (u n) -> p u n", u=4)
                    gcs = GC[:, tt, :].rearrange("p (r h) -> p r h", r=2)[:, :, 2 * g:2 * g + 2]
                    for r in range(2):
                        ins = V_.tensor_tensor(dif[:, 2 * r:2 * r + 2, :],
                                               ps[:, r * 256:(r + 1) * 256].rearrange("p (h n) -> p h n", h=2),
                                               bc(gcs[:, r, :], 2, [P, 2, P]), ALU.subtract)
                    ln(ins)
                    V_.tensor_scalar(bDEC[:, s, :], bDEC[:, s, :], 0.0, None, ALU.min).then_inc(signal(it, "dve", "dif"), 1)
                    dve.wait_ge(*done(it, "act", "egr"))
                    for r in range(2):
                        e0 = CH - 1 if r == 0 else 0
                        ins = V_.tensor_copy(
                            bD[:, sl, 4 * r:4 * r + 4].rearrange("p (h c) -> p h c", h=2),
                            E1T[:, s, r * 256:(r + 1) * 256].rearrange("p (h c n) -> p h c n", h=2, n=CH)[:, :, :, e0])
                elif k == "d2":
                    _, l, g, tt = it
                    s, sl = dpar(it), slot_of(it)
                    dve.wait_ge(*done(("d1", l, g, tt), "act"))
                    pit = tile_before(it, 2)
                    if pit:
                        dve.wait_ge(*done(("dx",) + pit[1:] + (NLEV - 1,), "pe"))
                    gv = ps[:, 0:256]
                    kv = ps[:, 256:512]
                    for r in range(2):
                        c2 = slice(r * 256, (r + 1) * 256)
                        ins = V_.tensor_tensor(bLT[:, s, c2], gv, bDEC[:, s, c2], ALU.mult)
                    if tt in tiles(l):
                        slot_free(dve, "dve", it)
                        ln(ins)
                        for r in range(2):
                            c2 = slice(r * 256, (r + 1) * 256)
                            ins = V_.tensor_tensor(bDEC[:, s, c2].rearrange("p (h n) -> p h n", h=2),
                                                   bDEC[:, s, c2].rearrange("p (h n) -> p h n", h=2),
                                                   bc(cum(r), 1, [P, 2, P]), ALU.mult)
                        ln(ins)
                        for r in range(2):
                            c2 = slice(r * 256, (r + 1) * 256)
                            ins = V_.tensor_tensor(bATT[:, sl, c2], kv, bDEC[:, s, c2], ALU.mult)
                elif k == "d3":
                    _, l, g, tt = it
                    s, sl = dpar(it), slot_of(it)
                    pit = tile_before(it, 2)
                    if pit:
                        dve.wait_ge(*done(("du",) + pit[1:], "pe"))
                    slot_free(dve, "dve", it)
                    dve.wait_ge(*done(("dg", l), "act"))
                    dve.wait_ge(*done(("dg", l), "dve"))
                    dve.wait_ge(*done(("d2", l, g, tt), "dve"))

                    def per(tab, r):
                        return bc(tab[:, tt, r * BH + 2 * g:r * BH + 2 * g + 2], 2, [P, 2, P])

                    for r in range(2):
                        c2 = slice(r * 256, (r + 1) * 256)

                        def h2(a):
                            return a.rearrange("p (h n) -> p h n", h=2)

                        V_.tensor_tensor(h2(bX[:, s, c2]), bc(ident, 1, [P, 2, P]), per(BETA, r), ALU.mult)
                        ins = V_.tensor_tensor(h2(bXT[:, s, c2]), bc(ident, 1, [P, 2, P]), per(BETA, r), ALU.mult)
                elif k == "dx":
                    _, l, g, tt, lev = it
                    s = dpar(it)
                    pit = tile_before(it, 2)
                    if pit and lev == 0:
                        dve.wait_ge(*done(("du",) + pit[1:], "pe"))
                    lm = K[:, C_LEV + 2 * lev * P:C_LEV + (2 * lev + 2) * P].rearrange("p (r n) -> p r n", r=2)
                    for r in range(2):
                        c2 = slice(r * 256, (r + 1) * 256)
                        ins = V_.tensor_tensor(bP[:, s, c2].rearrange("p (h n) -> p h n", h=2),
                                               ps[:, c2].rearrange("p (h n) -> p h n", h=2),
                                               bc(lm[:, r, :], 1, [P, 2, P]), ALU.mult)
                elif k == "dy":
                    _, l, g, tt, lev = it
                    s = dpar(it)
                    dve.wait_ge(*done(("dy", l, g, tt, lev - 1) if lev else ("d3", l, g, tt), "dve"))
                    if lev < NLEV - 1:
                        V_.tensor_tensor(bX[:, s, :], bX[:, s, :], ps[:, :], ALU.subtract)
                    ins = V_.tensor_tensor(bXT[:, s, :], bXT[:, s, :], psum(it, 1)[:, :], ALU.subtract)
                    if lev == NLEV - 1:
                        ln(ins)
                        for r in range(2):
                            c2 = slice(r * 256, (r + 1) * 256)
                            ins = V_.tensor_tensor(bP[:, s, c2].rearrange("p (h n) -> p h n", h=2),
                                                   bXT[:, s, c2].rearrange("p (h n) -> p h n", h=2),
                                                   bc(EGC[:, tt, r * BH + 2 * g:r * BH + 2 * g + 2], 2, [P, 2, P]), ALU.mult)
                elif k == "sv":
                    _, l, g, n = it
                    p = prev_kind(it)
                    if p:
                        dve.wait_ge(*done(("so",) + p[1:], "pe"))
                    for r in range(2):
                        cc = chunk_of(r, n)
                        tt, p0 = cc // 2, (cc % 2) * CH
                        sl = slot_of(("d1", l, g, tt))
                        dve.wait_ge(*done(("du", l, g, tt), "act"))
                        u = bU[p0:p0 + CH, sl, r * 256:(r + 1) * 256]
                        vn = bVN[p0:p0 + CH, :]
                        if n:
                            ins = V_.tensor_tensor(vn, u, ps[p0:p0 + CH, 0:256], ALU.subtract)
                        else:
                            ins = V_.tensor_copy(vn, u)
                    ln(ins)
                    for r in range(2):
                        cc = chunk_of(r, n)
                        tt, p0 = cc // 2, (cc % 2) * CH
                        ins = V_.tensor_tensor(bVE[p0:p0 + CH, :].rearrange("p (h n) -> p h n", h=2),
                                               bVN[p0:p0 + CH, :].rearrange("p (h n) -> p h n", h=2),
                                               bc(ERV[p0:p0 + CH, tt, r * BH + 2 * g:r * BH + 2 * g + 2], 2, [CH, 2, P]), ALU.mult)
                elif k == "so":
                    _, l, g, n = it
                    p = prev_kind(it)
                    if p:
                        dve.wait_ge(*done(p, "dve"))
                    if n < NCH - 1:
                        for r in range(2):
                            cc = chunk_of(r, n)
                            tt = cc // 2
                            sl = slot_of(("d1", l, g, tt))
                            dve.wait_ge(*done(("d1", l, g, tt), "dve"))
                            for hh in range(2):
                                u = 2 * r + hh
                                cs = slice(u * P, (u + 1) * P)
                                if n:
                                    ins = V_.scalar_tensor_tensor(bS[:, cs], bS[:, cs], bD[:, sl, 2 * u + cc % 2:2 * u + cc % 2 + 1],
                                                                  psum(it, 1 + r)[:, hh * P:(hh + 1) * P], ALU.mult, ALU.add)
                                else:
                                    ins = V_.tensor_copy(bS[:, cs], psum(it, 1 + r)[:, hh * P:(hh + 1) * P])
                    if chunk_of(0, n) // 2 in tiles(l):
                        for tt in tiles(l):
                            dve.wait_ge(*done(("yT", l, 0, tt, 1), "pe"))
                        for r in range(2):
                            cc = chunk_of(r, n)
                            tt, p0 = cc // 2, (cc % 2) * CH
                            o = O[p0:p0 + CH, tt, g * 256:(g + 1) * 256]
                            if step_of(1 - r, cc) > n:
                                ins = V_.tensor_copy(o, ps[p0:p0 + CH, 0:256])
                            else:
                                ins = V_.tensor_tensor(o, o, ps[p0:p0 + CH, 0:256], ALU.add)
                elif k in ("mq", "mkv"):
                    _, l, tt = it
                    dve.wait_ge(*done(it, "act"))
                    p = plan_prev(it, ("mq", "mkv"))
                    if p:
                        dve.wait_ge(*done(p, "pe", "turned"))
                    if k == "mkv" and tt == 0:
                        for q in range(2):
                            w = RW[:, l, q, :]
                            cwt = RT[:, 2 * q, :].rearrange("p (t n) -> p t n", t=TT)
                            V_.tensor_tensor(cwt, kc(C_COS, 256).rearrange("p (t n) -> p t n", t=TT), bc(w, 1, [P, TT, ROPE]), ALU.mult)
                            for a in range(2):
                                for hf in range(2):
                                    d = RT[:, 2 * q + 1, :].rearrange("p (t a h f) -> p t a h f", t=TT, a=2, h=2)[:, :, a, hf, :]
                                    sn = kc(C_SIN, 256).rearrange("p (t a h f) -> p t a h f", t=TT, a=2, h=2)[:, :, a, hf, :]
                                    ws = w.rearrange("p (a h f) -> p a h f", a=2, h=2)[:, a, 1 - hf, :]
                                    ins = V_.tensor_tensor(d, sn, bc(ws, 1, [P, TT, 16]), ALU.mult)
                        ln(ins)
                    if k == "mq":
                        ins = V_.tensor_scalar(MT1[:, 0:QL], ps[:, 0:QL], mS[:, 0:1], None, ALU.mult)
                    else:
                        V_.tensor_scalar(MT1[:, 0:KVL], ps[:, 0:KVL], mS[:, 0:1], None, ALU.mult)
                        ln(V_.tensor_scalar(MT3[:, 0:64], ps[:, KVL:KVL + 64], mS[:, 1:2], None, ALU.mult))
                        rope(dve, MT1[:, KVL:KVL + 64], MT3[:, 0:64], 1, tt, 1)
                        link(dve, "dve", V_.tensor_copy(MT3[:, 64:65], EPSC[:, :]))
                        ins = V_.tensor_copy(MT1[:, KVL + 64:KVL + 128], MT1[:, KVL:KVL + 64])
                    ins.then_inc(mine, 1)
                    dve.wait_ge(*done(it, "pe", "turned"))
                    n = 3 if k == "mq" else 2
                    dst = (MQL if k == "mq" else MKL)[:, :, tt * P:(tt + 1) * P]
                    pr = PR_QN if k == "mq" else PR_KVN
                    ins = V_.tensor_tensor(dst, ps[:, 0:n * P].rearrange("p (j n) -> p j n", j=n),
                                           bc(PAR[:, l, pr:pr + n], 2, [P, n, P]), ALU.mult)
                    if k == "mkv":
                        ins = V_.tensor_copy(KRT[:, tt * P:(tt + 1) * P], ps[:, 256:384])
                    ins.then_inc(signal(it, "dve", "turned"), 1)
                    continue
                elif k == "muk":
                    _, l, g, tt = it
                    dve.wait_ge(*done(it, "act", "sq"))
                    V_.tensor_reduce(mS[:, 4:6], MT2[:, 0:256].rearrange("p (h n) -> p h n", h=2), AX_X,
                                     ALU.add).then_inc(signal(it, "dve", "ssq"), 1)
                    dve.wait_ge(*done(it, "act"))
                    if g:
                        dve.wait_ge(*done(("mkT", l, g - 1, tt), "pe"))
                    v4 = ps[:, :].rearrange("p (h w n) -> p h w n", h=2, w=2)
                    ins = V_.tensor_tensor(KN[:, tt, :].rearrange("p (h n) -> p h n", h=2), v4[:, :, 0, :],
                                           bc(mS[:, 4:6], 2, [P, 2, P]), ALU.mult)
                elif k == "muq":
                    _, l, g, tt = it
                    dve.wait_ge(*done(it, "act", "sq"))
                    m2 = MT2[:, 0:384].rearrange("p (h n) -> p h n", h=2)
                    V_.tensor_reduce(mS[:, 4:6], m2[:, :, 0:NOPE], AX_X, ALU.add)
                    V_.tensor_reduce(mS[:, 6:8], m2[:, :, NOPE:192], AX_X, ALU.add).then_inc(signal(it, "dve", "ssq"), 1)
                    dve.wait_ge(*done(it, "act"))
                    if g:
                        dve.wait_ge(*done(("mqT", l, g - 1, tt), "pe"))
                    v3 = ps[:, 0:384].rearrange("p (h n) -> p h n", h=2)
                    V_.tensor_tensor(QN[:, tt, 0:256].rearrange("p (h n) -> p h n", h=2), v3[:, :, 0:NOPE],
                                     bc(mS[:, 4:6], 2, [P, 2, P]), ALU.mult)
                    ln(V_.tensor_tensor(MT3[:, 0:128].rearrange("p (h n) -> p h n", h=2), v3[:, :, NOPE:192],
                                        bc(mS[:, 6:8], 2, [P, 2, ROPE]), ALU.mult))
                    ins = rope(dve, QN[:, tt, 256:384], MT3[:, 0:128], 0, tt, 2)
                elif k == "mqT":
                    _, l, g, tt = it
                    if g:
                        dve.wait_ge(*done(("ms", l, 2 * g - 1, TT - 1), "pe"))
                    dve.wait_ge(*done(it, "act"))
                    ins = V_.tensor_scalar(QNT[:, :, tt * P:(tt + 1) * P], ps[:, 0:256].rearrange("p (h n) -> p h n", h=2),
                                           QKW[:, l:l + 1], None, ALU.mult)
                elif k == "ms":
                    _, l, h, tt = it
                    nk = LC if tt < 2 else T
                    j = nth(it, "act") % 4
                    p = prev_kind(it, 4)
                    if p:
                        dve.wait_ge(*done(("mo",) + p[1:], "dve"))
                        dve.wait_ge(*done(p, "act"))
                    ln(V_.tensor_reduce(MST[:, j, 2:3], ps[:, 0:nk], AX_X, ALU.max))
                    V_.tensor_scalar(MST[:, j, 0:1], MST[:, j, 2:3], -MSCALE, None, ALU.mult).then_inc(signal(it, "dve", "max"), 1)
                    dve.wait_ge(*done(it, "act"))
                    ins = V_.reciprocal(MST[:, j, 3:4], MST[:, j, 1:2])
                elif k == "mo":
                    _, l, h, tt = it
                    j = nth(it, "act") % 4
                    dve.wait_ge(*done(("ms", l, h, tt), "dve"))
                    for t in tiles(l):
                        dve.wait_ge(*done(("yT", l, 1, t, 1), "pe"))
                    ins = V_.tensor_scalar(O[:, tt, h * P:(h + 1) * P], ps[:, 0:P], MST[:, j, 3:4], None, ALU.mult)
                else:
                    raise AssertionError(k)
                ins.then_inc(mine, 1)

    return nc


_INS = ["x", "c", "ctx", "c_ctx", "norm_w", "ada_w", "ada_b", "w_in", "gla_gate_w2", "gla_gate_b", "gla_norm_w",
        "gdn_conv_w", "gdn_a_log", "gdn_dt_bias", "gdn_norm_w", "mla_q_norm_w", "mla_q_up", "mla_kv_norm_w",
        "mla_kv_up", "mla_qn_nope", "mla_qn_rope", "mla_kn_nope", "mla_kn_rope", "w_branch", "w_out"]


def kernel(**inputs):
    import numpy as _np
    import concourse.bacc as _bacc
    from concourse import mybir as _mybir
    from concourse.bass_utils import run_bass_kernel_spmd as _run

    nc = _bacc.Bacc("TRN2", target_bir_lowering=False, num_devices=1)
    arrays, args = {}, []
    for name in _INS:
        a = _np.ascontiguousarray(inputs[name])
        arrays[f"in_{name}_dram"] = a
        args.append(nc.dram_tensor(f"in_{name}_dram", a.shape, _mybir.dt.from_np(a.dtype), kind="ExternalInput").ap())
    a = constants()
    arrays["shape_constants"] = a
    args.append(nc.dram_tensor("shape_constants", a.shape, _mybir.dt.from_np(a.dtype), kind="ExternalInput").ap())
    out = nc.dram_tensor("out_dram", (1, LX, D), F32, kind="ExternalOutput").ap()
    hybrid_block(nc, *args, out)
    r = _run(nc, [arrays], core_ids=[0])
    return r.results[0]["out_dram"]
```

```python
import math
from contextlib import ExitStack

import numpy as np

import concourse.bass as bass
from concourse import mybir

ALU = mybir.AluOpType
ACT = mybir.ActivationFunctionType
F32 = mybir.dt.float32
U32 = mybir.dt.uint32
AX_X = mybir.AxisListType.X

P = 128
D = 1024
KT = D // P
DEPTH = 2
LC = LX = 256
T = LC + LX
TT = T // P
CH = 64
NCH = T // CH
EPS = 1e-6
GRID_W = 64

AH, ADK, ADV = 4, 128, 256
RANK = 16
BH, BDK = 8, 128
CONV = 5
MH, NOPE, ROPE, MDV = 8, 128, 64, 128
QL, KVL = 384, 256
MSCALE = (NOPE + ROPE) ** -0.5

SIZES = (("aq", 512), ("ak", 512), ("av", 1024), ("alr", 32), ("az", 1024),
         ("bq", 1024), ("bk", 1024), ("bv", 1024), ("bab", 32), ("bz", 1024),
         ("cq", QL), ("ckv", KVL), ("ckr", ROPE), ("cz", 1024), ("mg", 3 * D))
COL = {}
_at = 0
for _n, _s in SIZES:
    COL[_n] = _at
    _at += _s
N_IN = _at

NLEV = 6
C_ID, C_CUM, C_REV = 0, 128, 384
C_IDC = 640
C_CUMC = C_IDC + CH
C_LEV = C_CUMC + 2 * CH
C_COS = C_LEV + 2 * NLEV * CH
C_SIN = C_COS + 256
NCONST = C_SIN + 256


def constants():
    c = np.zeros((P, NCONST), np.float32)
    i, j = np.meshgrid(np.arange(P), np.arange(P), indexing="ij")
    same = (i // CH) == (j // CH)
    c[:, C_ID:C_ID + P] = i == j
    c[:, C_CUM:C_CUM + P] = same & (i <= j)
    c[:, C_CUM + P:C_CUM + 2 * P] = same & (i >= j)
    c[:, C_REV:C_REV + P] = same & (i > j)
    c[:, C_REV + P:C_REV + 2 * P] = same & (i < j)

    def halves(m):
        return np.concatenate([m[:CH, :CH], m[CH:, CH:]])

    c[:, C_IDC:C_IDC + CH] = halves(c[:, C_ID:C_ID + P])
    for r in range(2):
        c[:, C_CUMC + r * CH:C_CUMC + (r + 1) * CH] = halves(c[:, C_CUM + r * P:C_CUM + (r + 1) * P])
    for lev in range(NLEV):
        b = 2 ** lev
        bi, bj = i // b, j // b
        at = C_LEV + 2 * lev * CH
        c[:, at:at + CH] = halves((bi % 2 == 1) & (bj == bi - 1))
        c[:, at + CH:at + 2 * CH] = halves((bi % 2 == 0) & (bj == bi + 1))
    f = ROPE // 4
    inv = np.power(np.float32(10000.0), -np.arange(f, dtype=np.float32) / np.float32(f)).astype(np.float32)
    t = np.arange(LX)
    ang = np.stack([(t // GRID_W).astype(np.float32)[:, None] * inv,
                    (t % GRID_W).astype(np.float32)[:, None] * inv], axis=1)
    cos = np.ones((TT, P, 2, 2, f), np.float32)
    sin = np.zeros((TT, P, 2, 2, f), np.float32)
    q0 = LC // P
    cos[q0:] = np.cos(ang).reshape(TT - q0, P, 2, 1, f)
    sin[q0:, :, :, 0] = -np.sin(ang).reshape(TT - q0, P, 2, f)
    sin[q0:, :, :, 1] = np.sin(ang).reshape(TT - q0, P, 2, f)
    c[:, C_COS:C_COS + 256] = cos.transpose(1, 0, 2, 3, 4).reshape(P, 256)
    c[:, C_SIN:C_SIN + 256] = sin.transpose(1, 0, 2, 3, 4).reshape(P, 256)
    return c


PR_NORM, PR_ADAB, PR_GLA, PR_GDN, PR_QN, PR_KVN, PR_QNN, PR_KNN, PR_C, PR_CC = 0, 8, 32, 34, 35, 38, 40, 41, 42, 50
PR_N = 58


def weave(*seqs, phase=()):
    phase = tuple(phase) + (0.5,) * len(seqs)
    tagged = [((i + phase[n]) / len(s), n, i, it) for n, s in enumerate(seqs) for i, it in enumerate(s)]
    return [t[3] for t in sorted(tagged, key=lambda t: t[:3])]


def chunk_of(r, n):
    if r == 0:
        return n
    return NCH // 2 - 1 - n if n < NCH // 2 else 3 * NCH // 2 - 1 - n


def step_of(r, c):
    return [chunk_of(r, n) for n in range(NCH)].index(c)


def tiles(l):
    return list(range(TT)) if l < DEPTH - 1 else list(range(LC // P, TT))


def low_rank(l):
    return [("mkv", l, tt) for tt in range(TT)] + [("mq", l, tt) for tt in tiles(l)]


FILL = (0.49, 1, 1.42)
PHASE_A = (0.11, 0.97, 0.56, 0.43)
PHASE_B = (0.17, 0.5, 0.07)
PHASE_F = (0.3, 0.23)
SPLIT = ("gate", "z", "dsilu", "dsil2", "dn")
NPIECE = {"gate": 4, "ys": 4, "z": 4, "mod": 4, "dqkv": 4, "gqk": 4, "gv": 4}


def pieces(it):
    return [("pc",) + it + (i,) for i in range(NPIECE[it[0]] - 1)] + [it]


def schedule():
    s = [("xin", tt, h) for tt in range(TT) for h in range(2)]
    s += [("par", l) for l in range(DEPTH)]
    s += [("norm", 0)] + [("mod", 0, j) for j in range(4)]

    def zs(l, br):
        u = [(l, br, tt, h) for h in range(2) for tt in tiles(l)]
        out = []
        for i in range(len(u) + 1):
            p = pieces(("z",) + u[i]) if i < len(u) else []
            out += p[:2] + ([("v", "z") + u[i - 1]] if i else []) + p[2:]
            if i:
                out.append(("z2",) + u[i - 1])
        return out

    def yts(l, br):
        return [("yT", l, br, tt, h) for tt in tiles(l) for h in range(2)]

    def merge(l, br):
        out = []
        for e in range(9):
            if e < 8:
                out += pieces(("gate", l, br, e))
            p = pieces(("ys", l, br, e - 1)) if e else []
            out += p[:2] + ([("v", "gate", l, br, e)] if e < 8 else []) + p[2:]
        return out

    def mods(l, js):
        return [i for j in js for i in pieces(("mod", l, j))]

    def gproj(l, g):
        return ([i for j in range(4) for i in pieces(("gqk", l, g, j))]
                + [i for tt in range(TT) for i in pieces(("gv", l, g, tt))])

    def gla(l):
        out = [("lr", l)]
        for g in range(2):
            out += weave(gproj(l, 0) if g == 0 else [], [("ga", l, g, tt) for tt in range(TT)])
            heads = [("ge", l, g, tt) for tt in range(TT)]
            for h in (2 * g, 2 * g + 1):
                heads += [("gb", l, h, r) for r in range(2)]
                heads += [("gatt", l, h, r) for r in range(2)]
                heads += [("gw", l, h, 0, 0), ("gw", l, h, 1, 0), ("gw", l, h, 0, 1), ("gw", l, h, 1, 1)]
                heads += [("go", l, h, tt) for tt in tiles(l) if tt < 2]
                heads += [("gw", l, h, 0, 2), ("gw", l, h, 1, 2), ("gw", l, h, 0, 3), ("gw", l, h, 1, 3)]
                heads += [("go", l, h, tt) for tt in tiles(l) if tt >= 2]
            out += weave(heads, gproj(l, 1) if g == 0 else mods(l, (4, 5)))
        return out

    def dproj(l, g):
        out = []
        for j in range(8):
            after = [("v", "dsilu", l, g, j - 2), ("dsil2", l, g, j - 2), ("v", "dsil2", l, g, j - 2)] if j >= 2 else []
            if 2 <= j < 6:
                after += [("dnq", l, g, j - 2), ("dn", l, g, j - 2), ("v", "dn", l, g, j - 2)]
            out += weave(pieces(("dqkv", l, g, j)) if j < 6 else [],
                         [("cv", l, g, j - 1, tap) for tap in range(CONV)] if 1 <= j < 7 else [], after)
            if 1 <= j < 7:
                out.append(("dsilu", l, g, j - 1))
        return out

    def head(l, g, tt):
        return [("d1", l, g, tt), ("d2", l, g, tt), ("d3", l, g, tt)]

    def invert(l, g, tt):
        out = []
        for lev in range(NLEV):
            out += [("dx", l, g, tt, lev), ("dy", l, g, tt, lev)]
        return out + [("du", l, g, tt)]

    def scan(l, g, a, b):
        out = []
        for n in range(a, b):
            out += [("sv", l, g, n), ("so", l, g, n)]
        return out

    def gdn(l, fill):
        first = dproj(l, 0)
        first = [("ab", l)] + first[:10] + [("dg", l)] + first[10:]
        first += weave(head(l, 0, 0) + invert(l, 0, 0), head(l, 0, 1) + invert(l, 0, 1))
        parts = []
        for g in range(4):
            parts.append((FILL[0] if g < 3 else FILL[1],
                          weave(head(l, g, 2), head(l, g, 3))
                          + weave(scan(l, g, 0, 4), invert(l, g, 2), invert(l, g, 3), dproj(l, g + 1) if g < 3 else [],
                                  phase=PHASE_A)))
            parts.append((1 if g < 3 else FILL[2],
                          weave(scan(l, g, 4, 8), *([head(l, g + 1, t) + invert(l, g + 1, t) for t in range(2)] if g < 3 else []),
                                phase=PHASE_B)))
        total, rest, done, at = sum(w for w, _ in parts), [], 0, 0
        for w, part in parts:
            done += w
            upto = round(len(fill) * done / total)
            rest += weave(part, fill[at:upto], phase=PHASE_F)
            at = upto
        return first, rest

    def up(l, g):
        out = []
        for tt in range(TT):
            out.append(("muk", l, g, tt))
            if tt in tiles(l):
                out.append(("muq", l, g, tt))
        for tt in range(TT):
            out.append(("mkT", l, g, tt))
            if tt in tiles(l):
                out.append(("mqT", l, g, tt))
        return out

    def att(l, g):
        u = [(l, h, tt) for h in (2 * g, 2 * g + 1) for tt in tiles(l)]
        out = []
        for i in range(len(u) + 2):
            if i < len(u):
                out.append(("ms",) + u[i])
            if 1 <= i <= len(u):
                out.append(("mp",) + u[i - 1])
            if i >= 2:
                out.append(("mo",) + u[i - 2])
        return out

    def mla(l):
        first = []
        low = low_rank(l)
        for i in range(len(low) + 1):
            if i < len(low):
                first.append(low[i])
            if i:
                first.append(("mt", l, low[i - 1][2], int(low[i - 1][0] == "mkv")))
        first += up(l, 0)
        rest = att(l, 0)
        for g in range(1, 4):
            rest += up(l, g) + att(l, g)
        return first, rest

    for l in range(DEPTH):
        s += ([("norm", l)] if l else []) + [("nh", l)]
        s += gla(l)
        s += [("rstd", l, 0)]
        first, rest = gdn(l, merge(l, 0) + (mods(l + 1, range(4)) if l + 1 < DEPTH else []))
        s += weave(first, zs(l, 0) + yts(l, 0)) + rest
        s += [("rstd", l, 1)]
        first, rest = mla(l)
        s += weave(first, zs(l, 1) + yts(l, 1))
        s += weave(rest, merge(l, 1))
        s += zs(l, 2) + yts(l, 2) + merge(l, 2)
        s += [("out", l, e) for e in range(8)]
    s += [("xout", tt, h) for tt in tiles(DEPTH - 1) for h in range(2)]
    return s


PHASE = {"lr": 0, "gqk": 0, "gv": 0, "ga": 0, "ge": 0, "gb": 0, "gatt": 0, "gw": 0, "go": 0,
         "ab": 1, "dg": 1, "dqkv": 1, "cv": 1, "dsilu": 1, "dsil2": 1, "dnq": 1, "dn": 1, "d1": 1, "d2": 1, "d3": 1, "dx": 1, "dy": 1,
         "du": 1, "sv": 1, "so": 1,
         "mkv": 2, "mq": 2, "mt": 2, "muk": 2, "muq": 2, "mkT": 2, "mqT": 2, "ms": 2, "mp": 2, "mo": 2}

PROJ = {"xin", "par", "mod", "norm", "z", "yT", "gate", "ys", "out", "xout", "lr", "gqk", "gv", "dqkv",
        "ab", "mkv", "mq", "mt"}
NBANK = {"nh": 0, "cv": 0, "dsilu": 0, "dsil2": 0, "dnq": 0, "z2": 0, "rstd": 0, "du": 2, "so": 3, "gw": 2, "ge": 2, "mkv": 1, "d3": 1}
READERS = {"xin": ("act",), "par": ("act",), "mod": ("dve",), "norm": ("act",), "z": ("act", "dve"),
           "yT": ("dve",), "gate": ("act", "dve"), "ys": ("dve",), "out": ("dve",), "xout": ("act",),
           "lr": ("act",), "gqk": ("act",), "gv": ("act",), "ga": ("act", "dve"), "ge": ("act", "dve"),
           "gb": ("act",), "gatt": ("dve",), "gw": ("dve",), "go": ("act", "dve"),
           "ab": ("dve",), "dg": ("act", "dve"), "dqkv": ("act",), "dn": ("act",), "d1": ("act", "dve"),
           "d2": ("dve",), "d3": ("act",), "dx": ("dve",), "dy": ("dve",), "du": ("act",),
           "sv": ("dve",), "so": ("dve",), "mkv": ("act", "dve"), "mq": ("act", "dve"), "mt": ("dve",),
           "muk": ("act", "dve"), "muq": ("act", "dve"), "mkT": ("act",), "mqT": ("act", "dve"),
           "ms": ("act", "dve"), "mp": ("act",), "mo": ("dve",)}


NWORK = 20540
UNIT = 256
NSLOT_W = 5


def units_of(it):
    if it[0] == "pc":
        return units_of(it[1:-1])
    k, l = it[0], it[1]

    def two(name, *key):
        return [((name, l) + key + (i,), i * UNIT, UNIT) for i in range(2)]

    if k == "mod":
        return two("ada", it[2])
    if k == "lr":
        return [(("alr", l), 0, 32)]
    if k == "gqk":
        return [(("aq" if it[3] < 2 else "ak", l, it[2]), 0, UNIT)]
    if k == "gv":
        return two("av", it[2])
    if k == "z":
        return two("z", it[2], it[4])
    if k in ("gate", "ys"):
        return [((k, l, it[2], it[3] // 2), 0, UNIT)]
    if k == "out":
        return [(("wo", l, it[2] // 2), 0, UNIT)]
    if k == "ab":
        return [(("bab", l), 0, 32)]
    if k == "dqkv":
        return [((("bq", "bk", "bv")[it[3] // 2], l, it[2]), 0, UNIT)]
    if k == "mkv":
        return [(("ckv", l), 0, KVL), (("ckr", l), KVL, ROPE)]
    if k == "mq":
        return [(("cq", l, 0), 0, UNIT), (("cq", l, 1), UNIT, QL - UNIT)]
    if k == "muk":
        return [(("kup", l, it[2]), 0, 512)]
    if k == "muq":
        return [(("qup", l, it[2]), 0, 384)]
    return []


def hybrid_block(nc, x, c, ctx_in, c_ctx, norm_w, ada_w, ada_b, w_in, gla_gate_w2, gla_gate_b, gla_norm_w,
                 gdn_conv_w, gdn_a_log, gdn_dt_bias, gdn_norm_w, mla_q_norm_w, mla_q_up, mla_kv_norm_w,
                 mla_kv_up, mla_qn_nope, mla_qn_rope, mla_kn_nope, mla_kn_rope, w_branch, w_out,
                 consts, out):
    plan = schedule()
    assert len(set(plan)) == len(plan)
    where = {it: i for i, it in enumerate(plan)}
    kinds = {}
    for it in plan:
        kinds.setdefault(it[0], []).append(it)

    banks, before, holder = {}, {}, {}
    NPROJ = 3

    def read_at(b):
        h = holder.get(b)
        if h is None:
            return -1
        return where[("z2",) + h[1:] if h[0] == "z" else ("v",) + h if h[0] in SPLIT else h]

    for now, it in enumerate(plan):
        it = it[1:-1] if it[0] == "pc" else it
        if it in banks or it[0] == "v":
            continue
        ring = range(NPROJ) if it[0] in PROJ else range(NPROJ, 8)
        take = sorted(ring, key=read_at)[:NBANK.get(it[0], 1)]
        assert all(read_at(b) < now for b in take), (it, [holder.get(b) for b in ring])
        banks[it], before[it] = take, [holder[b] for b in take if b in holder]
        for b in take:
            holder[b] = it

    units, width, last_use = [], {}, {}
    for it in plan:
        for u, _, w in units_of(it):
            if u not in last_use:
                units.append(u)
                width[u] = w
            last_use[u] = it
    slot, occupant, replaced, nload, load_of = {}, [None] * NSLOT_W, {}, [0] * NSLOT_W, {}
    first_use = {}
    for it in plan:
        for u, _, _ in units_of(it):
            first_use.setdefault(u, it)
    for u in units:
        i = min(range(NSLOT_W), key=lambda i: -1 if occupant[i] is None else where[last_use[occupant[i]]])
        if occupant[i] is not None:
            assert where[last_use[occupant[i]]] < where[first_use[u]], (u, occupant)
            replaced[u] = occupant[i]
        occupant[i], slot[u] = u, i
        nload[i] += 1
        load_of[u] = nload[i]

    with ExitStack() as stack:
        def sb(name, shape):
            return stack.enter_context(nc.sbuf_tensor(name, shape, F32))

        hT = sb("hT", [P, KT, T])
        ring = sb("ring", [P, NSLOT_W, KT * UNIT])
        MT = sb("MT", [P, KT, T])
        yT = sb("yT", [P, KT, T])
        O = sb("O", [P, TT, D])
        K = sb("K", [P, NCONST])
        PAR = sb("PAR", [P, DEPTH, P])
        CW = sb("CW", [P, DEPTH, CONV * 24])
        MOD = sb("MOD", [P, DEPTH, 24, 2])
        SC = sb("SC", [P, 16])
        SCt = sb("SCt", [P, 2, 16])
        SCW = sb("SCW", [P, 8, 2])
        NW4 = sb("NW4", [P, DEPTH, 2, 4])
        QKW = sb("QKW", [P, DEPTH])
        ONES = sb("ONES", [P, P])
        ALB = sb("ALB", [P, DEPTH, 32])
        RW = sb("RW", [P, DEPTH, 2, ROPE])
        SSQ = sb("SSQ", [P, 2, TT, 8])
        EPSC = sb("EPSC", [P, 1])
        E1 = sb("E1", [P, 2, 512])
        SQ = sb("SQ", [P, 2, 512])
        RS = sb("RS", [P, 512])
        WORK = sb("WORK", [P, NWORK])
        xs = nc.dram_tensor("xs", (DEPTH, P, KT, T), F32, kind="Internal").ap()

        top = {}

        def area(phase, n):
            at = top.get(phase, 0)
            top[phase] = at + n
            assert top[phase] <= NWORK, (phase, top[phase])
            return WORK[:, at:at + n]

        W2A = area(0, 1024).rearrange("p (r n) -> p r n", r=2)
        LRT = area(0, 512)
        QK = area(0, 4096).rearrange("p (g j n) -> p g j n", g=2, j=4)
        V = area(0, 4096).rearrange("p (g t n) -> p g t n", g=2, t=4)
        LA = area(0, 2048).rearrange("p (t n) -> p t n", t=4)
        LT1 = area(0, 512)
        EB = area(0, 512)
        EI = area(0, 512)
        AQ = area(0, 1024).rearrange("p (r n) -> p r n", r=2)
        AKI = area(0, 1024).rearrange("p (r n) -> p r n", r=2)
        AKE = area(0, 2048).rearrange("p (t n) -> p t n", t=4)
        AER = EB
        HS = area(0, 2048).rearrange("p (r s n) -> p r s n", r=2, s=4)
        ATT = area(0, 1024).rearrange("p (r n) -> p r n", r=2)
        ADEC = area(0, 16).rearrange("p (r n) -> p r n", r=2)
        NSLOT = 4
        bATT = area(1, NSLOT * 256).rearrange("p (s n) -> p s n", s=NSLOT)
        bQD = area(1, NSLOT * 512).rearrange("p (s n) -> p s n", s=NSLOT)
        bKT = area(1, NSLOT * 256).rearrange("p (s n) -> p s n", s=NSLOT)
        bWT = area(1, NSLOT * 512).rearrange("p (s n) -> p s n", s=NSLOT)
        bU = area(1, NSLOT * 512).rearrange("p (s n) -> p s n", s=NSLOT)
        bD = area(1, NSLOT * 8).rearrange("p (s n) -> p s n", s=NSLOT)
        bLF = area(1, 1024).rearrange("p (s n) -> p s n", s=2)
        bPF = area(1, 1024).rearrange("p (s n) -> p s n", s=2)
        bTF = area(1, 1024).rearrange("p (s n) -> p s n", s=2)
        bXX = area(1, 1024).rearrange("p (s n) -> p s n", s=2)
        bP = area(1, 512).rearrange("p (s n) -> p s n", s=2)
        bV2 = area(1, 512).rearrange("p (s n) -> p s n", s=2)
        bDEC = bXX
        KQV = area(1, 3072).rearrange("p (j n) -> p j n", j=6)
        PAD = area(1, 1040).rearrange("p (s n) -> p s n", s=4)
        CA = area(1, 1024).rearrange("p (s n) -> p s n", s=2)
        CE = area(1, 512)
        bS = area(1, 512)
        bVN = area(1, 256)
        bVE = area(1, 256)
        GG = area(1, 64).rearrange("p (t n) -> p t n", t=4)
        BETA = area(1, 64).rearrange("p (t n) -> p t n", t=4)
        GTMP = area(1, 64).rearrange("p (t n) -> p t n", t=4)
        GTM2 = area(1, 64).rearrange("p (t n) -> p t n", t=4)
        GC = area(1, 64).rearrange("p (t n) -> p t n", t=4)
        EGC = area(1, 64).rearrange("p (t n) -> p t n", t=4)
        ERV = area(1, 64).rearrange("p (t n) -> p t n", t=4)
        EAL = area(1, 16)
        RT = area(2, 4 * TT * ROPE).rearrange("p (q n) -> p q n", q=4)
        MQL = area(2, 3 * 512).rearrange("p (k n) -> p k n", k=3)
        MKL = area(2, 2 * 512).rearrange("p (k n) -> p k n", k=2)
        KRT = area(2, 512)
        MT1 = area(2, 768).rearrange("p (s n) -> p s n", s=2)
        MT2 = area(2, 512)
        MT3 = area(2, 512)
        ROT = area(2, 256)
        mS = area(2, 16)
        QN = area(2, 512 * 4).rearrange("p (t n) -> p t n", t=4)
        KN = area(2, 256 * 4).rearrange("p (t n) -> p t n", t=4)
        MV = area(2, 2048).rearrange("p (g t n) -> p g t n", g=2, t=4)
        QNT = area(2, 1024).rearrange("p (h n) -> p h n", h=2)
        QRT = area(2, 512)
        KNT = area(2, 1024).rearrange("p (h n) -> p h n", h=2)
        PM = area(2, 1024).rearrange("p (s n) -> p s n", s=2)
        PT = area(2, 1024).rearrange("p (s n) -> p s n", s=2)
        MST = area(2, 24).rearrange("p (s n) -> p s n", s=4)

        bank = [stack.enter_context(nc.psum_tensor(f"bank{i}", [P, 512], F32)) for i in range(8)]

        sems, order = {}, {}

        def signal(it, who, mark=""):
            key = (it[0], who, mark)
            if key not in sems:
                sems[key] = stack.enter_context(nc.semaphore("_".join(x for x in key if x)))
            return sems[key]

        def nth(it, who):
            k = it[0]
            if (k, who) not in order:
                mine = [i for i in kinds[k] if takes_part(i, who)]
                order[k, who] = {i: n + 1 for n, i in enumerate(mine)}
            return order[k, who][it]

        def takes_part(it, who):
            if it[0] == "sv" and who == "pe":
                return it[3] > 0
            if it[0] == "dy" and who == "act":
                return it[4] < NLEV - 1
            if who == "pool":
                return it[3] in tiles(it[1])
            return True

        def done(it, who, mark=""):
            assert takes_part(it, who), (it, who)
            return signal(it, who, mark), nth(it, who)

        chain_sem = {w: stack.enter_context(nc.semaphore(f"{w}_chain")) for w in ("dve", "act", "pool")}
        chain_n = {w: 0 for w in chain_sem}

        def link(eng, me, ins):
            chain_n[me] += 1
            ins.then_inc(chain_sem[me], 1)
            eng.wait_ge(chain_sem[me], chain_n[me])

        s_unit = [stack.enter_context(nc.semaphore(f"unit_in{i}")) for i in range(NSLOT_W)]
        s_const = stack.enter_context(nc.semaphore("const_in"))
        s_tok = stack.enter_context(nc.semaphore("tokens_in"))
        s_par = stack.enter_context(nc.semaphore("par_in"))
        s_row = stack.enter_context(nc.semaphore("rows_in"))
        s_wz = stack.enter_context(nc.semaphore("w2_zeroed"))
        s_w2 = stack.enter_context(nc.semaphore("w2_in"))
        s_one = stack.enter_context(nc.semaphore("ones_set"))
        s_spill = stack.enter_context(nc.semaphore("spilled"))
        s_back = stack.enter_context(nc.semaphore("reloaded"))
        s_out = stack.enter_context(nc.semaphore("out_written"))
        s_sq = stack.enter_context(nc.semaphore("norm_squares"))
        s_squ = stack.enter_context(nc.semaphore("norm_summed"))
        s_rt = stack.enter_context(nc.semaphore("rotary_tables"))
        s_scaled = stack.enter_context(nc.semaphore("input_scaled"))
        s_h = stack.enter_context(nc.semaphore("input_normalised"))
        s_zero2 = stack.enter_context(nc.semaphore("blocks_zeroed"))
        s_zero = stack.enter_context(nc.semaphore("zeros_set"))

        def kc(at, n=P):
            return K[:, at:at + n]

        ident = kc(C_ID)

        def cum(r):
            return kc(C_CUM + r * P)

        def rev(r):
            return kc(C_REV + r * P)

        def blk(buf, s, c2):
            return buf[c2 * CH:(c2 + 1) * CH, s, :].rearrange("p (u c n) -> p u c n", u=4, c=2)[:, :, c2, :]

        def cmp4(ap):
            return ap.rearrange("p (u n) -> p u n", u=4)

        def bc(ap, axis, shape):
            return ap.unsqueeze(axis).broadcast_to(shape)

        def rh(ap, r=2):
            return ap.rearrange("p (r h n) -> p r h n", r=r, h=2)

        def prev_kind(it, back=1):
            i = nth(it, "order") - 1 - back
            return kinds[it[0]][i] if i >= 0 else None

        phase_items = {}
        for it in plan:
            if it[0] in PHASE:
                phase_items.setdefault((it[1], PHASE[it[0]]), []).append(it)
        phase_last = {}
        for key, its in phase_items.items():
            d = {}
            for it in its:
                d[it[0]] = it
            phase_last[key] = list(d.values())

        parts = {"pe": set(), "act": set(), "dve": set(), "pool": set()}
        NOACT = {"nh", "cv", "pc", "mt", "mod", "out", "yT", "dx", "gatt", "gw", "sv", "so", "mo", "d2", "ab"}
        NODVE = {"norm", "dqkv", "pc", "dnq", "xin", "gqk", "gv", "lr", "du", "mp", "xout", "mkT"}
        POOLK = {"d1"}
        for k in kinds:
            if k == "v":
                continue
            if k not in ("nh", "cv", "dsilu", "dsil2", "dnq", "z2", "rstd"):
                parts["pe"].add(k)
            if k not in NOACT:
                parts["act"].add(k)
            if k not in NODVE:
                parts["dve"].add(k)
            if k in POOLK:
                parts["pool"].add(k)

        def fence(eng, me, it, entered):
            key = (it[1], PHASE[it[0]])
            if key in entered:
                return
            entered.add(key)
            n = key[0] * 3 + key[1]
            if n == 0:
                return
            for lit in phase_last[(n - 1) // 3, (n - 1) % 3]:
                for who in ("pe", "act", "dve", "pool"):
                    if who != me and lit[0] in parts[who] and takes_part(lit, who):
                        eng.wait_ge(*done(lit, who))
                if me in ("act", "dve", "pool") and lit[0] in parts[me] and takes_part(lit, me):
                    eng.wait_ge(*done(lit, me))

        def psum(it, i=0):
            return bank[banks[it][i]]

        def claim(pe, it):
            for b in before[it]:
                if b[0] == "z":
                    pe.wait_ge(*done(("z2",) + b[1:], "dve"))
                else:
                    for who in READERS[b[0]]:
                        pe.wait_ge(*done(b, who))

        def rows_of(u):
            return {"kup": KVL // P, "qup": QL // P}.get(u[0], KT)

        def weights(it, i=0):
            u = units_of(it)[i][0]
            n = rows_of(u)
            return ring[:, slot[u], 0:n * width[u]].rearrange("p (k n) -> p k n", k=n)

        def units_here(pe, it):
            for u, _, _ in units_of(it):
                pe.wait_ge(s_unit[slot[u]], 16 * load_of[u])

        def unit_source(u):
            kind, l = u[0], u[1]
            w = w_in[l]
            at = {"ada": lambda: (ada_w[l], u[2] * 512 + u[3] * UNIT),
                  "alr": lambda: (w, COL["alr"]),
                  "aq": lambda: (w, COL["aq"] + u[2] * UNIT),
                  "ak": lambda: (w, COL["ak"] + u[2] * UNIT),
                  "av": lambda: (w, COL["av"] + u[2] * 512 + u[3] * UNIT),
                  "z": lambda: (w, COL["abc"[u[2]] + "z"] + u[3] * 512 + u[4] * UNIT),
                  "gate": lambda: (w, COL["mg"] + u[2] * D + u[3] * UNIT),
                  "ys": lambda: (w_branch[l, u[2]], u[3] * UNIT),
                  "wo": lambda: (w_out[l], u[2] * UNIT),
                  "bab": lambda: (w, COL["bab"]),
                  "bq": lambda: (w, COL["bq"] + u[2] * UNIT),
                  "bk": lambda: (w, COL["bk"] + u[2] * UNIT),
                  "bv": lambda: (w, COL["bv"] + u[2] * UNIT),
                  "ckv": lambda: (w, COL["ckv"]),
                  "ckr": lambda: (w, COL["ckr"]),
                  "cq": lambda: (w, COL["cq"] + u[2] * UNIT),
                  "qup": lambda: (mla_q_up[l], u[2] * 384),
                  "kup": lambda: (mla_kv_up[l], u[2] * 512)}[kind]
            src, c0 = at()
            return src[:, c0:c0 + width[u]].rearrange("(k p) n -> p k n", p=P)

        E1T = SQ

        def dpar(it):
            return it[3] % 2

        def slot_of(it):
            return (it[2] * TT + it[3]) % NSLOT

        def slot_free(eng, me, it):
            l, g, tt = it[1], it[2], it[3]
            n = g * TT + tt - NSLOT
            if n >= 0:
                pg, pt = n // TT, n % TT
                eng.wait_ge(*done(("so", l, pg, 3 if pt < 2 else 7), "pe"))
                eng.wait_ge(*done(("so", l, pg, 3 if pt < 2 else 7), "dve"))

        def seg(ap2d, s):
            return ap2d[:, s * LC:(s + 1) * LC]

        bSQ = RS

        def ms_par(it):
            return nth(it, "act") % 2

        dq_index = {i: n for n, i in enumerate(kinds["dqkv"])}
        mu = [i for i in plan if i[0] in ("muk", "muq")]
        mu_index = {i: n for n, i in enumerate(mu)}

        zg = [i for i in plan if i[0] in ("z", "gate")]
        zg_index = {i: n for n, i in enumerate(zg)}

        def plan_prev(it, ks):
            i = where[it] - 1
            while i >= 0:
                if plan[i][0] in ks:
                    return plan[i]
                i -= 1
            return None

        def tile_before(it, n):
            at = (it[1] * 4 + it[2]) * TT + it[3] - n
            return ("d1", at // (4 * TT), at // TT % 4, at % TT) if at >= 0 else None

        def rope(dve, dst, src, q, tt, nh):
            cwt = RT[:, 2 * q, tt * ROPE:(tt + 1) * ROPE]
            swt = RT[:, 2 * q + 1, tt * ROPE:(tt + 1) * ROPE]
            for i in range(nh):
                sv = src[:, i * ROPE:(i + 1) * ROPE]
                link(dve, "dve", nc.vector.tensor_tensor(dst[:, i * ROPE:(i + 1) * ROPE], sv, cwt, ALU.mult))
                for hf in range(2):
                    s4 = sv.rearrange("p (a h f) -> p a h f", a=2, h=2)[:, :, 1 - hf, :]
                    w4 = swt.rearrange("p (a h f) -> p a h f", a=2, h=2)[:, :, hf, :]
                    d4 = ROT[:, i * ROPE:(i + 1) * ROPE].rearrange("p (a h f) -> p a h f", a=2, h=2)[:, :, hf, :]
                    ins = nc.vector.tensor_tensor(d4, s4, w4, ALU.mult)
                link(dve, "dve", ins)
                ins = nc.vector.tensor_tensor(dst[:, i * ROPE:(i + 1) * ROPE], dst[:, i * ROPE:(i + 1) * ROPE],
                                              ROT[:, i * ROPE:(i + 1) * ROPE], ALU.add)
            return ins
        block = stack.enter_context(nc.Block())

        @block.sync
        def _(sp):
            sp.dma_start(K[:, :], consts).then_inc(s_const, 16)
            sp.dma_start(O[:, 0:2, :], ctx_in[0].rearrange("(t p) d -> p t d", p=P)).then_inc(s_tok, 16)
            sp.dma_start(O[:, 2:4, :], x[0].rearrange("(t p) d -> p t d", p=P)).then_inc(s_tok, 16)
            for l in range(DEPTH):
                st = MT[:, l, 0:P]
                for row, src in ((PR_NORM, norm_w[l]), (PR_ADAB, ada_b[l]), (PR_GLA, gla_norm_w[l]),
                                 (PR_GDN, gdn_norm_w[l]), (PR_QN, mla_q_norm_w[l]), (PR_KVN, mla_kv_norm_w[l]),
                                 (PR_QNN, mla_qn_nope[l]), (PR_KNN, mla_kn_nope[l]), (PR_C, c[0]), (PR_CC, c_ctx)):
                    n = src.shape[0] // P
                    sp.dma_start(MT[row:row + n, l, 0:P], src.rearrange("(r c) -> r c", c=P)).then_inc(s_par, 16)
                sp.dma_start(MT[0:CONV * 24, 2 + l, 0:P], gdn_conv_w[l].rearrange("j (r c) -> (j r) c", c=P)).then_inc(s_par, 16)
                sp.dma_start(ALB[:, l, 0:16], gdn_a_log[l].rearrange("r h -> (r h)").partition_broadcast(P)).then_inc(s_row, 16)
                sp.dma_start(ALB[:, l, 16:32], gdn_dt_bias[l].rearrange("r h -> (r h)").partition_broadcast(P)).then_inc(s_row, 16)
                sp.dma_start(RW[:, l, 0, :], mla_qn_rope[l].partition_broadcast(P)).then_inc(s_row, 16)
                sp.dma_start(RW[:, l, 1, :], mla_kn_rope[l].partition_broadcast(P)).then_inc(s_row, 16)
            for u in units:
                if u in replaced:
                    sp.wait_ge(*done(last_use[replaced[u]], "pe"))
                n = rows_of(u)
                sp.dma_start(ring[:, slot[u], 0:n * width[u]].rearrange("p (k n) -> p k n", k=n),
                             unit_source(u)).then_inc(s_unit[slot[u]], 16)

        @block.gpsimd
        def _(pool):
            entered = set()
            pool.memset(ONES[:, :], 1.0).then_inc(s_one, 1)
            pool.memset(EPSC[:, :], EPS).then_inc(s_one, 1)
            for it in plan:
                k = it[0]
                if k in PHASE and (k in POOLK or k in ("lr", "dqkv")):
                    fence(pool, "pool", it, entered)
                if k == "lr":
                    l = it[1]
                    pool.memset(W2A[0:2 * RANK + 1, :, :], 0.0).then_inc(s_wz, 1)
                    pool.wait_ge(s_wz, l + 1)
                    for r in range(2):
                        pool.dma_start(W2A[r * RANK:(r + 1) * RANK, r, :], gla_gate_w2[l, r]).then_inc(s_w2, 16)
                    pool.dma_start(W2A[2 * RANK:2 * RANK + 1, :, :], gla_gate_b[l:l + 1]).then_inc(s_w2, 16)
                    pool.memset(LRT[2 * RANK:2 * RANK + 1, :], 1.0).then_inc(s_zero, 1)
                    pool.wait_ge(s_zero, 3 * l + 1)
                    pool.memset(ATT[:, :, :], 0.0).then_inc(s_zero, 1)
                elif k == "dqkv" and it[2] == 0 and it[3] == 0:
                    pool.memset(PAD[:, :, :], 0.0).then_inc(s_zero, 1)
                    for buf in (bLF, bPF, bTF):
                        pool.memset(buf[:, :, :], 0.0).then_inc(s_zero2, 1)
                elif k == "d1":
                    _, l, g, tt = it
                    sl = slot_of(it)
                    if tt in tiles(l):
                        pool.wait_ge(*done(it, "act", "egr"))
                        pool.wait_ge(*done(("dn", l, g, 1), "dve"))
                        slot_free(pool, "pool", it)
                        for r in range(2):
                            ins = pool.tensor_tensor(
                                bQD[:, sl, r * 256:r * 256 + 256].rearrange("p (h n) -> p h n", h=2),
                                KQV[:, 0:2, tt * P:tt * P + P],
                                E1T[:, dpar(it), r * 256:r * 256 + 256].rearrange("p (h n) -> p h n", h=2),
                                ALU.mult)
                        ins.then_inc(signal(it, "pool"), 1)
                elif k == "norm":
                    l = it[1]
                    last = ("xin", TT - 1, 1) if l == 0 else ("out", l - 1, 7)
                    pool.wait_ge(*done(last, "act" if l == 0 else "dve"))
                    pool.dma_start(xs[l], yT[:, :, :]).then_inc(s_spill, 16)
                elif k == "out" and it[2] == 0:
                    l = it[1]
                    pool.wait_ge(s_spill, 16 * (l + 1))
                    pool.wait_ge(*done(("ys", l, 2, 7), "pe"))
                    pool.dma_start(yT[:, :, :], xs[l]).then_inc(s_back, 16)
            for tt in tiles(DEPTH - 1):
                pool.wait_ge(*done(("xout", tt, 1), "act"))
                r0 = tt * P - LC
                pool.dma_start(out[0, r0:r0 + P, :], O[:, tt, :]).then_inc(s_out, 16)
            pool.wait_ge(s_out, 16 * len(tiles(DEPTH - 1)))

        @block.tensor
        def _(pe):
            entered = set()

            def mm(o, a, b, start=True, stop=True):
                return nc.tensor.matmul(o, a, b, start=start, stop=stop, skip_group_check=True)

            def tr(o, a):
                return nc.tensor.transpose(o, a, ident)

            pe.wait_ge(s_const, 16)
            pe.wait_ge(s_one, 2)
            for it in plan:
                piece, last_piece = 0, 0
                if it[0] == "pc":
                    piece = it[-1]
                    it = it[1:-1]
                    last_piece = NPIECE[it[0]] - 1
                elif it[0] in NPIECE and ("pc",) + it + (0,) in where:
                    piece = last_piece = NPIECE[it[0]] - 1
                k, l = it[0], it[1]
                if k not in parts["pe"] or not takes_part(it, "pe"):
                    continue
                if piece == 0:
                    claim(pe, it)
                ps = psum(it)
                q0 = 0 if (len(it) and k not in ("xin", "xout", "par") and l < DEPTH - 1) else LC
                if k == "xin":
                    _, tt, h = it
                    pe.wait_ge(s_tok, 32)
                    for j in range(4):
                        ins = tr(ps[:, j * P:(j + 1) * P], O[:, tt, (4 * h + j) * P:(4 * h + j + 1) * P])
                elif k == "xout":
                    _, tt, h = it
                    pe.wait_ge(*done(("out", DEPTH - 1, 7), "dve"))
                    for j in range(4):
                        ins = tr(ps[:, j * P:(j + 1) * P], yT[:, 4 * h + j, tt * P:(tt + 1) * P])
                elif k == "par":
                    pe.wait_ge(s_par, 16 * 22)
                    tr_in = MT[0:PR_N, l, 0:P]
                    nc.tensor.transpose(ps[:, 0:PR_N], tr_in, K[0:PR_N, C_ID:C_ID + PR_N])
                    n = CONV * 24
                    ins = nc.tensor.transpose(ps[:, P:P + n], MT[0:n, 2 + l, 0:P], K[0:n, C_ID:C_ID + n])
                elif k == "mod":
                    units_here(pe, it)
                    pe.wait_ge(*done(("par", 0), "dve"))
                    for t in range(4) if last_piece == 0 else (piece,):
                        w = weights(it, t // 2)
                        for kk in range(KT):
                            ins = mm(ps[:, 2 * t:2 * t + 2], w[:, kk, (t % 2) * P:(t % 2 + 1) * P], SC[:, kk:kk + 9:8],
                                     kk == 0, kk == KT - 1)
                elif k == "norm":
                    for kk in range(KT):
                        pe.wait_ge(s_sq, l * KT + kk + 1)
                        ins = mm(ps[:, :], ONES[:, :], SQ[:, kk % 2, :], kk == 0, kk == KT - 1)
                        if kk < KT - 1:
                            ins.then_inc(s_squ, 1)
                elif k == "lr":
                    units_here(pe, it)
                    w = weights(it)
                    for kk in range(KT):
                        if kk < KT - 1:
                            pe.wait_ge(s_h, l * (KT - 1) + kk + 1)
                        else:
                            pe.wait_ge(*done(("nh", l), "dve"))
                        ins = mm(ps[0:2 * RANK, :], w[:, kk, :], hT[:, kk, :],
                                 kk == 0, kk == KT - 1)
                elif k in ("gqk", "dqkv", "gate", "ys", "out"):
                    units_here(pe, it)
                    src, j = hT, it[-1]
                    if k == "ys":
                        src = yT
                        for tt in tiles(l):
                            pe.wait_ge(*done(("yT", l, it[2], tt, 1), "dve"))
                    elif k == "out":
                        src = MT
                        pe.wait_ge(*done(("ys", l, 2, 7), "dve"))
                    a0 = 0 if (k in ("gqk", "dqkv") and j >= 2) else q0
                    w = weights(it)[:, :, (j % 2) * P:(j % 2 + 1) * P]
                    n = KT // (last_piece + 1)
                    for kk in range(piece * n, piece * n + n):
                        ins = mm(ps[:, a0:T], w[:, kk, :], src[:, kk, a0:T], kk == 0, kk == KT - 1)
                elif k in ("gv", "z", "mkv", "mq"):
                    units_here(pe, it)
                    tt = it[3] if k in ("gv", "z") else it[2]
                    todo = [(i, kk) for i in range(len(units_of(it))) for kk in range(KT)]
                    n = len(todo) // (last_piece + 1)
                    for i, kk in todo[piece * n:piece * n + n]:
                            c0, wd = units_of(it)[i][1:]
                            ins = mm(ps[:, c0:c0 + wd], hT[:, kk, tt * P:(tt + 1) * P], weights(it, i)[:, kk, :],
                                     kk == 0, kk == KT - 1)
                elif k == "ab":
                    units_here(pe, it)
                    for tt in range(TT):
                        for kk in range(KT):
                            ins = mm(ps[:, tt * 32:tt * 32 + 32], hT[:, kk, tt * P:(tt + 1) * P], weights(it)[:, kk, :],
                                     kk == 0, kk == KT - 1)
                elif k == "yT":
                    _, l, br, tt, h = it
                    pe.wait_ge(*done(("z2", l, br, tt, h), "dve"))
                    for j in range(4):
                        ins = tr(ps[:, j * P:(j + 1) * P], O[:, tt, (4 * h + j) * P:(4 * h + j + 1) * P])
                elif k == "ga":
                    _, l, g, tt = it
                    pe.wait_ge(*done(("lr", l), "act"))
                    pe.wait_ge(s_zero, 3 * l + 1)
                    pe.wait_ge(s_w2, 48 * (l + 1))
                    for r in range(2):
                        ins = mm(ps[:, r * 256:r * 256 + 256], LRT[0:2 * RANK + 1, tt * P:(tt + 1) * P],
                                 W2A[0:2 * RANK + 1, r, g * 256:g * 256 + 256])
                elif k == "gb":
                    _, l, h, r = it
                    g, hh = h // 2, h % 2
                    for tt in range(TT):
                        pe.wait_ge(*done(("ga", l, g, tt), "dve"))
                        ins = mm(ps[:, tt * P:(tt + 1) * P], LA[:, tt, (2 * r + hh) * P:(2 * r + hh + 1) * P], cum(r))
                elif k == "ge":
                    _, l, g, tt = it
                    pe.wait_ge(*done(("ga", l, g, tt), "dve"))
                    for r in range(2):
                        mm(ps[:, r * 256:r * 256 + 256], rev(r), LA[:, tt, r * 256:r * 256 + 256])
                    for hh in range(2):
                        pe.wait_ge(*done(("gqk", l, g, 2 + hh), "act"))
                        ins = tr(psum(it, 1)[:, hh * P:(hh + 1) * P], QK[:, g, 2 + hh, tt * P:(tt + 1) * P])
                elif k == "gatt":
                    _, l, h, r = it
                    pe.wait_ge(*done(("gb", l, h, r), "dve"))
                    for tt in tiles(l):
                        ins = mm(ps[:, tt * P:(tt + 1) * P], AKI[:, r, tt * P:(tt + 1) * P],
                                 AQ[:, r, tt * P:(tt + 1) * P])
                elif k == "gw":
                    _, l, h, r, m = it
                    g, hh = h // 2, h % 2
                    for i in range(2):
                        n = 2 * m + i
                        if n == NCH - 1:
                            continue
                        cc = chunk_of(r, n)
                        tt, p0 = cc // 2, (cc % 2) * CH
                        pe.wait_ge(*done(("ge", l, h // 2, tt), "dve"))
                        pe.wait_ge(*done(("gv", l, h // 2, tt), "act"))
                        ins = mm(psum(it, i)[:, 0:256], AKE[p0:p0 + CH, tt, (2 * r + hh) * P:(2 * r + hh + 1) * P],
                                 V[p0:p0 + CH, g, tt, hh * ADV:(hh + 1) * ADV])
                elif k == "go":
                    _, l, h, tt = it
                    g, hh = h // 2, h % 2
                    for r in range(2):
                        pe.wait_ge(*done(("gatt", l, h, r), "dve"))
                        pe.wait_ge(*done(("gw", l, h, r, 1 if tt < 2 else 3), "dve"))
                        mm(ps[:, 0:ADV], ATT[:, r, tt * P:(tt + 1) * P], V[:, g, tt, hh * ADV:(hh + 1) * ADV],
                           r == 0, False)
                    todo = [(r, cc) for r in range(2) for cc in (2 * tt, 2 * tt + 1) if step_of(r, cc) > 0]
                    for i, (r, cc) in enumerate(todo):
                        p0 = (cc % 2) * CH
                        ins = mm(ps[p0:p0 + CH, 0:ADV], AQ[:, r, cc * CH:(cc + 1) * CH],
                                 HS[:, r, step_of(r, cc) % 4, :], False, i >= len(todo) - 2)
                elif k == "dg":
                    pe.wait_ge(*done(it, "dve", "gg"))
                    for tt in range(TT):
                        for r in range(2):
                            a = GG[:, tt, r * BH:(r + 1) * BH]
                            mm(ps[:, tt * 16 + r * BH:tt * 16 + (r + 1) * BH], cum(r), a)
                            ins = mm(ps[:, 64 + tt * 16 + r * BH:64 + tt * 16 + (r + 1) * BH], rev(r), a)
                elif k == "dn":
                    pe.wait_ge(*done(("dnq",) + it[1:], "act"))
                    a0 = q0 if it[3] < 2 else 0
                    ins = mm(ps[:, a0:T], ONES[:, :], bSQ[:, a0:T])
                elif k == "d1":
                    _, l, g, tt = it
                    pe.wait_ge(*done(("dg", l), "dve"))
                    for r in range(2):
                        for hh in range(2):
                            u = 2 * r + hh
                            ins = mm(ps[:, u * P:(u + 1) * P],
                                     GG[:, tt, r * BH + 2 * g + hh:r * BH + 2 * g + hh + 1].broadcast_to([P, P]), cum(r))
                elif k == "d2":
                    _, l, g, tt = it
                    for j in range(4):
                        if j >= 2 or l < DEPTH - 1 or tt >= 2:
                            pe.wait_ge(*done(("dn", l, g, j), "dve"))
                    for c2 in range(2):
                        rows, t0 = slice(c2 * CH, (c2 + 1) * CH), tt * P + c2 * CH
                        for hh in range(2):
                            kk = KQV[:, 2 + hh, t0:t0 + CH]
                            ins = mm(ps[rows, hh * CH:(hh + 1) * CH], kk, kk)
                            if tt in tiles(l):
                                ins = mm(ps[rows, (2 + hh) * CH:(3 + hh) * CH], kk, KQV[:, hh, t0:t0 + CH])
                elif k == "d3":
                    _, l, g, tt = it
                    pe.wait_ge(*done(("dsil2", l, g, 5), "dve"))
                    for j in range(4):
                        ins = tr(ps[:, j * P:(j + 1) * P], KQV[:, 2 + j, tt * P:(tt + 1) * P])
                elif k == "dx":
                    _, l, g, tt, lev = it
                    s = dpar(it)
                    pe.wait_ge(*done(("dy", l, g, tt, lev - 1) if lev else ("d3", l, g, tt), "dve"))
                    for u in range(4):
                        uc = slice(u * CH, (u + 1) * CH)
                        ins = mm(ps[:, uc], bLF[:, s, u * P:(u + 1) * P], bXX[:, s, uc])
                elif k == "dy":
                    _, l, g, tt, lev = it
                    s = dpar(it)
                    if lev < NLEV - 1:
                        pe.wait_ge(*done(("dx", l, g, tt, lev), "dve", "compact"))
                        pe.wait_ge(*done(("dy", l, g, tt, lev - 1) if lev else ("d3", l, g, tt), "act"))
                        for u in range(4):
                            uc = slice(u * CH, (u + 1) * CH)
                            mm(ps[:, uc], bTF[:, s, u * P:(u + 1) * P], bP[:, s, uc])
                    pe.wait_ge(*done(("dx", l, g, tt, lev), "dve"))
                    for u in range(4):
                        ut = slice(256 + u * CH, 256 + (u + 1) * CH)
                        ins = mm(ps[:, ut], bPF[:, s, u * P:(u + 1) * P], bXX[:, s, ut])
                elif k == "du":
                    _, l, g, tt = it
                    s = dpar(it)
                    pe.wait_ge(*done(("dy", l, g, tt, NLEV - 1), "dve"))
                    pe.wait_ge(*done(("d3", l, g, tt), "act"))
                    for u in range(4):
                        hc = slice((u % 2) * P, (u % 2 + 1) * P)
                        c4 = slice(u * P, (u + 1) * P)
                        mm(ps[:, c4], bTF[:, s, c4], bV2[:, s, hc])
                        ins = mm(psum(it, 1)[:, c4], bKT[:, slot_of(it), hc], bPF[:, s, c4])
                elif k == "sv":
                    _, l, g, n = it
                    pe.wait_ge(*done(("so", l, g, n - 1), "dve"))
                    for r in range(2):
                        cc = chunk_of(r, n)
                        tt, p0 = cc // 2, (cc % 2) * CH
                        pe.wait_ge(*done(("du", l, g, tt), "act"))
                        sl = slot_of(("d1", l, g, tt))
                        for hh in range(2):
                            u = 2 * r + hh
                            ins = mm(ps[p0:p0 + CH, hh * P:(hh + 1) * P],
                                     bWT[:, sl, u * P + p0:u * P + p0 + CH], bS[:, u * P:(u + 1) * P])
                elif k == "so":
                    _, l, g, n = it
                    pe.wait_ge(*done(("sv", l, g, n), "dve"))
                    for r in range(2):
                        cc = chunk_of(r, n)
                        tt, p0 = cc // 2, (cc % 2) * CH
                        sl = slot_of(("d1", l, g, tt))
                        if tt in tiles(l):
                            pe.wait_ge(*done(("d1", l, g, tt), "pool"))
                        for hh in range(2):
                            u = 2 * r + hh
                            vn = bVN[p0:p0 + CH, hh * P:(hh + 1) * P]
                            if tt in tiles(l):
                                o = ps[p0:p0 + CH, hh * P:(hh + 1) * P]
                                if n:
                                    mm(o, bQD[:, sl, u * P + p0:u * P + p0 + CH], bS[:, u * P:(u + 1) * P], True, False)
                                ins = mm(o, bATT[p0:p0 + CH, sl, u * CH:(u + 1) * CH], vn, n == 0, True)
                            if n < NCH - 1:
                                ins = mm(psum(it, 1 + r)[:, hh * P:(hh + 1) * P], bKT[p0:p0 + CH, sl, hh * P:(hh + 1) * P],
                                         bVE[p0:p0 + CH, hh * P:(hh + 1) * P])
                elif k == "mt":
                    _, l, tt, kv = it
                    pe.wait_ge(*done(("mkv" if kv else "mq", l, tt), "dve"))
                    for j in range(3):
                        ins = tr(ps[:, j * P:(j + 1) * P], MT1[:, tt % 2, j * P:(j + 1) * P])
                elif k == "muk":
                    _, l, g, tt = it
                    units_here(pe, it)
                    pe.wait_ge(*done(("mt", l, tt, 1), "dve"))
                    w = weights(it)
                    for kk in range(2):
                        ins = mm(ps[:, :], MKL[:, kk, tt * P:(tt + 1) * P], w[:, kk, :], kk == 0, kk == 1)
                elif k == "muq":
                    _, l, g, tt = it
                    units_here(pe, it)
                    pe.wait_ge(*done(("mt", l, tt, 0), "dve"))
                    w = weights(it)
                    for kk in range(3):
                        ins = mm(ps[:, 0:384], MQL[:, kk, tt * P:(tt + 1) * P], w[:, kk, :], kk == 0, kk == 2)
                elif k == "mkT":
                    _, l, g, tt = it
                    pe.wait_ge(*done(("muk", l, g, tt), "dve"))
                    for hh in range(2):
                        ins = tr(ps[:, hh * P:(hh + 1) * P], KN[:, tt, hh * P:(hh + 1) * P])
                elif k == "mqT":
                    _, l, g, tt = it
                    pe.wait_ge(*done(("muq", l, g, tt), "dve"))
                    for j in range(3):
                        ins = tr(ps[:, j * P:(j + 1) * P], QN[:, tt, j * P:(j + 1) * P])
                elif k == "ms":
                    _, l, h, tt = it
                    g, hh = h // 2, h % 2
                    nk = LC if tt < 2 else T
                    pe.wait_ge(*done(("mqT", l, g, tt), "act"))
                    pe.wait_ge(*done(("mqT", l, g, tt), "dve"))
                    pe.wait_ge(*done(("mkT", l, g, nk // P - 1), "act"))
                    mm(ps[:, 0:nk], QNT[:, hh, tt * P:(tt + 1) * P], KNT[:, hh, 0:nk], True, False)
                    ins = mm(ps[:, 0:nk], QRT[hh * 64:hh * 64 + 64, tt * P:(tt + 1) * P],
                             KRT[hh * 64:hh * 64 + 64, 0:nk], False, True)
                elif k == "mp":
                    _, l, h, tt = it
                    nk = LC if tt < 2 else T
                    pe.wait_ge(*done(("ms", l, h, tt), "act"))
                    s = ms_par(it)
                    for j in range(nk // P):
                        ins = tr(ps[:, j * P:(j + 1) * P], PM[:, s, j * P:(j + 1) * P])
                elif k == "mo":
                    _, l, h, tt = it
                    nk = LC if tt < 2 else T
                    pe.wait_ge(*done(("mp", l, h, tt), "act"))
                    s = ms_par(it)
                    n = nk // P
                    for j in range(n):
                        ins = mm(ps[:, 0:P], PT[:, s, j * P:(j + 1) * P],
                                 MV[:, (h // 2) % 2, j, (h % 2) * P:(h % 2 + 1) * P], j == 0, j == n - 1)
                else:
                    raise AssertionError(k)
                if piece == last_piece:
                    ins.then_inc(signal(it, "pe"), 1)

        @block.scalar
        def _(act):
            entered = set()

            def log1p_exp(dst, src):
                link(act, "act", nc.scalar.activation(dst, src, ACT.Abs))
                link(act, "act", nc.scalar.activation(dst, dst, ACT.Exp, scale=-1.0))
                return nc.scalar.activation(dst, dst, ACT.Ln, bias=1.0)

            def rsqrt(dst, src, n):
                link(act, "act", nc.scalar.activation(dst, src, ACT.Ln, bias=EPSC[0:dst.shape[0], :], scale=1.0 / n))
                return nc.scalar.activation(dst, dst, ACT.Exp, scale=-0.5)

            def row_rstd(ps, sums, at):
                for c0, w, i in sums:
                    ins = nc.scalar.activation(MT2[:, c0:c0 + w], ps[:, c0:c0 + w], ACT.Square,
                                               accum_out=mS[:, at + i:at + i + 1])
                link(act, "act", ins)
                n = 0
                for w in sorted({w for _, w, _ in sums}, reverse=True):
                    m = sum(1 for _, v, _ in sums if v == w)
                    ins = nc.scalar.activation(mS[:, at + n:at + n + m], mS[:, at + n:at + n + m], ACT.Ln,
                                               bias=EPSC[:, :], scale=1.0 / w)
                    n += m
                link(act, "act", ins)
                return nc.scalar.activation(mS[:, at:at + n], mS[:, at:at + n], ACT.Exp, scale=-0.5)

            nc.scalar.preload_act_table_set("natural_log_exp_and_others")
            act.wait_ge(s_one, 2)
            for it in plan:
                k, l = it[0], it[1]
                if k not in parts["act"] or not takes_part(it, "act"):
                    continue
                if k in PHASE:
                    fence(act, "act", it, entered)
                ps = psum(it) if banks[it] else None
                if k in parts["pe"] and k not in ("norm", "dg", "dn", "ys"):
                    act.wait_ge(*done(it, "pe"))
                mine = signal(it, "act")
                q0 = 0 if (k not in ("xin", "xout", "par") and l < DEPTH - 1) else LC
                if k == "xin":
                    _, tt, h = it
                    ins = nc.scalar.activation(yT[:, 4 * h:4 * h + 4, tt * P:(tt + 1) * P],
                                               ps[:, :].rearrange("p (j n) -> p j n", j=4), ACT.Copy)
                elif k == "xout":
                    _, tt, h = it
                    ins = nc.scalar.activation(O[:, tt, h * 512:(h + 1) * 512], ps[:, :], ACT.Copy)
                elif k == "par":
                    nc.scalar.activation(CW[:, l, :], ps[:, P:P + CONV * 24], ACT.Copy)
                    link(act, "act", nc.scalar.activation(PAR[:, l, 0:PR_N], ps[:, 0:PR_N], ACT.Copy))
                    ins = nc.scalar.activation(SCt[:, 0, :], PAR[:, l, PR_C:PR_C + 16], ACT.Exp, scale=-1.0) if l == 0 else \
                        nc.scalar.activation(SCt[:, 1, 0:1], EPSC[:, :], ACT.Copy)
                elif k == "norm":
                    if l:
                        act.wait_ge(*done(("out", l - 1, 7), "dve"))
                    else:
                        act.wait_ge(*done(("xin", TT - 1, 1), "act"))
                    for kk in range(KT):
                        n = l * (KT - 1) + kk
                        if kk >= 2:
                            act.wait_ge(s_squ, l * (KT - 1) + kk - 1)
                        elif l:
                            act.wait_ge(*done(("norm", l - 1), "pe"))
                        nc.scalar.activation(SQ[:, kk % 2, :], yT[:, kk, :], ACT.Square).then_inc(s_sq, 1)
                    act.wait_ge(*done(it, "pe"))
                    if l:
                        act.wait_ge(*done(("nh", l - 1), "dve"))
                    ins = rsqrt(RS[:, :], ps[:, :], D)
                elif k == "lr":
                    ins = nc.scalar.activation(LRT[0:2 * RANK, :], ps[0:2 * RANK, :], ACT.Copy)
                elif k == "gqk":
                    _, l, g, j = it
                    a0 = q0 if j < 2 else 0
                    ins = nc.scalar.activation(QK[:, g, j, a0:T], ps[:, a0:T], ACT.Copy)
                elif k == "gv":
                    _, l, g, tt = it
                    ins = nc.scalar.activation(V[:, g, tt, :], ps[:, :], ACT.Copy)
                elif k == "ga":
                    p = prev_kind(it)
                    if p:
                        act.wait_ge(*done(p, "dve"))
                    p = plan_prev(it, ("go",))
                    if p:
                        act.wait_ge(*done(p, "act"))
                    ins = log1p_exp(LT1, ps[:, :])
                elif k == "gb":
                    p = prev_kind(it)
                    if p:
                        act.wait_ge(*done(p, "dve"))
                    act.wait_ge(*done(("ge", l, it[2] // 2, TT - 1), "dve"))
                    nc.scalar.activation(EB, ps[:, :], ACT.Exp, scale=1.0 / 16)
                    ins = nc.scalar.activation(EI, ps[:, :], ACT.Exp, scale=-1.0 / 16)
                elif k == "ge":
                    p = prev_kind(it)
                    if p:
                        act.wait_ge(*done(p, "dve"))
                    if it[2] and it[3] == 0:
                        act.wait_ge(*done(("gb", l, 2 * it[2] - 1, 1), "dve"))
                    ins = nc.scalar.activation(AER, ps[:, :], ACT.Exp, scale=1.0 / 16)
                elif k == "go":
                    _, l, h, tt = it
                    act.wait_ge(*done(plan_prev(it, ("go", "ga")), "act"))
                    if plan_prev(it, ("go", "ga"))[0] == "ga":
                        act.wait_ge(*done(plan_prev(it, ("ga",)), "dve"))
                    ins = nc.scalar.activation(LT1[:, 0:ADV], ps[:, 0:ADV], ACT.Square,
                                               accum_out=SSQ[:, 0, tt, h:h + 1])
                elif k == "rstd":
                    _, l, br = it
                    t0 = tiles(l)[0]
                    nh = AH if br == 0 else BH
                    hd = D // nh
                    if br == 0:
                        act.wait_ge(*done(("go", l, AH - 1, TT - 1), "act"))
                    else:
                        act.wait_ge(*done(("so", l, 3, NCH - 1), "dve"))
                        for tt in tiles(l):
                            for h in range(BH):
                                if h == 0 and tt == t0:
                                    pass
                                link(act, "act", nc.scalar.activation(RS[:, 0:P], O[:, tt, h * P:(h + 1) * P], ACT.Square,
                                                       accum_out=SSQ[:, 1, tt, h:h + 1]))
                    ins = rsqrt(SSQ[:, br, t0:TT, 0:nh], SSQ[:, br, t0:TT, 0:nh], hd)
                elif k in ("z", "gate"):
                    n = zg_index[it]
                    if n >= 2:
                        p = zg[n - 2]
                        act.wait_ge(*done(("z2" if p[0] == "z" else "ys",) + p[1:], "dve"))
                    a0 = q0 if k == "gate" else 0
                    ins = log1p_exp(E1[:, n % 2, a0:512], ps[:, a0:512])
                elif k in ("z2", "ys"):
                    zi = ("z" if k == "z2" else "gate",) + it[1:]
                    act.wait_ge(*done(zi, "dve"))
                    e = E1[:, zg_index[zi] % 2, (q0 if k == "ys" else 0):512]
                    ins = nc.scalar.activation(e, e, ACT.Exp)
                elif k == "dg":
                    act.wait_ge(s_row, 16 * 8)
                    nc.scalar.activation(EAL, ALB[:, l, 0:16], ACT.Exp)
                    act.wait_ge(*done(it, "dve", "adt"))
                    link(act, "act", nc.scalar.activation(GTM2[:, :, :], GTMP[:, :, :], ACT.Abs))
                    nc.scalar.activation(BETA[:, :, :], BETA[:, :, :], ACT.Exp, scale=-1.0)
                    link(act, "act", nc.scalar.activation(GTM2[:, :, :], GTM2[:, :, :], ACT.Exp, scale=-1.0))
                    nc.scalar.activation(GTM2[:, :, :], GTM2[:, :, :], ACT.Ln, bias=1.0).then_inc(signal(it, "act", "sp"), 1)
                    act.wait_ge(*done(it, "pe"))
                    nc.scalar.activation(EGC[:, :, :], ps[:, 0:64].rearrange("p (t n) -> p t n", t=4), ACT.Exp)
                    ins = nc.scalar.activation(ERV[:, :, :], ps[:, 64:128].rearrange("p (t n) -> p t n", t=4), ACT.Exp)
                elif k == "dqkv":
                    act.wait_ge(s_zero, 3 * l + 3)
                    pj = dq_index[it] % 2
                    p = prev_kind(it, 2)
                    if p:
                        act.wait_ge(*done(("cv",) + p[1:] + (CONV - 1,), "dve"))
                    a0 = 1 if (it[3] < 2 and l == DEPTH - 1) else 0
                    ins = nc.scalar.activation(PAD[:, 2 * pj + a0:2 * pj + 2, 2:258],
                                               ps[:, a0 * LC:T].rearrange("p (s n) -> p s n", n=LC), ACT.Copy)
                elif k == "dsilu":
                    act.wait_ge(*done(("cv",) + it[1:] + (CONV - 1,), "dve"))
                    p = prev_kind(it)
                    if p:
                        act.wait_ge(*done(("dsil2",) + p[1:], "dve"))
                    a0 = q0 if it[3] < 2 else 0
                    pj = dq_index[("dqkv",) + it[1:]] % 2
                    ins = log1p_exp(CE[:, a0:T], CA[:, pj, a0:T])
                elif k == "dsil2":
                    act.wait_ge(*done(("dsilu",) + it[1:], "dve"))
                    a0 = q0 if it[3] < 2 else 0
                    pj = dq_index[("dqkv",) + it[1:]] % 2
                    ins = nc.scalar.activation(CE[:, a0:T], CE[:, a0:T], ACT.Exp)
                elif k == "dnq":
                    _, l, g, j = it
                    a0 = q0 if j < 2 else 0
                    act.wait_ge(*done(("dsil2", l, g, j), "dve"))
                    p = prev_kind(it)
                    if p:
                        act.wait_ge(*done(("dn",) + p[1:], "dve"))
                    ins = nc.scalar.activation(bSQ[:, a0:T], KQV[:, j, a0:T], ACT.Square)
                elif k == "dn":
                    _, l, g, j = it
                    a0 = q0 if j < 2 else 0
                    act.wait_ge(*done(it, "pe"))
                    ins = rsqrt(bSQ[:, a0:T], ps[:, a0:T], 1.0)
                elif k == "d1":
                    _, l, g, tt = it
                    s = dpar(it)
                    pit = tile_before(it, 2)
                    if pit:
                        if pit[3] in tiles(pit[1]):
                            act.wait_ge(*done(pit, "pool"))
                        act.wait_ge(*done(pit, "dve"))
                    nc.scalar.activation(E1T[:, s, :], ps[:, :], ACT.Exp).then_inc(signal(it, "act", "egr"), 1)
                    act.wait_ge(*done(it, "dve", "dif"))
                    ins = nc.scalar.activation(bDEC[:, s, 0:256], bDEC[:, s, 0:256], ACT.Exp)
                elif k == "d3":
                    _, l, g, tt = it
                    s = dpar(it)
                    pit = tile_before(it, 2)
                    if pit:
                        act.wait_ge(*done(("du",) + pit[1:], "pe"))
                    slot_free(act, "act", it)
                    nc.scalar.activation(bKT[:, slot_of(it), :], ps[:, 0:256], ACT.Copy)
                    nc.scalar.activation(bV2[:, s, :], ps[:, 256:512], ACT.Copy)
                    act.wait_ge(*done(it, "dve"))
                    for c2 in range(2):
                        ins = nc.scalar.activation(blk(bTF, s, c2), cmp4(bXX[c2 * CH:(c2 + 1) * CH, s, 256:512]), ACT.Copy)
                elif k == "dy":
                    _, l, g, tt, lev = it
                    s = dpar(it)
                    act.wait_ge(*done(it, "dve"))
                    act.wait_ge(*done(("dy", l, g, tt, lev - 1) if lev else ("d3", l, g, tt), "act"))
                    for c2 in range(2):
                        ins = nc.scalar.activation(blk(bTF, s, c2), cmp4(bXX[c2 * CH:(c2 + 1) * CH, s, 256:512]), ACT.Copy)
                elif k == "du":
                    sl = slot_of(it)
                    slot_free(act, "act", it)
                    nc.scalar.activation(bU[:, sl, :], ps[:, :], ACT.Copy)
                    ins = nc.scalar.activation(bWT[:, sl, :], psum(it, 1)[:, :], ACT.Copy)
                elif k in ("mq", "mkv"):
                    p = plan_prev(it, ("mq", "mkv"))
                    if p:
                        act.wait_ge(*done(p, "dve"))
                    w = QL if k == "mq" else KVL
                    sums = [(0, w, 0)] + ([(KVL, ROPE, 1)] if k == "mkv" else [])
                    ins = row_rstd(ps, sums, 0)
                elif k in ("muk", "muq"):
                    _, l, g, tt = it
                    p = plan_prev(it, ("muk", "muq"))
                    if p:
                        act.wait_ge(*done(p, "act"))
                    n = mu_index[it]
                    if n >= 2:
                        act.wait_ge(*done(mu[n - 2], "dve"))
                    if k == "muk":
                        if g >= 2:
                            act.wait_ge(*done(("mo", l, 2 * (g - 2) + 1, TT - 1), "pe"))
                        v4 = ps[:, :].rearrange("p (h w n) -> p h w n", h=2, w=2)
                        nc.scalar.activation(MV[:, g % 2, tt, :].rearrange("p (h n) -> p h n", h=2), v4[:, :, 1, :], ACT.Copy)
                        ins = row_rstd(ps, [(0, NOPE, 0), (256, NOPE, 1)], 4 + 4 * (n % 2))
                    else:
                        ins = row_rstd(ps, [(0, NOPE, 0), (192, NOPE, 1), (NOPE, ROPE, 2), (192 + NOPE, ROPE, 3)],
                                       4 + 4 * (n % 2))
                elif k == "mkT":
                    _, l, g, tt = it
                    if g:
                        act.wait_ge(*done(("ms", l, 2 * g - 1, TT - 1), "pe"))
                    ins = nc.scalar.activation(KNT[:, :, tt * P:(tt + 1) * P],
                                               ps[:, 0:256].rearrange("p (h n) -> p h n", h=2), ACT.Copy)
                elif k == "mqT":
                    _, l, g, tt = it
                    if g:
                        act.wait_ge(*done(("ms", l, 2 * g - 1, TT - 1), "pe"))
                    ins = nc.scalar.activation(QRT[:, tt * P:(tt + 1) * P], ps[:, 256:384], ACT.Copy)
                elif k == "ms":
                    _, l, h, tt = it
                    nk = LC if tt < 2 else T
                    s = ms_par(it)
                    act.wait_ge(*done(it, "dve", "max"))
                    p = prev_kind(it, 2)
                    if p:
                        act.wait_ge(*done(("mp",) + p[1:], "pe"))
                    ins = nc.scalar.activation(PM[:, s, 0:nk], ps[:, 0:nk], ACT.Exp, bias=MST[:, nth(it, "act") % 4, 0:1],
                                               scale=MSCALE, accum_out=MST[:, nth(it, "act") % 4, 1:2])
                elif k == "mp":
                    _, l, h, tt = it
                    nk = LC if tt < 2 else T
                    s = ms_par(it)
                    p = prev_kind(it, 2)
                    if p:
                        act.wait_ge(*done(("mo",) + p[1:], "pe"))
                    ins = nc.scalar.activation(PT[:, s, 0:nk], ps[:, 0:nk], ACT.Copy)
                else:
                    raise AssertionError(k)
                ins.then_inc(mine, 1)

        @block.vector
        def _(dve):
            entered = set()
            V_ = nc.vector
            for it in plan:
                if it[0] == "v":
                    it = it[1:]
                elif it[0] in SPLIT:
                    continue
                k, l = it[0], it[1]
                if k not in parts["dve"]:
                    continue
                if k in PHASE:
                    fence(dve, "dve", it, entered)
                ps = psum(it) if banks[it] else None
                if k in parts["pe"] and takes_part(it, "pe") and k not in ("dg",):
                    dve.wait_ge(*done(it, "pe"))
                mine = signal(it, "dve")
                q0 = 0 if (k not in ("par",) and l < DEPTH - 1) else LC

                def ln(ins):
                    link(dve, "dve", ins)

                if k == "par":
                    dve.wait_ge(*done(it, "act"))
                    if l == 0:
                        ln(V_.tensor_scalar(SCt[:, 0, :], SCt[:, 0, :], 1.0, None, ALU.add))
                        ln(V_.reciprocal(SCt[:, 0, :], SCt[:, 0, :]))
                        ln(V_.tensor_tensor(SC[:, :], SCt[:, 0, :], PAR[:, l, PR_C:PR_C + 16], ALU.mult))
                    V_.tensor_tensor(QKW[:, l:l + 1], PAR[:, l, PR_QNN:PR_QNN + 1], PAR[:, l, PR_KNN:PR_KNN + 1], ALU.mult)
                    V_.tensor_copy(NW4[:, l, 0, :].rearrange("p (a b) -> p a b", a=2),
                                   bc(PAR[:, l, PR_GLA:PR_GLA + 2], 1, [P, 2, 2]))
                    ins = V_.tensor_copy(NW4[:, l, 1, :], PAR[:, l, PR_GDN:PR_GDN + 1].broadcast_to([P, 4]))
                elif k == "mod":
                    _, l, j = it
                    o = V_.tensor_tensor(MOD[:, l, 4 * j:4 * j + 4, :], ps[:, 0:8].rearrange("p (t s) -> p t s", s=2),
                                         bc(PAR[:, l, PR_ADAB + 4 * j:PR_ADAB + 4 * j + 4], 2, [P, 4, 2]), ALU.add)
                    ins = o
                elif k == "nh":
                    dve.wait_ge(*done(("norm", l), "act"))
                    dve.wait_ge(*done(("mod", l, 3), "dve"))
                    ln(V_.tensor_scalar(SCW[:, :, :], MOD[:, l, 8:16, :], 1.0, None, ALU.add))
                    ln(V_.tensor_tensor(SCW[:, :, :], SCW[:, :, :], bc(PAR[:, l, PR_NORM:PR_NORM + 8], 2, [P, 8, 2]), ALU.mult))
                    if l:
                        for br in range(3):
                            dve.wait_ge(*done(("gate", l - 1, br, 7), "pe"))
                    for kk in range(KT + 1):
                        if kk < KT:
                            V_.tensor_tensor(hT[:, kk, :], yT[:, kk, :], RS[:, :], ALU.mult).then_inc(s_scaled, 1)
                        if kk:
                            dve.wait_ge(s_scaled, l * KT + kk)
                            for s in range(2):
                                sel = 1 - s
                                ins = V_.tensor_scalar(seg(hT[:, kk - 1, :], s), seg(hT[:, kk - 1, :], s),
                                                       SCW[:, kk - 1, sel:sel + 1], MOD[:, l, kk - 1, sel:sel + 1],
                                                       ALU.mult, ALU.add)
                            if kk < KT:
                                ins.then_inc(s_h, 1)
                elif k == "z":
                    _, l, br, tt, h = it
                    n = zg_index[it]
                    e = E1[:, n % 2, :]
                    dve.wait_ge(*done(it, "act"))
                    ins = V_.scalar_tensor_tensor(e, ps[:, :], 0.0, e, ALU.min, ALU.subtract)
                elif k == "z2":
                    _, l, br, tt, h = it
                    zi = ("z", l, br, tt, h)
                    e = E1[:, zg_index[zi] % 2, :]
                    ps = psum(zi)
                    dve.wait_ge(*done(it, "act"))
                    o = O[:, tt, h * 512:(h + 1) * 512]
                    if br < 2:
                        nh = (AH if br == 0 else BH) // 2
                        dve.wait_ge(*done(("rstd", l, br), "act"))
                        V_.tensor_tensor(e, e, ps[:, :], ALU.mult)
                        if br == 0:
                            dve.wait_ge(*done(("go", l, AH - 1, TT - 1), "dve"))
                        else:
                            dve.wait_ge(*done(("so", l, 3, NCH - 1), "dve"))
                        ln(V_.tensor_tensor(o.rearrange("p (h n) -> p h n", h=nh), o.rearrange("p (h n) -> p h n", h=nh),
                                            bc(SSQ[:, br, tt, h * nh:(h + 1) * nh], 2, [P, nh, 512 // nh]), ALU.mult))
                    else:
                        dve.wait_ge(*done(("mo", l, MH - 1, TT - 1), "dve"))
                        ln(V_.tensor_tensor(e, e, ps[:, :], ALU.mult))
                    ins = V_.tensor_tensor(o, o, e, ALU.mult)
                elif k == "yT":
                    _, l, br, tt, h = it
                    if br:
                        dve.wait_ge(*done(("ys", l, br - 1, 7), "pe"))
                    else:
                        dve.wait_ge(s_spill, 16 * (l + 1))
                    dst = yT[:, 4 * h:4 * h + 4, tt * P:(tt + 1) * P]
                    src = ps[:, :].rearrange("p (j n) -> p j n", j=4)
                    if br < 2:
                        ins = V_.tensor_tensor(dst, src, bc(NW4[:, l, br, :], 2, [P, 4, P]), ALU.mult)
                    else:
                        ins = V_.tensor_copy(dst, src)
                elif k == "gate":
                    n = zg_index[it]
                    e = E1[:, n % 2, q0:512]
                    dve.wait_ge(*done(it, "act"))
                    ins = V_.scalar_tensor_tensor(e, ps[:, q0:512], 0.0, e, ALU.min, ALU.subtract)
                elif k == "ys":
                    _, l, br, e8 = it
                    gi = ("gate",) + it[1:]
                    e = E1[:, zg_index[gi] % 2, q0:512]
                    dve.wait_ge(*done(it, "act"))
                    m = MT[:, e8, q0:T]
                    if br == 0:
                        if l:
                            dve.wait_ge(*done(("out", l - 1, 7), "pe"))
                        ins = V_.tensor_tensor(m, ps[:, q0:T], e, ALU.mult)
                    else:
                        dve.wait_ge(*done(("ys", l, br - 1, e8), "dve"))
                        ln(V_.tensor_tensor(e, ps[:, q0:T], e, ALU.mult))
                        ins = V_.tensor_tensor(m, m, e, ALU.add)
                elif k == "out":
                    _, l, e8 = it
                    dve.wait_ge(*done(("mod", l, 5), "dve"))
                    dve.wait_ge(s_back, 16 * (l + 1))
                    for s in range(q0 // LC, 2):
                        sel = 1 - s
                        ins = V_.scalar_tensor_tensor(seg(yT[:, e8, :], s), ps[:, s * LC:(s + 1) * LC],
                                                      MOD[:, l, 16 + e8, sel:sel + 1], seg(yT[:, e8, :], s),
                                                      ALU.mult, ALU.add)
                elif k == "ga":
                    _, l, g, tt = it
                    dve.wait_ge(*done(it, "act"))
                    if g:
                        dve.wait_ge(*done(("gb", l, 2 * g - 1, 1), "pe"))
                        dve.wait_ge(*done(("ge", l, g - 1, TT - 1), "pe"))
                    ins = V_.scalar_tensor_tensor(LA[:, tt, :], ps[:, :], 0.0, LT1, ALU.min, ALU.subtract)
                elif k == "gb":
                    _, l, h, r = it
                    g, hh = h // 2, h % 2
                    dve.wait_ge(*done(it, "act"))
                    if h:
                        dve.wait_ge(*done(("go", l, h - 1, TT - 1), "pe"))
                        dve.wait_ge(*done(("gatt", l, h - 1, 1), "pe"))
                        dve.wait_ge(*done(("gw", l, h - 1, r, 3), "dve"))
                    e0 = CH - 1 if r == 0 else 0
                    V_.tensor_copy(ADEC[:, r, :], EB[:, e0:e0 + T - CH + 1:CH])
                    dve.wait_ge(*done(("gqk", l, g, hh), "act"))
                    V_.scalar_tensor_tensor(AQ[:, r, q0:T], QK[:, g, hh, q0:T], ADK ** -0.5, EB[:, q0:T], ALU.mult, ALU.mult)
                    dve.wait_ge(*done(("gqk", l, g, 2 + hh), "act"))
                    ins = V_.tensor_tensor(AKI[:, r, :], QK[:, g, 2 + hh, :], EI, ALU.mult)
                elif k == "ge":
                    _, l, g, tt = it
                    dve.wait_ge(*done(it, "act"))
                    if g:
                        dve.wait_ge(*done(("gw", l, 2 * g - 1, 1, 3), "pe"))
                        dve.wait_ge(*done(("gw", l, 2 * g - 1, 0, 3), "pe"))
                    kt = psum(it, 1)[:, 0:256].rearrange("p (h n) -> p h n", h=2)
                    for r in range(2):
                        ins = V_.tensor_tensor(AKE[:, tt, r * 256:(r + 1) * 256].rearrange("p (h n) -> p h n", h=2),
                                               AER[:, r * 256:(r + 1) * 256].rearrange("p (h n) -> p h n", h=2), kt, ALU.mult)
                elif k == "gatt":
                    _, l, h, r = it
                    if h:
                        dve.wait_ge(*done(("go", l, h - 1, TT - 1), "pe"))
                    dve.wait_ge(s_zero, 3 * l + 2)
                    nt = len(tiles(l))
                    ins = V_.copy_predicated(ATT[:, r, q0:T].rearrange("p (t n) -> p t n", t=nt),
                                             bc(cum(r).bitcast(U32), 1, [P, nt, P]),
                                             ps[:, q0:T].rearrange("p (t n) -> p t n", t=nt))
                elif k == "gw":
                    _, l, h, r, m = it
                    if m >= 2 and l < DEPTH - 1:
                        dve.wait_ge(*done(("go", l, h, 1), "pe"))
                    elif h:
                        dve.wait_ge(*done(("go", l, h - 1, TT - 1), "pe"))
                    dve.wait_ge(*done(("gb", l, h, r), "dve"))
                    for i in range(2):
                        n = 2 * m + i
                        if n == NCH - 1:
                            continue
                        cc = chunk_of(r, n)
                        w = psum(it, i)[:, 0:256]
                        if n == 0:
                            ln(V_.tensor_copy(HS[:, r, 1, :], w))
                        else:
                            if i == 0:
                                dve.wait_ge(*done(("gw", l, h, r, m - 1), "dve"))
                            ins = V_.scalar_tensor_tensor(HS[:, r, (n + 1) % 4, :], HS[:, r, n % 4, :], ADEC[:, r, cc:cc + 1],
                                                          w, ALU.mult, ALU.add)
                            if i == 0 and n + 1 < NCH - 1:
                                ln(ins)
                elif k == "go":
                    _, l, h, tt = it
                    dve.wait_ge(*done(it, "act"))
                    ins = V_.tensor_copy(O[:, tt, h * ADV:(h + 1) * ADV], ps[:, 0:ADV])
                elif k == "rstd":
                    ins = V_.tensor_copy(SCt[:, 1, 1:2], EPSC[:, :])
                elif k == "ab":
                    dve.wait_ge(s_row, 16 * 8)
                    v = ps[:, 0:128].rearrange("p (t n) -> p t n", t=4)
                    V_.tensor_tensor(GTMP[:, :, :], v[:, :, 0:16], bc(ALB[:, l, 16:32], 1, [P, 4, 16]), ALU.add)
                    ins = V_.tensor_copy(BETA[:, :, :], v[:, :, 16:32])
                elif k == "dg":
                    dve.wait_ge(*done(("ab", l), "dve"))
                    ln(V_.tensor_copy(GC[:, :, :], GTMP[:, :, :]))
                    V_.tensor_scalar(GC[:, :, :], GC[:, :, :], 0.0, None, ALU.max).then_inc(signal(it, "dve", "adt"), 1)
                    dve.wait_ge(*done(it, "act", "sp"))
                    ln(V_.tensor_scalar(BETA[:, :, :], BETA[:, :, :], 1.0, None, ALU.add))
                    ln(V_.reciprocal(BETA[:, :, :], BETA[:, :, :]))
                    ln(V_.tensor_tensor(GG[:, :, :], GC[:, :, :], GTM2[:, :, :], ALU.add))
                    V_.scalar_tensor_tensor(GG[:, :, :], GG[:, :, :], -1.0, bc(EAL, 1, [P, 4, 16]), ALU.mult,
                                            ALU.mult).then_inc(signal(it, "dve", "gg"), 1)
                    dve.wait_ge(*done(it, "pe"))
                    dve.wait_ge(*done(it, "act"))
                    ln(V_.tensor_copy(GC[:, :, :], ps[:, 0:64].rearrange("p (t n) -> p t n", t=4)))
                    ins = V_.memset(bS, 0.0)
                elif k == "cv":
                    _, l, g, j, tap = it
                    pj = dq_index["dqkv", l, g, j] % 2
                    if tap:
                        dve.wait_ge(*done(("cv", l, g, j, tap - 1), "dve"))
                    else:
                        dve.wait_ge(*done(("dqkv", l, g, j), "act"))
                        p = prev_kind(("dqkv", l, g, j), 2)
                        if p:
                            dve.wait_ge(*done(("dsil2",) + p[1:], "dve"))
                    a0 = 1 if (j < 2 and l == DEPTH - 1) else 0
                    tile = (j // 2) * 8 + 2 * g + j % 2
                    acc = CA[:, pj, a0 * LC:T].rearrange("p (s n) -> p s n", n=LC)
                    wv = CW[:, l, tap * 24 + tile:tap * 24 + tile + 1]
                    src = PAD[:, 2 * pj + a0:2 * pj + 2, tap:tap + LC]
                    if tap == 0:
                        ins = V_.tensor_scalar(acc, src, wv, None, ALU.mult)
                    else:
                        ins = V_.scalar_tensor_tensor(acc, src, wv, acc, ALU.mult, ALU.add)
                elif k == "dsilu":
                    _, l, g, j = it
                    dve.wait_ge(*done(it, "act"))
                    a0 = q0 if j < 2 else 0
                    pj = dq_index[("dqkv",) + it[1:]] % 2
                    ins = V_.scalar_tensor_tensor(CE[:, a0:T], CA[:, pj, a0:T], 0.0, CE[:, a0:T],
                                                  ALU.min, ALU.subtract)
                elif k == "dsil2":
                    _, l, g, j = it
                    dve.wait_ge(*done(it, "act"))
                    a0 = q0 if j < 2 else 0
                    pj = dq_index[("dqkv",) + it[1:]] % 2
                    if g:
                        dve.wait_ge(*done(("d3", l, g - 1, TT - 1), "pe"))
                        dve.wait_ge(*done(("d1", l, g - 1, TT - 1), "pool"))
                    ins = V_.tensor_tensor(KQV[:, j, a0:T], CA[:, pj, a0:T], CE[:, a0:T], ALU.mult)
                elif k == "dn":
                    _, l, g, j = it
                    dve.wait_ge(*done(it, "act"))
                    a0 = q0 if j < 2 else 0
                    sc = BDK ** -0.5 if j < 2 else 1.0
                    ins = V_.scalar_tensor_tensor(KQV[:, j, a0:T], KQV[:, j, a0:T], sc, bSQ[:, a0:T], ALU.mult, ALU.mult)
                elif k == "d1":
                    _, l, g, tt = it
                    s, sl = dpar(it), slot_of(it)
                    pit = tile_before(it, 2)
                    if pit:
                        dve.wait_ge(*done(("dx",) + pit[1:] + (NLEV - 1,), "pe"))
                    slot_free(dve, "dve", it)
                    dve.wait_ge(*done(it, "act", "egr"))
                    for c2 in range(2):
                        rows = slice(c2 * CH, (c2 + 1) * CH)
                        gcs = GC[rows, tt, :].rearrange("p (r h) -> p r h", r=2)[:, :, 2 * g:2 * g + 2]
                        ins = V_.tensor_tensor(
                            bDEC[rows, s, 0:256].rearrange("p (r h n) -> p r h n", r=2, h=2),
                            ps[rows, :].rearrange("p (r h n) -> p r h n", r=2, h=2)[:, :, :, c2 * CH:(c2 + 1) * CH],
                            bc(gcs, 3, [CH, 2, 2, CH]), ALU.subtract)
                    ln(ins)
                    V_.tensor_scalar(bDEC[:, s, 0:256], bDEC[:, s, 0:256], 0.0, None, ALU.min).then_inc(signal(it, "dve", "dif"), 1)
                    dve.wait_ge(*done(it, "act", "egr"))
                    for r in range(2):
                        e0 = CH - 1 if r == 0 else 0
                        ins = V_.tensor_copy(
                            bD[:, sl, 4 * r:4 * r + 4].rearrange("p (h c) -> p h c", h=2),
                            E1T[:, s, r * 256:(r + 1) * 256].rearrange("p (h c n) -> p h c n", h=2, n=CH)[:, :, :, e0])
                elif k == "d2":
                    _, l, g, tt = it
                    s, sl = dpar(it), slot_of(it)
                    dve.wait_ge(*done(("d1", l, g, tt), "act"))
                    dve.wait_ge(s_zero2, 3 * (l + 1))
                    pit = tile_before(it, 2)
                    if pit:
                        dve.wait_ge(*done(("dx",) + pit[1:] + (NLEV - 1,), "pe"))
                    for c2 in range(2):
                        rows = slice(c2 * CH, (c2 + 1) * CH)
                        ins = V_.tensor_tensor(blk(bLF, s, c2).rearrange("p (r h) n -> p r h n", r=2),
                                               bc(ps[rows, 0:2 * CH].rearrange("p (h n) -> p h n", h=2), 1, [CH, 2, 2, CH]),
                                               bDEC[rows, s, 0:256].rearrange("p (r h n) -> p r h n", r=2, h=2), ALU.mult)
                    if tt in tiles(l):
                        slot_free(dve, "dve", it)
                        ln(ins)
                        dec = bDEC[:, s, 0:256].rearrange("p (r h n) -> p r h n", r=2, h=2)
                        cumc = kc(C_CUMC, 2 * CH).rearrange("p (r n) -> p r n", r=2)
                        ln(V_.tensor_tensor(dec, dec, bc(cumc, 2, [P, 2, 2, CH]), ALU.mult))
                        ins = V_.tensor_tensor(bATT[:, sl, :].rearrange("p (r n) -> p r n", r=2),
                                               bc(ps[:, 2 * CH:4 * CH], 1, [P, 2, 2 * CH]),
                                               bDEC[:, s, 0:256].rearrange("p (r n) -> p r n", r=2), ALU.mult)
                elif k == "d3":
                    _, l, g, tt = it
                    s, sl = dpar(it), slot_of(it)
                    pit = tile_before(it, 2)
                    if pit:
                        dve.wait_ge(*done(("du",) + pit[1:], "pe"))
                    slot_free(dve, "dve", it)
                    dve.wait_ge(*done(("dg", l), "act"))
                    dve.wait_ge(*done(("dg", l), "dve"))
                    dve.wait_ge(*done(("d2", l, g, tt), "dve"))
                    beta = BETA[:, tt, :].rearrange("p (r h) -> p r h", r=2)[:, :, 2 * g:2 * g + 2]
                    for i in range(2):
                        ins = V_.tensor_tensor(bXX[:, s, i * 256:(i + 1) * 256].rearrange("p (r h n) -> p r h n", r=2, h=2),
                                               kc(C_IDC, CH).unsqueeze(1).unsqueeze(1).broadcast_to([P, 2, 2, CH]),
                                               bc(beta, 3, [P, 2, 2, CH]), ALU.mult)
                elif k == "dx":
                    _, l, g, tt, lev = it
                    s = dpar(it)
                    pit = tile_before(it, 2)
                    if pit and lev == 0:
                        dve.wait_ge(*done(("du",) + pit[1:], "pe"))
                    lm = kc(C_LEV + 2 * lev * CH, 2 * CH).rearrange("p (r n) -> p r n", r=2)
                    ins = V_.tensor_tensor(bP[:, s, :].rearrange("p (r h n) -> p r h n", r=2, h=2),
                                           ps[:, 0:256].rearrange("p (r h n) -> p r h n", r=2, h=2),
                                           bc(lm, 2, [P, 2, 2, CH]), ALU.mult)
                    ins.then_inc(signal(it, "dve", "compact"), 1)
                    for c2 in range(2):
                        rows = slice(c2 * CH, (c2 + 1) * CH)
                        ins = V_.tensor_tensor(blk(bPF, s, c2).rearrange("p (r h) n -> p r h n", r=2),
                                               ps[rows, 0:256].rearrange("p (r h n) -> p r h n", r=2, h=2),
                                               bc(lm[rows], 2, [CH, 2, 2, CH]), ALU.mult)
                elif k == "dy":
                    _, l, g, tt, lev = it
                    s = dpar(it)
                    dve.wait_ge(*done(("dy", l, g, tt, lev - 1) if lev else ("d3", l, g, tt), "dve"))
                    if lev < NLEV - 1:
                        ins = V_.tensor_tensor(bXX[:, s, :], bXX[:, s, :], ps[:, :], ALU.subtract)
                    else:
                        dve.wait_ge(*done(("dy", l, g, tt, lev - 1), "act"))
                        for c2 in range(2):
                            rows = slice(c2 * CH, (c2 + 1) * CH)
                            ins = V_.tensor_tensor(blk(bTF, s, c2), cmp4(bXX[rows, s, 256:512]), cmp4(ps[rows, 256:512]),
                                                   ALU.subtract)
                        ln(ins)
                        eg = EGC[:, tt, :].rearrange("p (r h) -> p r h", r=2)[:, :, 2 * g:2 * g + 2]
                        ins = V_.tensor_tensor(bPF[:, s, :].rearrange("p (r h n) -> p r h n", r=2, h=2),
                                               bTF[:, s, :].rearrange("p (r h n) -> p r h n", r=2, h=2),
                                               bc(eg, 3, [P, 2, 2, P]), ALU.mult)
                elif k == "sv":
                    _, l, g, n = it
                    p = prev_kind(it)
                    if p:
                        dve.wait_ge(*done(("so",) + p[1:], "pe"))
                    for r in range(2):
                        cc = chunk_of(r, n)
                        tt, p0 = cc // 2, (cc % 2) * CH
                        sl = slot_of(("d1", l, g, tt))
                        dve.wait_ge(*done(("du", l, g, tt), "act"))
                        u = bU[p0:p0 + CH, sl, r * 256:(r + 1) * 256]
                        vn = bVN[p0:p0 + CH, :]
                        if n:
                            ins = V_.tensor_tensor(vn, u, ps[p0:p0 + CH, 0:256], ALU.subtract)
                        else:
                            ins = V_.tensor_copy(vn, u)
                    ln(ins)
                    for r in range(2):
                        cc = chunk_of(r, n)
                        tt, p0 = cc // 2, (cc % 2) * CH
                        ins = V_.tensor_tensor(bVE[p0:p0 + CH, :].rearrange("p (h n) -> p h n", h=2),
                                               bVN[p0:p0 + CH, :].rearrange("p (h n) -> p h n", h=2),
                                               bc(ERV[p0:p0 + CH, tt, r * BH + 2 * g:r * BH + 2 * g + 2], 2, [CH, 2, P]), ALU.mult)
                elif k == "so":
                    _, l, g, n = it
                    p = prev_kind(it)
                    if p:
                        dve.wait_ge(*done(p, "dve"))
                    if n < NCH - 1:
                        for r in range(2):
                            cc = chunk_of(r, n)
                            tt = cc // 2
                            sl = slot_of(("d1", l, g, tt))
                            dve.wait_ge(*done(("d1", l, g, tt), "dve"))
                            for hh in range(2):
                                u = 2 * r + hh
                                cs = slice(u * P, (u + 1) * P)
                                if n:
                                    ins = V_.scalar_tensor_tensor(bS[:, cs], bS[:, cs], bD[:, sl, 2 * u + cc % 2:2 * u + cc % 2 + 1],
                                                                  psum(it, 1 + r)[:, hh * P:(hh + 1) * P], ALU.mult, ALU.add)
                                else:
                                    ins = V_.tensor_copy(bS[:, cs], psum(it, 1 + r)[:, hh * P:(hh + 1) * P])
                    if chunk_of(0, n) // 2 in tiles(l):
                        for tt in tiles(l):
                            dve.wait_ge(*done(("yT", l, 0, tt, 1), "pe"))
                        for r in range(2):
                            cc = chunk_of(r, n)
                            tt, p0 = cc // 2, (cc % 2) * CH
                            o = O[p0:p0 + CH, tt, g * 256:(g + 1) * 256]
                            if step_of(1 - r, cc) > n:
                                ins = V_.tensor_copy(o, ps[p0:p0 + CH, 0:256])
                            else:
                                ins = V_.tensor_tensor(o, o, ps[p0:p0 + CH, 0:256], ALU.add)
                elif k in ("mq", "mkv"):
                    _, l, tt = it
                    dve.wait_ge(*done(it, "act"))
                    i = low_rank(l).index(it)
                    if i >= 2:
                        b = low_rank(l)[i - 2]
                        dve.wait_ge(*done(("mt", l, b[2], int(b[0] == "mkv")), "pe"))
                    if k == "mkv" and tt == 0:
                        for q in range(2):
                            w = RW[:, l, q, :]
                            cwt = RT[:, 2 * q, :].rearrange("p (t n) -> p t n", t=TT)
                            V_.tensor_tensor(cwt, kc(C_COS, 256).rearrange("p (t n) -> p t n", t=TT), bc(w, 1, [P, TT, ROPE]), ALU.mult)
                            for a in range(2):
                                for hf in range(2):
                                    d = RT[:, 2 * q + 1, :].rearrange("p (t a h f) -> p t a h f", t=TT, a=2, h=2)[:, :, a, hf, :]
                                    sn = kc(C_SIN, 256).rearrange("p (t a h f) -> p t a h f", t=TT, a=2, h=2)[:, :, a, hf, :]
                                    ws = w.rearrange("p (a h f) -> p a h f", a=2, h=2)[:, a, 1 - hf, :]
                                    ins = V_.tensor_tensor(d, sn, bc(ws, 1, [P, TT, 16]), ALU.mult)
                        ln(ins)
                    if k == "mq":
                        ins = V_.tensor_scalar(MT1[:, tt % 2, 0:QL], ps[:, 0:QL], mS[:, 0:1], None, ALU.mult)
                    else:
                        V_.tensor_scalar(MT1[:, tt % 2, 0:KVL], ps[:, 0:KVL], mS[:, 0:1], None, ALU.mult)
                        ln(V_.tensor_scalar(MT3[:, 0:64], ps[:, KVL:KVL + 64], mS[:, 1:2], None, ALU.mult))
                        ln(rope(dve, MT1[:, tt % 2, KVL:KVL + 64], MT3[:, 0:64], 1, tt, 1))
                        ins = V_.tensor_copy(MT1[:, tt % 2, KVL + 64:KVL + 128], MT1[:, tt % 2, KVL:KVL + 64])
                elif k == "mt":
                    _, l, tt, kv = it
                    n = 2 if kv else 3
                    dst = (MKL if kv else MQL)[:, :, tt * P:(tt + 1) * P]
                    pr = PR_KVN if kv else PR_QN
                    ins = V_.tensor_tensor(dst, ps[:, 0:n * P].rearrange("p (j n) -> p j n", j=n),
                                           bc(PAR[:, l, pr:pr + n], 2, [P, n, P]), ALU.mult)
                    if kv:
                        ins = V_.tensor_copy(KRT[:, tt * P:(tt + 1) * P], ps[:, 256:384])
                elif k == "muk":
                    _, l, g, tt = it
                    m4 = 4 + 4 * (mu_index[it] % 2)
                    dve.wait_ge(*done(it, "act"))
                    if g:
                        dve.wait_ge(*done(("mkT", l, g - 1, tt), "pe"))
                    v4 = ps[:, :].rearrange("p (h w n) -> p h w n", h=2, w=2)
                    ins = V_.tensor_tensor(KN[:, tt, :].rearrange("p (h n) -> p h n", h=2), v4[:, :, 0, :],
                                           bc(mS[:, m4:m4 + 2], 2, [P, 2, P]), ALU.mult)
                elif k == "muq":
                    _, l, g, tt = it
                    m4 = 4 + 4 * (mu_index[it] % 2)
                    dve.wait_ge(*done(it, "act"))
                    if g:
                        dve.wait_ge(*done(("mqT", l, g - 1, tt), "pe"))
                    v3 = ps[:, 0:384].rearrange("p (h n) -> p h n", h=2)
                    V_.tensor_tensor(QN[:, tt, 0:256].rearrange("p (h n) -> p h n", h=2), v3[:, :, 0:NOPE],
                                     bc(mS[:, m4:m4 + 2], 2, [P, 2, P]), ALU.mult)
                    ln(V_.tensor_tensor(MT3[:, 0:128].rearrange("p (h n) -> p h n", h=2), v3[:, :, NOPE:192],
                                        bc(mS[:, m4 + 2:m4 + 4], 2, [P, 2, ROPE]), ALU.mult))
                    ins = rope(dve, QN[:, tt, 256:384], MT3[:, 0:128], 0, tt, 2)
                elif k == "mqT":
                    _, l, g, tt = it
                    if g:
                        dve.wait_ge(*done(("ms", l, 2 * g - 1, TT - 1), "pe"))
                    dve.wait_ge(*done(it, "act"))
                    ins = V_.tensor_scalar(QNT[:, :, tt * P:(tt + 1) * P], ps[:, 0:256].rearrange("p (h n) -> p h n", h=2),
                                           QKW[:, l:l + 1], None, ALU.mult)
                elif k == "ms":
                    _, l, h, tt = it
                    nk = LC if tt < 2 else T
                    j = nth(it, "act") % 4
                    p = prev_kind(it, 4)
                    if p:
                        dve.wait_ge(*done(("mo",) + p[1:], "dve"))
                        dve.wait_ge(*done(p, "act"))
                    ln(V_.tensor_reduce(MST[:, j, 2:3], ps[:, 0:nk], AX_X, ALU.max))
                    V_.tensor_scalar(MST[:, j, 0:1], MST[:, j, 2:3], -MSCALE, None, ALU.mult).then_inc(signal(it, "dve", "max"), 1)
                    dve.wait_ge(*done(it, "act"))
                    ins = V_.reciprocal(MST[:, j, 3:4], MST[:, j, 1:2])
                elif k == "mo":
                    _, l, h, tt = it
                    j = nth(it, "act") % 4
                    dve.wait_ge(*done(("ms", l, h, tt), "dve"))
                    for t in tiles(l):
                        dve.wait_ge(*done(("yT", l, 1, t, 1), "pe"))
                    ins = V_.tensor_scalar(O[:, tt, h * P:(h + 1) * P], ps[:, 0:P], MST[:, j, 3:4], None, ALU.mult)
                else:
                    raise AssertionError(k)
                ins.then_inc(mine, 1)

    return nc


_INS = ["x", "c", "ctx", "c_ctx", "norm_w", "ada_w", "ada_b", "w_in", "gla_gate_w2", "gla_gate_b", "gla_norm_w",
        "gdn_conv_w", "gdn_a_log", "gdn_dt_bias", "gdn_norm_w", "mla_q_norm_w", "mla_q_up", "mla_kv_norm_w",
        "mla_kv_up", "mla_qn_nope", "mla_qn_rope", "mla_kn_nope", "mla_kn_rope", "w_branch", "w_out"]


def kernel(**inputs):
    import numpy as _np
    import concourse.bacc as _bacc
    from concourse import mybir as _mybir
    from concourse.bass_utils import run_bass_kernel_spmd as _run

    nc = _bacc.Bacc("TRN2", target_bir_lowering=False, num_devices=1)
    arrays, args = {}, []
    for name in _INS:
        a = _np.ascontiguousarray(inputs[name])
        arrays[f"in_{name}_dram"] = a
        args.append(nc.dram_tensor(f"in_{name}_dram", a.shape, _mybir.dt.from_np(a.dtype), kind="ExternalInput").ap())
    a = constants()
    arrays["shape_constants"] = a
    args.append(nc.dram_tensor("shape_constants", a.shape, _mybir.dt.from_np(a.dtype), kind="ExternalInput").ap())
    out = nc.dram_tensor("out_dram", (1, LX, D), F32, kind="ExternalOutput").ap()
    hybrid_block(nc, *args, out)
    r = _run(nc, [arrays], core_ids=[0])
    return r.results[0]["out_dram"]
```
